# Optimizing a Trainium2 kernel written in Bass

```python
import math
import jax, jax.numpy as jnp
from jax import lax
import numpy as np

D_MODEL = 1024
BATCH = 1
SEQ = 1024
DEPTH = 1

ROPE_THETA = 10000.0
EPS = 1e-6
Q_BLOCK = 128

MLA_HEADS = 4
MLA_Q_RANK = 256
MLA_KV_RANK = 256
MLA_NOPE_DIM = 128
MLA_ROPE_DIM = 64
MLA_V_DIM = 128

DIFF_HEADS = 4
DIFF_QK_DIM = 64
DIFF_V_DIM = 2 * DIFF_QK_DIM

MIX_WIDTH = MLA_HEADS * MLA_V_DIM + DIFF_HEADS * DIFF_V_DIM
IN_SPLITS = (MLA_Q_RANK, MLA_KV_RANK, MLA_ROPE_DIM,
             DIFF_HEADS * 2 * DIFF_QK_DIM, DIFF_HEADS * 2 * DIFF_QK_DIM, DIFF_HEADS * DIFF_V_DIM)
IN_COLS = sum(IN_SPLITS)

N_GROUPS = 4
EXPERTS_PER_GROUP = 8
N_EXPERTS = N_GROUPS * EXPERTS_PER_GROUP
TOP_K = 2
D_EXPERT = 512
MOE_BLOCK = 128


def rms_norm(x, g):
    xf = x.astype(jnp.float32)
    y = xf * lax.rsqrt(jnp.mean(xf * xf, axis=-1, keepdims=True) + EPS)
    return (y * g.astype(jnp.float32)).astype(x.dtype)

def rope(x, pos):
    d = x.shape[-1]
    inv = ROPE_THETA ** (-jnp.arange(0, d, 2, dtype=jnp.float32) / d)
    ang = pos.astype(jnp.float32)[:, None] * inv[None, :]
    shape = (1, x.shape[1]) + (1,) * (x.ndim - 3) + (d // 2,)
    cos = jnp.cos(ang).reshape(shape)
    sin = jnp.sin(ang).reshape(shape)
    xf = x.astype(jnp.float32)
    x1, x2 = xf[..., : d // 2], xf[..., d // 2:]
    return jnp.concatenate([x1 * cos - x2 * sin, x2 * cos + x1 * sin], axis=-1).astype(x.dtype)

def to_blocks(t):
    b, s = t.shape[0], t.shape[1]
    return t.reshape((b, s // Q_BLOCK, Q_BLOCK) + t.shape[2:]).swapaxes(0, 1)

def from_blocks(t):
    nb, b, qb = t.shape[0], t.shape[1], t.shape[2]
    return t.swapaxes(0, 1).reshape((b, nb * qb) + t.shape[3:])

def mla_attention(q_nope, q_pe, k_nope, k_pe, v):
    scale = (q_nope.shape[-1] + q_pe.shape[-1]) ** -0.5

    def block(args):
        qn, qr = args
        s = (jnp.einsum('bqhd,bkhd->bhqk', qn, k_nope)
             + jnp.einsum('bqhr,bkr->bhqk', qr, k_pe)).astype(jnp.float32) * scale
        p = jax.nn.softmax(s, axis=-1).astype(v.dtype)
        return jnp.einsum('bhqk,bkhd->bqhd', p, v)

    return from_blocks(lax.map(block, (to_blocks(q_nope), to_blocks(q_pe))))

def diff_attention(q1, q2, k1, k2, v, lam):
    scale = q1.shape[-1] ** -0.5

    def block(args):
        a1, a2 = args
        s1 = jnp.einsum('bqhd,bkhd->bhqk', a1, k1).astype(jnp.float32) * scale
        s2 = jnp.einsum('bqhd,bkhd->bhqk', a2, k2).astype(jnp.float32) * scale
        p = (jax.nn.softmax(s1, axis=-1) - lam * jax.nn.softmax(s2, axis=-1)).astype(v.dtype)
        return jnp.einsum('bhqk,bkhd->bqhd', p, v)

    return from_blocks(lax.map(block, (to_blocks(q1), to_blocks(q2))))

def hier_moe(h, w_rg, b_rg, w_re, b_re, w_gate, w_up, w_down):
    b, s, d = h.shape
    t = b * s
    a = t * TOP_K
    hf = h.reshape(t, d)
    hf32 = hf.astype(jnp.float32)
    g_logits = hf32 @ w_rg.astype(jnp.float32) + b_rg.astype(jnp.float32)
    g_prob, g_idx = lax.top_k(jax.nn.softmax(g_logits, axis=-1), 1)
    e_logits = (hf32 @ w_re.astype(jnp.float32) + b_re.astype(jnp.float32)).reshape(t, N_GROUPS, EXPERTS_PER_GROUP)
    e_sel = jnp.take_along_axis(e_logits, g_idx[:, :, None], axis=1)[:, 0]
    top_l, top_i = lax.top_k(e_sel, TOP_K)
    weights = (g_prob * jax.nn.softmax(top_l, axis=-1)).astype(h.dtype)
    eid = g_idx * EXPERTS_PER_GROUP + top_i

    e_flat = eid.reshape(a).astype(jnp.int32)
    t_flat = jnp.repeat(jnp.arange(t, dtype=jnp.int32), TOP_K)
    w_flat = weights.reshape(a)
    order = jnp.argsort(e_flat)
    e_s, t_s, w_s = e_flat[order], t_flat[order], w_flat[order]
    counts = jnp.zeros((N_EXPERTS,), jnp.int32).at[e_flat].add(1)
    starts = jnp.cumsum(counts) - counts
    padded = ((counts + MOE_BLOCK - 1) // MOE_BLOCK) * MOE_BLOCK
    pends = jnp.cumsum(padded)
    pstarts = pends - padded
    dest = pstarts[e_s] + (jnp.arange(a, dtype=jnp.int32) - starts[e_s])
    rows = a + N_EXPERTS * MOE_BLOCK
    nb = rows // MOE_BLOCK
    row_token = jnp.zeros((rows,), jnp.int32).at[dest].set(t_s)
    row_weight = jnp.zeros((rows,), h.dtype).at[dest].set(w_s)
    block_expert = jnp.minimum(
        jnp.searchsorted(pends, jnp.arange(nb, dtype=jnp.int32) * MOE_BLOCK, side='right'),
        N_EXPERTS - 1).astype(jnp.int32)
    xs = hf[row_token].reshape(nb, MOE_BLOCK, d)

    def expert_block(args):
        xb, e = args
        g = xb @ w_gate[e]
        u = xb @ w_up[e]
        return (jax.nn.silu(g) * u) @ w_down[e]

    ys = lax.map(expert_block, (xs, block_expert)).reshape(rows, d)
    out = jnp.zeros((t, d), h.dtype).at[row_token].add(ys * row_weight[:, None])
    return out.reshape(b, s, d)

def first_inputs(seed: int = 0) -> dict:
    key = jax.random.key(seed)
    ks = jax.random.split(key, 32)
    f32 = jnp.float32
    L, D = DEPTH, D_MODEL

    def nrm(k, shape, std):
        return jax.random.normal(k, shape, f32) * std

    def gain(k, shape):
        return 1.0 + 0.02 * jax.random.normal(k, shape, f32)

    return {
        'x': nrm(ks[0], (BATCH, SEQ, D), 1.0),
        'c': nrm(ks[1], (BATCH, D), 1.0),
        'w_ada': nrm(ks[2], (L, D, 6 * D), 0.5 * D ** -0.5),
        'b_ada': nrm(ks[3], (L, 6 * D), 0.02),
        'norm1_g': gain(ks[4], (L, D)),
        'w_in': nrm(ks[5], (L, D, IN_COLS), D ** -0.5),
        'q_a_norm_g': gain(ks[6], (L, MLA_Q_RANK)),
        'w_q_up': nrm(ks[7], (L, MLA_Q_RANK, MLA_HEADS * (MLA_NOPE_DIM + MLA_ROPE_DIM)), MLA_Q_RANK ** -0.5),
        'kv_a_norm_g': gain(ks[8], (L, MLA_KV_RANK)),
        'w_kv_up': nrm(ks[9], (L, MLA_KV_RANK, MLA_HEADS * (MLA_NOPE_DIM + MLA_V_DIM)), MLA_KV_RANK ** -0.5),
        'lambda_q1': nrm(ks[10], (L, DIFF_QK_DIM), 0.1),
        'lambda_k1': nrm(ks[11], (L, DIFF_QK_DIM), 0.1),
        'lambda_q2': nrm(ks[12], (L, DIFF_QK_DIM), 0.1),
        'lambda_k2': nrm(ks[13], (L, DIFF_QK_DIM), 0.1),
        'subln_g': gain(ks[14], (L, DIFF_V_DIM)),
        'w_out': nrm(ks[15], (L, MIX_WIDTH, D), MIX_WIDTH ** -0.5),
        'norm2_g': gain(ks[16], (L, D)),
        'w_router_group': nrm(ks[17], (L, D, N_GROUPS), D ** -0.5),
        'b_router_group': nrm(ks[18], (L, N_GROUPS), 0.01),
        'w_router_expert': nrm(ks[19], (L, D, N_EXPERTS), D ** -0.5),
        'b_router_expert': nrm(ks[20], (L, N_EXPERTS), 0.01),
        'w_expert_gate': nrm(ks[21], (L, N_EXPERTS, D, D_EXPERT), D ** -0.5),
        'w_expert_up': nrm(ks[22], (L, N_EXPERTS, D, D_EXPERT), D ** -0.5),
        'w_expert_down': nrm(ks[23], (L, N_EXPERTS, D_EXPERT, D), D_EXPERT ** -0.5),
        'final_norm_g': gain(ks[24], (D,)),
    }

def first_block(x, c, w_ada, b_ada, norm1_g, w_in, q_a_norm_g, w_q_up, kv_a_norm_g, w_kv_up,
              lambda_q1, lambda_k1, lambda_q2, lambda_k2, subln_g, w_out, norm2_g,
              w_router_group, b_router_group, w_router_expert, b_router_expert,
              w_expert_gate, w_expert_up, w_expert_down, final_norm_g):
    b, s, _ = x.shape
    pos = jnp.arange(s, dtype=jnp.int32)
    offsets = [int(v) for v in np.cumsum(IN_SPLITS)[:-1]]
    for l in range(DEPTH):
        mod = jax.nn.silu(c) @ w_ada[l] + b_ada[l]
        shift1, scale1, gate1, shift2, scale2, gate2 = jnp.split(mod, 6, axis=-1)

        h = rms_norm(x, norm1_g[l]) * (1.0 + scale1[:, None, :]) + shift1[:, None, :]
        z = h @ w_in[l]
        c_q, c_kv, k_pe, dq, dk, dv = jnp.split(z, offsets, axis=-1)

        q = (rms_norm(c_q, q_a_norm_g[l]) @ w_q_up[l]).reshape(b, s, MLA_HEADS, MLA_NOPE_DIM + MLA_ROPE_DIM)
        q_nope, q_pe = q[..., :MLA_NOPE_DIM], rope(q[..., MLA_NOPE_DIM:], pos)
        kv = (rms_norm(c_kv, kv_a_norm_g[l]) @ w_kv_up[l]).reshape(b, s, MLA_HEADS, MLA_NOPE_DIM + MLA_V_DIM)
        k_nope, v_mla = kv[..., :MLA_NOPE_DIM], kv[..., MLA_NOPE_DIM:]
        k_pe = rope(k_pe[:, :, None, :], pos)[:, :, 0, :]
        mla_out = mla_attention(q_nope, q_pe, k_nope, k_pe, v_mla).reshape(b, s, MLA_HEADS * MLA_V_DIM)

        dq = rope(dq.reshape(b, s, DIFF_HEADS, 2, DIFF_QK_DIM), pos)
        dk = rope(dk.reshape(b, s, DIFF_HEADS, 2, DIFF_QK_DIM), pos)
        dv = dv.reshape(b, s, DIFF_HEADS, DIFF_V_DIM)
        lambda_init = 0.8 - 0.6 * math.exp(-0.3 * l)
        lam = (jnp.exp(jnp.sum(lambda_q1[l].astype(jnp.float32) * lambda_k1[l].astype(jnp.float32)))
               - jnp.exp(jnp.sum(lambda_q2[l].astype(jnp.float32) * lambda_k2[l].astype(jnp.float32)))
               + lambda_init)
        d_out = diff_attention(dq[..., 0, :], dq[..., 1, :], dk[..., 0, :], dk[..., 1, :], dv, lam)
        d_out = (rms_norm(d_out, subln_g[l]) * (1.0 - lambda_init)).reshape(b, s, DIFF_HEADS * DIFF_V_DIM)

        mix = jnp.concatenate([mla_out, d_out], axis=-1) @ w_out[l]
        x = x + gate1[:, None, :] * mix

        h2 = rms_norm(x, norm2_g[l]) * (1.0 + scale2[:, None, :]) + shift2[:, None, :]
        moe = hier_moe(h2, w_router_group[l], b_router_group[l], w_router_expert[l], b_router_expert[l],
                       w_expert_gate[l], w_expert_up[l], w_expert_down[l])
        x = x + gate2[:, None, :] * moe
    return rms_norm(x, final_norm_g)


CHUNK = 64
N_MIXERS = 2
CONV_WIDTH = 3
N_HEADS = 16
HEAD_DIM = D_MODEL // N_HEADS
LEFT_CHUNKS = 8
BAND = (LEFT_CHUNKS + 1) * CHUNK
MAX_REL_DIST = 256
N_REL = 2 * MAX_REL_DIST + 1
D_FF = (((8 * D_MODEL + 2) // 3 + 255) // 256) * 256
N_CONV_LAYERS = (DEPTH + N_MIXERS - 1) // N_MIXERS
N_ATTN_LAYERS = DEPTH // N_MIXERS
N_ADA = 6
RMS_EPS = 1e-6
NEG_INF = -1e30


def rms_norm_2(x, g):
    xf = x.astype(jnp.float32)
    y = xf * lax.rsqrt(jnp.mean(xf * xf, axis=-1, keepdims=True) + RMS_EPS)
    return (y * g.astype(jnp.float32)).astype(x.dtype)

def modulate(h, shift, scale):
    return h * (1.0 + scale[:, None, :]) + shift[:, None, :]

def short_conv_mixer(h, w_in, w_conv, w_out):
    d = h.shape[-1]
    bcv = h @ w_in
    gate_b, gate_c, v = jnp.split(bcv, 3, axis=-1)
    u = gate_c * v
    conv = lax.conv_general_dilated(
        u, w_conv[:, None, :].astype(u.dtype),
        window_strides=(1,), padding=[(CONV_WIDTH - 1, 0)],
        dimension_numbers=("NWC", "WIO", "NWC"), feature_group_count=d)
    return (gate_b * conv) @ w_out

def _rel_bias_index():
    qi = np.arange(CHUNK)[:, None]
    kj = np.arange(BAND)[None, :]
    dist = qi + LEFT_CHUNKS * CHUNK - kj
    return (np.clip(dist, -MAX_REL_DIST, MAX_REL_DIST) + MAX_REL_DIST).astype(np.int32)

def chunked_rel_attention(h, w_qkv, rel_bias, w_out):
    b, s, d = h.shape
    n_chunks = s // CHUNK
    qkv = (h @ w_qkv).reshape(b, s, 3, N_HEADS, HEAD_DIM)
    q = qkv[:, :, 0] * (HEAD_DIM ** -0.5)
    k = qkv[:, :, 1]
    v = qkv[:, :, 2]
    pad = ((0, 0), (LEFT_CHUNKS * CHUNK, 0), (0, 0), (0, 0))
    k_pad = jnp.pad(k, pad)
    v_pad = jnp.pad(v, pad)
    q_chunks = q.reshape(b, n_chunks, CHUNK, N_HEADS, HEAD_DIM).transpose(1, 0, 2, 3, 4)
    bias = rel_bias.astype(jnp.float32)[:, jnp.asarray(_rel_bias_index())]
    key_slot = jnp.arange(BAND)

    def one_chunk(args):
        n, qc = args
        kb = lax.dynamic_slice_in_dim(k_pad, n * CHUNK, BAND, axis=1)
        vb = lax.dynamic_slice_in_dim(v_pad, n * CHUNK, BAND, axis=1)
        scores = jnp.einsum("bqhd,bkhd->bhqk", qc, kb).astype(jnp.float32) + bias[None]
        valid = key_slot >= (LEFT_CHUNKS - n) * CHUNK
        scores = jnp.where(valid[None, None, None, :], scores, NEG_INF)
        p = jax.nn.softmax(scores, axis=-1).astype(vb.dtype)
        return jnp.einsum("bhqk,bkhd->bqhd", p, vb)

    out = lax.map(one_chunk, (jnp.arange(n_chunks, dtype=jnp.int32), q_chunks))
    out = out.transpose(1, 0, 2, 3, 4).reshape(b, s, d)
    return out @ w_out

def swiglu(h, w_gate_up, w_down):
    g, u = jnp.split(h @ w_gate_up, 2, axis=-1)
    return (jax.nn.silu(g) * u) @ w_down

def second_inputs(seed: int = 0) -> dict:
    key = jax.random.key(seed)
    ks = jax.random.split(key, 14)
    f32 = jnp.float32
    sd = D_MODEL ** -0.5
    x = jax.random.normal(ks[0], (BATCH, SEQ, D_MODEL), f32)
    c = jax.random.normal(ks[1], (BATCH, D_MODEL), f32)
    ada_w = jax.random.normal(ks[2], (DEPTH, D_MODEL, N_ADA * D_MODEL), f32) * (0.5 * sd)
    ada_b = jax.random.normal(ks[3], (DEPTH, N_ADA * D_MODEL), f32) * 0.02
    norm_gains = 1.0 + 0.02 * jax.random.normal(ks[4], (DEPTH, 4, D_MODEL), f32)
    conv_w_in = jax.random.normal(ks[5], (N_CONV_LAYERS, D_MODEL, 3 * D_MODEL), f32) * sd
    conv_w = jax.random.normal(ks[6], (N_CONV_LAYERS, CONV_WIDTH, D_MODEL), f32) * (CONV_WIDTH ** -0.5)
    conv_w_out = jax.random.normal(ks[7], (N_CONV_LAYERS, D_MODEL, D_MODEL), f32) * sd
    attn_w_qkv = jax.random.normal(ks[8], (N_ATTN_LAYERS, D_MODEL, 3 * D_MODEL), f32) * sd
    attn_rel_bias = jax.random.normal(ks[9], (N_ATTN_LAYERS, N_HEADS, N_REL), f32) * 0.1
    attn_w_out = jax.random.normal(ks[10], (N_ATTN_LAYERS, D_MODEL, D_MODEL), f32) * sd
    ffn_w_gate_up = jax.random.normal(ks[11], (DEPTH, D_MODEL, 2 * D_FF), f32) * sd
    ffn_w_down = jax.random.normal(ks[12], (DEPTH, D_FF, D_MODEL), f32) * (D_FF ** -0.5)
    return {"x": x, "c": c, "ada_w": ada_w, "ada_b": ada_b, "norm_gains": norm_gains,
            "conv_w_in": conv_w_in, "conv_w": conv_w, "conv_w_out": conv_w_out,
            "attn_w_qkv": attn_w_qkv, "attn_rel_bias": attn_rel_bias, "attn_w_out": attn_w_out,
            "ffn_w_gate_up": ffn_w_gate_up, "ffn_w_down": ffn_w_down}

def second_block(x, c, ada_w, ada_b, norm_gains, conv_w_in, conv_w, conv_w_out,
              attn_w_qkv, attn_rel_bias, attn_w_out, ffn_w_gate_up, ffn_w_down):
    c_act = jax.nn.silu(c)
    for i in range(DEPTH):
        mod = c_act @ ada_w[i] + ada_b[i]
        sh_m, sc_m, g_m, sh_f, sc_f, g_f = jnp.split(mod, N_ADA, axis=-1)
        h = modulate(rms_norm_2(x, norm_gains[i, 0]), sh_m, sc_m)
        j = i // N_MIXERS
        if i % N_MIXERS == 0:
            h = short_conv_mixer(h, conv_w_in[j], conv_w[j], conv_w_out[j])
        else:
            h = chunked_rel_attention(h, attn_w_qkv[j], attn_rel_bias[j], attn_w_out[j])
        x = x + g_m[:, None, :] * rms_norm_2(h, norm_gains[i, 1])
        h = modulate(rms_norm_2(x, norm_gains[i, 2]), sh_f, sc_f)
        h = swiglu(h, ffn_w_gate_up[i], ffn_w_down[i])
        x = x + g_f[:, None, :] * rms_norm_2(h, norm_gains[i, 3])
    return x


def setup_inputs(seed=0):
    out = dict(first_inputs(seed))
    for name, value in second_inputs(seed + 1).items():
        if name != "x":
            out[name + "_2"] = value
    return out


def reference(
    x, c, w_ada, b_ada, norm1_g, w_in, q_a_norm_g, w_q_up, kv_a_norm_g, w_kv_up, lambda_q1,
    lambda_k1, lambda_q2, lambda_k2, subln_g, w_out, norm2_g, w_router_group, b_router_group,
    w_router_expert, b_router_expert, w_expert_gate, w_expert_up, w_expert_down, final_norm_g,
    c_2, ada_w_2, ada_b_2, norm_gains_2, conv_w_in_2, conv_w_2, conv_w_out_2, attn_w_qkv_2,
    attn_rel_bias_2, attn_w_out_2, ffn_w_gate_up_2, ffn_w_down_2,
):
    x = first_block(
        x, c, w_ada, b_ada, norm1_g, w_in, q_a_norm_g, w_q_up, kv_a_norm_g, w_kv_up, lambda_q1,
        lambda_k1, lambda_q2, lambda_k2, subln_g, w_out, norm2_g, w_router_group,
        b_router_group, w_router_expert, b_router_expert, w_expert_gate, w_expert_up,
        w_expert_down, final_norm_g,
    )
    return second_block(
        x, c_2, ada_w_2, ada_b_2, norm_gains_2, conv_w_in_2, conv_w_2, conv_w_out_2,
        attn_w_qkv_2, attn_rel_bias_2, attn_w_out_2, ffn_w_gate_up_2, ffn_w_down_2,
    )


_drawn_inputs = setup_inputs


def setup_inputs(seed=0):
    import zlib

    import numpy as np

    out = dict(_drawn_inputs(seed))
    spreads = {}
    factors = {'norm1_g': 8.0,
     'q_a_norm_g': 8.0,
     'w_q_up': 2.856,
     'kv_a_norm_g': 8.0,
     'lambda_q1': 8.0,
     'lambda_k1': 2.744,
     'lambda_q2': 200.0,
     'lambda_k2': 2.971,
     'subln_g': 8.0,
     'norm2_g': 4.373,
     'b_router_group': 8.0,
     'b_router_expert': 8.0,
     'norm_gains_2': 3.707}
    for name, (base, spread) in spreads.items():
        noise = np.random.default_rng([zlib.crc32(name.encode()), seed]).standard_normal(out[name].shape)
        drawn = base * np.exp(spread * noise) if base else spread * noise
        out[name] = __import__('jax').numpy.asarray(drawn.astype(out[name].dtype))
    for name, factor in factors.items():
        out[name] = (out[name] * factor).astype(out[name].dtype)
    return out
```

```python
from contextlib import ExitStack

import numpy as np

import concourse.bass as bass
from concourse import mybir

ALU = mybir.AluOpType
ACT = mybir.ActivationFunctionType
F32 = mybir.dt.float32
U32 = mybir.dt.uint32
AX_X = mybir.AxisListType.X
ds = bass.ds

P = 128
T = 1024
D = 1024
NT = T // P
KD = D // P
HALF = 512
EPS = 1e-6
QR, KVR, NOPE, ROPE, VD = 256, 256, 128, 64, 128
HEADS = 4
DQK = 64
QH = NOPE + ROPE
KVH = NOPE + VD
DQ0 = QR + KVR + ROPE
DK0 = DQ0 + HEADS * 2 * DQK
DV0 = DK0 + HEADS * 2 * DQK
GROUPS, PER_GROUP = 4, 8
EXPERTS = GROUPS * PER_GROUP
FE = 512
KE = FE // P
Y_BLOCKS = 50
MAX_BLOCKS = 48
FF = 2816
KF = FF // P
LAMBDA_INIT = 0.2
BIG = 3.0e38


class Program:
    pass


def sems(nc, g, names):
    made = [nc.alloc_semaphore(n) for n in names.split()]
    g.sems += made
    return made


def clear_sems(nc, g):
    nc.clear_and_free_semaphores(g.sems)
    nc.all_engine_barrier()
    g.sems = []


def load_constants(nc, g, a):
    rows = [[("norm1_g", a["norm1_g"], 8), ("norm2_g", a["norm2_g"], 8), ("q_g", a["q_a_norm_g"], 2),
             ("kv_g", a["kv_a_norm_g"], 2), ("sub_g", a["subln_g"], 1),
             ("g0", a["norm_gains_2"][0, 0:1, :], 8), ("g2", a["norm_gains_2"][0, 2:3, :], 8),
             ("b_ada", a["b_ada"], 48)],
            [("b_ada2", a["ada_b_2"], 48), ("conv_w", a["conv_w_2"][0, :, :], 24)]]
    with ExitStack() as ctx:
        const_in, x_in, rows_in, lam_in, rows_clear, turned, vec_ready, prod, lam_sum, lam_exp, ones_ready = sems(nc, g, "const_in x_in rows_in lam_in rows_clear turned vec_ready prod lam_sum lam_exp ones_ready")
        vrow = ctx.enter_context(nc.sbuf_tensor("vrow", [P, 2, P], F32))
        lamv = ctx.enter_context(nc.sbuf_tensor("lamv", [P, 4, DQK], F32))
        lamp = ctx.enter_context(nc.sbuf_tensor("lamp", [P, 2, DQK], F32))
        lams = ctx.enter_context(nc.sbuf_tensor("lams", [P, 2], F32))
        lame = ctx.enter_context(nc.sbuf_tensor("lame", [P, 2], F32))
        pv = ctx.enter_context(nc.psum_tensor("pv", [P, 2, P], F32))
        g.col = {}
        n_rows = 0
        with nc.Block() as block:

            @block.sync
            def _(sp):
                nonlocal n_rows
                sp.dma_start(g.ident[:], a["const_ident"]).then_inc(const_in, 16)
                sp.dma_start(g.cs[:], a["const_rope"].rearrange("s p t -> p s t")).then_inc(const_in, 16)
                sp.wait_ge(rows_clear, 1)
                for j, group in enumerate(rows):
                    at = 0
                    for name, src, n in group:
                        pat = "a (r q) -> (a r) q"
                        sp.dma_start(vrow[at:at + n, j, :], src.rearrange(pat, q=P)).then_inc(rows_in, 16)
                        g.col[name] = g.vcol[:, j, at:at + n]
                        at += n
                        n_rows += 1
                sp.dma_start(g.x[:], a["x"][0].rearrange("(n p) d -> p n d", p=P)).then_inc(x_in, 16)
                sp.wait_ge(x_in, 16)

            @block.scalar
            def _(act):
                for i, name in enumerate(("lambda_q1", "lambda_k1", "lambda_q2", "lambda_k2")):
                    act.dma_start(lamv[:, i, :], a[name][0].partition_broadcast(P)).then_inc(lam_in, 16)
                act.wait_ge(lam_sum, 2)
                act.activation(lame[:], lams[:], ACT.Exp).then_inc(lam_exp, 1)

            @block.tensor
            def _(pe):
                pe.wait_ge(const_in, 32)
                pe.wait_ge(rows_in, 16 * sum(len(r) for r in rows))
                for j in range(2):
                    pe.transpose(pv[:, j, :], vrow[:, j, :], g.ident[:]).then_inc(turned, 1)

            @block.vector
            def _(dve):
                dve.memset(vrow[:], 0.0).then_inc(rows_clear, 1)
                dve.memset(g.ones[:], 1.0).then_inc(ones_ready, 1)
                dve.memset(g.eps[:], EPS).then_inc(ones_ready, 1)
                dve.wait_ge(lam_in, 64)
                for i in range(2):
                    dve.tensor_tensor(lamp[:, i, :], lamv[:, 2 * i, :], lamv[:, 2 * i + 1, :], ALU.mult).then_inc(prod, 1)
                dve.wait_ge(prod, 2)
                for i in range(2):
                    dve.tensor_reduce(lams[:, i:i + 1], lamp[:, i, :], AX_X, ALU.add).then_inc(lam_sum, 1)
                dve.wait_ge(lam_exp, 1)
                dve.scalar_tensor_tensor(out=g.neg_lam[:], in0=lame[:, 1:2], scalar=-LAMBDA_INIT,
                                         in1=lame[:, 0:1], op0=ALU.add, op1=ALU.subtract).then_inc(lam_sum, 1)
                dve.wait_ge(turned, 2)
                dve.tensor_copy(g.vcol[:], pv[:]).then_inc(vec_ready, 1)


def modulation(nc, g, tag, c, w, bias, bias_col, mod_col, gate_row):
    with ExitStack() as ctx:
        c_in, bias_in, c_ready, sec_in0, sec_in1, sec_in2, sec_free, part, summed, acc_free, col_ps, row_ps, col_free, row_free = sems(nc, g, " ".join(tag + s for s in "c_in bias_in c_ready sec_in0 sec_in1 sec_in2 sec_free part summed acc_free col_ps row_ps col_free row_free".split()))
        sec_in = (sec_in0, sec_in1, sec_in2)
        ct = ctx.enter_context(nc.sbuf_tensor(tag + "ct", [P, KD], F32))
        cs = ctx.enter_context(nc.sbuf_tensor(tag + "cs", [P, KD], F32))
        sec = ctx.enter_context(nc.sbuf_tensor(tag + "sec", [P, 3, KD, D], F32))
        acc = ctx.enter_context(nc.sbuf_tensor(tag + "acc", [P, 3, D], F32))
        pcol = ctx.enter_context(nc.psum_tensor(tag + "pcol", [P, 16], F32))
        prow = ctx.enter_context(nc.psum_tensor(tag + "prow", [P, D], F32))
        w_v = w[0].rearrange("(p k) n -> p k n", k=KD)
        with nc.Block() as block:

            @block.sync
            def _(sp):
                sp.dma_start(ct[:], c[0].rearrange("(p k) -> p k", k=KD)).then_inc(c_in, 16)
                for i in range(2):
                    sp.dma_start(gate_row[:, i, :], bias[0, (3 * i + 2) * D:(3 * i + 3) * D].partition_broadcast(P)).then_inc(bias_in, 16)
                with sp.Fori(0, 2) as i:
                    for s in range(3):
                        sp.wait_ge(sec_free, 3 * i + s + 1)
                        sp.dma_start(sec[:, s, :, :], w_v[:, :, ds((3 * i + s) * D, D)]).then_inc(sec_in[s], 16)

            @block.scalar
            def _(act):
                act.wait_ge(c_in, 16)
                act.activation(cs[:], ct[:], ACT.Silu).then_inc(c_ready, 1)

            @block.vector
            def _(dve):
                dve.sem_inc(sec_free, 3)
                dve.sem_inc(col_free, 1)
                dve.sem_inc(row_free, 1)
                dve.wait_ge(c_ready, 1)
                dve.wait_ge(bias_in, 32)
                with dve.Fori(0, 2) as i:
                    for s in range(3):
                        dve.wait_ge(sec_in[s], 16 * i + 16)
                        if s == 0:
                            dve.wait_ge(acc_free, i + 1)
                        for k in range(KD):
                            if k == 0:
                                o = dve.tensor_scalar(acc[:, s, :], sec[:, s, k, :], cs[:, 0:1], None, ALU.mult)
                            else:
                                dve.wait_ge(part, 21 * i + 7 * s + k)
                                o = dve.scalar_tensor_tensor(out=acc[:, s, :], in0=sec[:, s, k, :], scalar=cs[:, k:k + 1],
                                                             in1=acc[:, s, :], op0=ALU.mult, op1=ALU.add)
                            if k < KD - 1:
                                o.then_inc(part, 1)
                        o.then_inc(summed, 1)
                        dve.wait_ge(summed, 3 * i + s + 1)
                        dve.sem_inc(sec_free, 1)
                    dve.wait_ge(col_ps, i + 1)
                    dve.tensor_tensor(mod_col[:, ds(i, 1), :], pcol[:].unsqueeze(1),
                                      bias_col[:, ds(24 * i, 16)].unsqueeze(1), ALU.add).then_inc(col_free, 1)
                    dve.wait_ge(row_ps, i + 1)
                    dve.tensor_tensor(gate_row[:, ds(i, 1), :], prow[:].unsqueeze(1), gate_row[:, ds(i, 1), :], ALU.add).then_inc(row_free, 1)

            @block.tensor
            def _(pe):
                pe.sem_inc(acc_free, 1)
                with pe.Fori(0, 2) as i:
                    pe.wait_ge(summed, 3 * i + 2)
                    pe.wait_ge(col_free, i + 1)
                    for j in range(16):
                        o = pe.matmul(pcol[:, j:j + 1], acc[:, j // KD, (j % KD) * P:(j % KD + 1) * P], g.ones[:, 0:1],
                                      start=True, stop=True)
                    o.then_inc(col_ps, 1)
                    pe.wait_ge(summed, 3 * i + 3)
                    pe.wait_ge(row_free, i + 1)
                    for h in range(2):
                        o = pe.matmul(prow[:, h * HALF:(h + 1) * HALF], g.ones[:], acc[:, 2, h * HALF:(h + 1) * HALF], start=True, stop=True)
                    o.then_inc(row_ps, 1)
                    pe.wait_ge(row_ps, i + 1)
                    pe.sem_inc(acc_free, 1)


def norm_transposed(nc, g, tag, gain, mod, out_t, keep=None):
    with ExitStack() as ctx:
        sq, root, rstd_ready, ab, staged, stage_free, turned, turned_free, row_ready, row_out0, row_out1 = sems(nc, g, " ".join(tag + s for s in "sq root rstd_ready ab staged stage_free turned turned_free row_ready row_out0 row_out1".split()))
        row_out = (row_out0, row_out1)
        junk = ctx.enter_context(nc.sbuf_tensor(tag + "junk", [P, D], F32))
        ss = ctx.enter_context(nc.sbuf_tensor(tag + "ss", [P, NT], F32))
        rs = ctx.enter_context(nc.sbuf_tensor(tag + "rs", [P, NT], F32))
        rstd = ctx.enter_context(nc.sbuf_tensor(tag + "rstd", [P, NT], F32))
        stage = ctx.enter_context(nc.sbuf_tensor(tag + "stage", [P, 2, NT, P], F32))
        rows = ctx.enter_context(nc.sbuf_tensor(tag + "rows", [P, 2, D], F32)) if keep is not None else None
        pt = ctx.enter_context(nc.psum_tensor(tag + "pt", [P, 2, T], F32))
        with nc.Block() as block:

            @block.scalar
            def _(act):
                for n in range(NT):
                    if n:
                        act.wait_ge(sq, n)
                    act.activation(junk[:], g.x[:, n, :], ACT.Square, accum_out=ss[:, n:n + 1]).then_inc(sq, 1)
                act.wait_ge(sq, NT)
                act.activation(rs[:], ss[:], ACT.Sqrt, bias=g.eps[:], scale=1.0 / D).then_inc(root, 1)
                act.wait_ge(ab, 1)
                with act.Fori(0, KD // 2) as i:
                    for b in range(2):
                        act.wait_ge(turned, 2 * i + b + 1)
                        act.activation(out_t[:, ds(2 * i + b, 1), :], pt[:, b:b + 1, :], ACT.Identity,
                                       bias=g.b_col[:, ds(2 * i + b, 1)], scale=g.a_col[:, ds(2 * i + b, 1)]).then_inc(turned_free, 1)

            @block.vector
            def _(dve):
                dve.sem_inc(stage_free, 2)
                dve.scalar_tensor_tensor(out=g.a_col[:], in0=mod[:, 8:16], scalar=1.0, in1=gain, op0=ALU.add, op1=ALU.mult)
                dve.tensor_copy(g.b_col[:], mod[:, 0:8]).then_inc(ab, 1)
                dve.wait_ge(root, 1)
                dve.reciprocal(rstd[:], rs[:]).then_inc(rstd_ready, 1)
                dve.wait_ge(rstd_ready, 1)
                with dve.Fori(0, KD // 2) as i:
                    for b in range(2):
                        dve.wait_ge(stage_free, 2 * i + b + 1)
                        dve.tensor_tensor(stage[:, b, :, :], g.x[:, :, ds((2 * i + b) * P, P)],
                                          rstd[:].unsqueeze(2).broadcast_to([P, NT, P]), ALU.mult).then_inc(staged, 1)
                if keep is not None:
                    for n in range(NT):
                        if n >= 2:
                            dve.wait_ge(row_out[n % 2], 16 * (n // 2))
                        dve.tensor_scalar(rows[:, n % 2, :], g.x[:, n, :], rstd[:, n:n + 1], None, ALU.mult).then_inc(row_ready, 1)

            @block.tensor
            def _(pe):
                pe.sem_inc(turned_free, 2)
                with pe.Fori(0, KD // 2) as i:
                    for b in range(2):
                        pe.wait_ge(staged, 2 * i + b + 1)
                        pe.wait_ge(turned_free, 2 * i + b + 1)
                        for n in range(NT):
                            o = pe.transpose(pt[:, b, n * P:(n + 1) * P], stage[:, b, n, :], g.ident[:])
                        o.then_inc(turned, 1)
                        pe.wait_ge(turned, 2 * i + b + 1)
                        pe.sem_inc(stage_free, 1)

            if keep is not None:
                @block.sync
                def _(sp):
                    for n in range(NT):
                        sp.wait_ge(row_ready, n + 1)
                        sp.dma_start(keep[n * P:(n + 1) * P, :], rows[:, n % 2, :]).then_inc(row_out[n % 2], 16)
                    for b in range(2):
                        sp.wait_ge(row_out[b], 8 * NT)


def rope_rotate(dve, out, ps, g, tmp, rows, step, k0):
    dve.tensor_tensor(tmp[0:rows, 0, :], ps[0:rows, :], g.cs[0:rows, 0, :], ALU.mult)
    for q in range(rows // 32):
        o = dve.tensor_tensor(tmp[32 * q:32 * q + 32, 1, :], ps[32 * (q ^ 1):32 * (q ^ 1) + 32, :],
                              g.cs[32 * q:32 * q + 32, 1, :], ALU.mult)
    o.then_inc(step, 1)
    dve.wait_ge(step, k0 + 1)
    return dve.tensor_tensor(out, tmp[0:rows, 0, :], tmp[0:rows, 1, :], ALU.add)


def latents(nc, g, a):
    with ExitStack() as ctx:
        w_in, proj, raw, squared, ssq, rooted, recip_r, lat_done, ps_free, rope_step = sems(nc, g, "l_w_in l_proj l_raw l_squared l_ssq l_rooted l_recip l_done l_ps_free l_rope")
        w = ctx.enter_context(nc.sbuf_tensor("l_w", [P, KD, DQ0], F32))
        raws, sqs = g.mix[:, 0:4, :], g.mix[:, 4:8, :]
        root = ctx.enter_context(nc.sbuf_tensor("l_root", [P, 2, T], F32))
        rinv = ctx.enter_context(nc.sbuf_tensor("l_rinv", [P, 2, T], F32))
        tmp = ctx.enter_context(nc.sbuf_tensor("l_tmp", [P, 2, T], F32))
        ps = ctx.enter_context(nc.psum_tensor("l_ps", [P, 2, T], F32))
        pss = ctx.enter_context(nc.psum_tensor("l_pss", [P, 2, T], F32))
        with nc.Block() as block:

            @block.sync
            def _(sp):
                sp.dma_start(w[:], a["w_in"][0].rearrange("(k p) n -> p k n", p=P)[:, :, 0:DQ0]).then_inc(w_in, 16)

            @block.tensor
            def _(pe):
                pe.wait_ge(w_in, 16)
                for c in range(5):
                    m = P if c < 4 else ROPE
                    if c >= 2:
                        pe.wait_ge(ps_free, c - 1)
                    for h in range(2):
                        for k in range(KD):
                            o = pe.matmul(ps[0:m, c % 2, h * HALF:(h + 1) * HALF], w[:, k, c * P:c * P + m],
                                          g.ht[:, k, h * HALF:(h + 1) * HALF], start=(k == 0), stop=(k == KD - 1))
                    o.then_inc(proj, 1)
                for j in range(2):
                    pe.wait_ge(squared, 2 * j + 2)
                    for h in range(2):
                        for c in range(2):
                            o = pe.matmul(pss[:, j, h * HALF:(h + 1) * HALF], g.ones[:], sqs[:, 2 * j + c, h * HALF:(h + 1) * HALF],
                                          start=(c == 0), stop=(c == 1))
                    o.then_inc(ssq, 1)

            @block.scalar
            def _(act):
                for c in range(4):
                    act.wait_ge(proj, c + 1)
                    act.activation(raws[:, c, :], ps[:, c % 2, :], ACT.Copy).then_inc(raw, 1)
                    act.wait_ge(raw, c + 1)
                    act.sem_inc(ps_free, 1)
                    act.activation(sqs[:, c, :], raws[:, c, :], ACT.Square).then_inc(squared, 1)
                for j in range(2):
                    act.wait_ge(ssq, j + 1)
                    act.activation(root[:, j, :], pss[:, j, :], ACT.Sqrt, bias=g.eps[:], scale=1.0 / QR).then_inc(rooted, 1)

            @block.vector
            def _(dve):
                dve.wait_ge(proj, 5)
                rope_rotate(dve, g.kpe[:], ps[:, 0, :], g, tmp, ROPE, rope_step, 0).then_inc(lat_done, 1)
                for j, gain in enumerate(("q_g", "kv_g")):
                    dve.wait_ge(rooted, j + 1)
                    dve.reciprocal(rinv[:, j, :], root[:, j, :]).then_inc(recip_r, 1)
                    dve.wait_ge(recip_r, j + 1)
                    for c in range(2):
                        dve.scalar_tensor_tensor(out=g.lat[:, 2 * j + c, :], in0=raws[:, 2 * j + c, :], scalar=g.col[gain][:, c:c + 1],
                                                 in1=rinv[:, j, :], op0=ALU.mult, op1=ALU.mult).then_inc(lat_done, 1)


def attention(nc, g, a, tag, diff):
    maps = 2 if diff else 1
    scale = float(DQK if diff else QH) ** -0.5
    kin = KD if diff else QR // P
    wcols = 3 * P if diff else QH + KVH
    uses = (2 + NT, 1 + NT) if diff else (2 + NT // 2, 2 + NT // 2)
    n_proj = 3 if diff else 4
    with ExitStack() as ctx:
        names = ("w_in w_used proj q_ready qpe_ready k_ready v_ready rope_step free0 free1 scored maxed nmax expd sumr "
                 "probs turned copied pt_free pv mixed t_free combined p_free")
        (w_in, w_used, proj, q_ready, qpe_ready, k_ready, v_ready, rope_step, free0, free1, scored, maxed, nmax, expd, sumr,
         probs, turned, copied, pt_free, pv, mixed, t_free, combined, p_free) = sems(nc, g, " ".join(tag + s for s in names.split()))
        free = (free0, free1)

        def sb(name, shape):
            return ctx.enter_context(nc.sbuf_tensor(tag + name, shape, F32))

        w = sb("w", [P, kin, wcols])
        qt = sb("qt", [P, T])
        kt = sb("kt", [P, T])
        qpe = sb("qpe", [ROPE, T]) if not diff else None
        v = sb("v", [P, NT, P])
        e = sb("e", [P, 2, maps, T])
        pr = sb("pr", [P, 2, T]) if diff else None
        tmp = pr if diff else e[:, :, 0, :]
        pt = sb("pt", [P, 2, NT, HALF])
        mx = sb("mx", [P, 2, maps])
        nm = sb("nm", [P, 2, maps])
        sm = sb("sm", [P, 2, maps])
        ri = sb("ri", [P, 2, maps])
        r2 = sb("r2", [P, 2])
        ps = [ctx.enter_context(nc.psum_tensor(tag + f"ps{i}", [P, T], F32)) for i in range(2)]
        ptr = ctx.enter_context(nc.psum_tensor(tag + "ptr", [P, NT, P], F32))
        po = ctx.enter_context(nc.psum_tensor(tag + "po", [P, HALF], F32))

        def slot(i, m):
            return (m, i + 2 - m) if diff else (i % 2, 2 + i // 2)

        if diff:
            win = a["w_in"][0].rearrange("(k p) n -> p k n", p=P)
        else:
            wq = a["w_q_up"][0].rearrange("(k p) n -> p k n", p=P)
            wkv = a["w_kv_up"][0].rearrange("(k p) n -> p k n", p=P)
        n_w = 3 if diff else 2

        with nc.Block() as block:

            @block.sync
            def _(sp):
                with sp.Fori(0, HEADS) as h:
                    sp.wait_ge(w_used, h + 1)
                    if diff:
                        for j, c0 in enumerate((DQ0, DK0, DV0)):
                            sp.dma_start(w[:, :, j * P:(j + 1) * P], win[:, :, ds(c0 + h * P, P)]).then_inc(w_in, 16)
                    else:
                        sp.dma_start(w[:, :, 0:QH], wq[:, :, ds(h * QH, QH)]).then_inc(w_in, 16)
                        sp.dma_start(w[:, :, QH:], wkv[:, :, ds(h * KVH, KVH)]).then_inc(w_in, 16)

            @block.tensor
            def _(pe):
                pe.sem_inc(free0, 1)
                pe.sem_inc(free1, 1)
                pe.sem_inc(w_used, 1)
                pe.sem_inc(pv, 1)
                with pe.Fori(0, HEADS) as h:
                    pe.wait_ge(w_in, 16 * n_w * (h + 1))

                    def project(buf, use, c0, m, src, c_src):
                        pe.wait_ge(free[buf], uses[buf] * h + use + 1)
                        for hf in range(2):
                            for k in range(kin):
                                o = pe.matmul(ps[buf][0:m, hf * HALF:(hf + 1) * HALF], w[:, k, c0:c0 + m],
                                              src[:, c_src + k, hf * HALF:(hf + 1) * HALF], start=(k == 0), stop=(k == kin - 1))
                        o.then_inc(proj, 1)

                    def values(buf, use, c0, src, c_src):
                        pe.wait_ge(free[buf], uses[buf] * h + use + 1)
                        for n in range(NT):
                            for k in range(kin):
                                o = pe.matmul(ps[buf][:, n * P:(n + 1) * P], src[:, c_src + k, n * P:(n + 1) * P],
                                              w[:, k, c0:c0 + P], start=(k == 0), stop=(k == kin - 1))
                        o.then_inc(proj, 1)

                    if diff:
                        project(0, 0, 0, P, g.ht, 0)
                        project(1, 0, P, P, g.ht, 0)
                        values(0, 1, 2 * P, g.ht, 0)
                    else:
                        project(0, 0, NOPE, ROPE, g.lat, 0)
                        project(1, 0, 0, NOPE, g.lat, 0)
                        project(0, 1, QH, NOPE, g.lat, 2)
                        values(1, 1, QH + NOPE, g.lat, 2)
                    pe.wait_ge(proj, n_proj * (h + 1))
                    pe.sem_inc(w_used, 1)
                    pe.wait_ge(q_ready, h + 1)
                    if not diff:
                        pe.wait_ge(qpe_ready, h + 1)
                    pe.wait_ge(k_ready, h + 1)

                    def scores(i):
                        for m in range(maps):
                            buf, use = slot(i, m)
                            pe.wait_ge(free[buf], uses[buf] * h + use + 1)
                            lo = m * DQK
                            hi = lo + DQK if diff else P
                            for hf in range(2):
                                cols = slice(hf * HALF, (hf + 1) * HALF)
                                o = pe.matmul(ps[buf][:, cols], qt[lo:hi, i * P:(i + 1) * P], kt[lo:hi, cols], start=True, stop=diff)
                                if not diff:
                                    o = pe.matmul(ps[buf][:, cols], qpe[:, i * P:(i + 1) * P], g.kpe[:, cols], start=False, stop=True)
                            o.then_inc(scored, 1)

                    def turn(i):
                        pe.wait_ge(probs, NT * h + i + 1)
                        pe.wait_ge(t_free, NT * h + i + 1)
                        src = pr[:, i % 2, :] if diff else e[:, i % 2, 0, :]
                        for n in range(NT):
                            o = pe.transpose(ptr[:, n, :], src[:, n * P:(n + 1) * P], g.ident[:])
                        o.then_inc(turned, 1)

                    def weigh(j):
                        pe.wait_ge(copied, NT * h + 4 * j + 4)
                        pe.wait_ge(v_ready, h + 1)
                        pe.wait_ge(mixed, 2 * h + j + 1)
                        for n in range(NT):
                            o = pe.matmul(po[:], v[:, n, :], pt[:, j, n, :], start=(n == 0), stop=(n == NT - 1))
                        o.then_inc(pv, 1)

                    for i in range(NT + 1):
                        if i < NT:
                            scores(i)
                        if i >= 1:
                            turn(i - 1)
                        if i == 5:
                            weigh(0)
                    weigh(1)

            @block.scalar
            def _(act):
                act.sem_inc(t_free, 1)
                with act.Fori(0, HEADS) as h:
                    if diff:
                        act.wait_ge(proj, 3 * h + 3)
                        act.wait_ge(pv, 2 * h + 1)
                        act.activation(v[:].rearrange("p n d -> p (n d)"), ps[0][:], ACT.Copy).then_inc(v_ready, 1)
                        act.wait_ge(v_ready, h + 1)
                        act.sem_inc(free0, 1)
                    else:
                        act.wait_ge(proj, 4 * h + 2)
                        act.activation(qt[:], ps[1][:], ACT.Copy).then_inc(q_ready, 1)
                        act.wait_ge(q_ready, h + 1)
                        act.sem_inc(free1, 1)
                        act.wait_ge(proj, 4 * h + 3)
                        act.activation(kt[:], ps[0][:], ACT.Copy).then_inc(k_ready, 1)
                        act.wait_ge(k_ready, h + 1)
                        act.sem_inc(free0, 1)
                        act.wait_ge(proj, 4 * h + 4)
                        act.wait_ge(pv, 2 * h + 1)
                        act.activation(v[:].rearrange("p n d -> p (n d)"), ps[1][:], ACT.Copy).then_inc(v_ready, 1)
                        act.wait_ge(v_ready, h + 1)
                        act.sem_inc(free1, 1)

                    def copy_turned(i):
                        act.wait_ge(turned, NT * h + i + 1)
                        if i % 4 == 0:
                            act.wait_ge(pv, 2 * h + 1)
                        act.activation(pt[:, i // 4, :, (i % 4) * P:(i % 4 + 1) * P], ptr[:], ACT.Copy).then_inc(copied, 1)
                        act.wait_ge(copied, NT * h + i + 1)
                        act.sem_inc(t_free, 1)

                    for i in range(NT):
                        for m in range(maps):
                            buf, use = slot(i, m)
                            act.wait_ge(nmax, maps * (NT * h + i) + m + 1)
                            if m == 0:
                                act.wait_ge(p_free, NT * h + i + 1)
                            act.activation(e[:, i % 2, m, :], ps[buf][:], ACT.Exp, bias=nm[:, i % 2, m:m + 1], scale=scale,
                                           accum_out=sm[:, i % 2, m:m + 1]).then_inc(expd, 1)
                            act.wait_ge(expd, maps * (NT * h + i) + m + 1)
                            act.sem_inc(free[buf], 1)
                        if i >= 1:
                            copy_turned(i - 1)
                    copy_turned(NT - 1)

            @block.vector
            def _(dve):
                dve.sem_inc(p_free, 2)
                dve.sem_inc(mixed, 1)
                with dve.Fori(0, HEADS) as h:
                    if diff:
                        dve.wait_ge(proj, 3 * h + 1)
                        rope_rotate(dve, qt[:], ps[0], g, tmp, P, rope_step, 2 * h).then_inc(q_ready, 1)
                        dve.wait_ge(q_ready, h + 1)
                        dve.sem_inc(free0, 1)
                        dve.wait_ge(proj, 3 * h + 2)
                        rope_rotate(dve, kt[:], ps[1], g, tmp, P, rope_step, 2 * h + 1).then_inc(k_ready, 1)
                        dve.wait_ge(k_ready, h + 1)
                        dve.sem_inc(free1, 1)
                    else:
                        dve.wait_ge(proj, 4 * h + 1)
                        rope_rotate(dve, qpe[:], ps[0], g, tmp, ROPE, rope_step, h).then_inc(qpe_ready, 1)
                        dve.sem_inc(free0, 1)

                    def find_max(i):
                        for m in range(maps):
                            n = maps * (NT * h + i) + m
                            dve.wait_ge(scored, n + 1)
                            dve.tensor_reduce(mx[:, i % 2, m:m + 1], ps[slot(i, m)[0]][:], AX_X, ALU.max).then_inc(maxed, 1)
                            dve.wait_ge(maxed, n + 1)
                            dve.tensor_scalar(nm[:, i % 2, m:m + 1], mx[:, i % 2, m:m + 1], -scale, None, ALU.mult).then_inc(nmax, 1)

                    def finish(i):
                        b = i % 2
                        dve.wait_ge(expd, maps * (NT * h + i + 1))
                        dve.reciprocal(ri[:, b, :], sm[:, b, :]).then_inc(sumr, 1)
                        if not diff:
                            dve.wait_ge(sumr, NT * h + i + 1)
                            dve.tensor_scalar(e[:, b, 0, :], e[:, b, 0, :], ri[:, b, 0:1], None, ALU.mult).then_inc(probs, 1)
                            return
                        dve.wait_ge(sumr, 2 * (NT * h + i) + 1)
                        dve.tensor_scalar(r2[:, b:b + 1], ri[:, b, 1:2], g.neg_lam[:], None, ALU.mult).then_inc(sumr, 1)
                        dve.wait_ge(sumr, 2 * (NT * h + i) + 2)
                        dve.tensor_scalar(e[:, b, 1, :], e[:, b, 1, :], r2[:, b:b + 1], None, ALU.mult).then_inc(combined, 1)
                        dve.wait_ge(combined, NT * h + i + 1)
                        dve.scalar_tensor_tensor(out=pr[:, b, :], in0=e[:, b, 0, :], scalar=ri[:, b, 0:1], in1=e[:, b, 1, :],
                                                 op0=ALU.mult, op1=ALU.add).then_inc(probs, 1)

                    def release(i):
                        dve.wait_ge(turned, NT * h + i + 1)
                        dve.sem_inc(p_free, 1)

                    for i in range(NT):
                        if i >= 2:
                            release(i - 2)
                        find_max(i)
                        finish(i)
                        if i == 6:
                            dve.wait_ge(pv, 2 * h + 2)
                            dve.tensor_copy(g.mix[:, ds((HEADS if diff else 0) + h, 1), 0:HALF], po[:].unsqueeze(1)).then_inc(mixed, 1)
                    release(NT - 2)
                    release(NT - 1)
                    dve.wait_ge(pv, 2 * h + 3)
                    dve.tensor_copy(g.mix[:, ds((HEADS if diff else 0) + h, 1), HALF:T], po[:].unsqueeze(1)).then_inc(mixed, 1)


def head_norm(nc, g):
    with ExitStack() as ctx:
        squared, summed, rooted, inv, done = sems(nc, g, "hn_squared hn_summed hn_rooted hn_inv hn_done")
        sq = ctx.enter_context(nc.sbuf_tensor("hn_sq", [P, HEADS, T], F32))
        root = ctx.enter_context(nc.sbuf_tensor("hn_root", [P, HEADS, T], F32))
        gs = ctx.enter_context(nc.sbuf_tensor("hn_gs", [P, 1], F32))
        ps = ctx.enter_context(nc.psum_tensor("hn_ps", [P, HEADS, T], F32))
        with nc.Block() as block:

            @block.scalar
            def _(act):
                for h in range(HEADS):
                    act.activation(sq[:, h, :], g.mix[:, HEADS + h, :], ACT.Square).then_inc(squared, 1)
                for h in range(HEADS):
                    act.wait_ge(summed, h + 1)
                    act.activation(root[:, h, :], ps[:, h, :], ACT.Sqrt, bias=g.eps[:], scale=1.0 / P).then_inc(rooted, 1)

            @block.tensor
            def _(pe):
                for h in range(HEADS):
                    pe.wait_ge(squared, h + 1)
                    for hf in range(2):
                        o = pe.matmul(ps[:, h, hf * HALF:(hf + 1) * HALF], g.ones[:], sq[:, h, hf * HALF:(hf + 1) * HALF], start=True, stop=True)
                    o.then_inc(summed, 1)

            @block.vector
            def _(dve):
                dve.tensor_scalar(gs[:], g.col["sub_g"], 1.0 - LAMBDA_INIT, None, ALU.mult).then_inc(inv, 1)
                for h in range(HEADS):
                    dve.wait_ge(rooted, h + 1)
                    dve.reciprocal(root[:, h, :], root[:, h, :]).then_inc(inv, 1)
                    dve.wait_ge(inv, h + 2)
                    dve.scalar_tensor_tensor(out=g.mix[:, HEADS + h, :], in0=g.mix[:, HEADS + h, :], scalar=gs[:], in1=root[:, h, :],
                                             op0=ALU.mult, op1=ALU.mult).then_inc(done, 1)


def project_rows(nc, g, tag, src_t, w_dram, gate, gain=None):
    with ExitStack() as ctx:
        w_in, gain_in, gg, done, freed, squared, rooted, inv, scaled, added = sems(nc, g, " ".join(tag + s for s in "w_in gain_in gg done freed squared rooted inv scaled added".split()))
        w = ctx.enter_context(nc.sbuf_tensor(tag + "w", [P, KD, D], F32))
        gr = ctx.enter_context(nc.sbuf_tensor(tag + "gr", [P, D], F32)) if gain is not None else None
        junk = ctx.enter_context(nc.sbuf_tensor(tag + "junk", [P, 2, D], F32)) if gain is not None else None
        ss = ctx.enter_context(nc.sbuf_tensor(tag + "ss", [P, 3, NT], F32))
        t = ctx.enter_context(nc.sbuf_tensor(tag + "t", [P, 2, D], F32))
        ps = ctx.enter_context(nc.psum_tensor(tag + "ps", [P, 2, D], F32))
        with nc.Block() as block:

            @block.sync
            def _(sp):
                if gain is not None:
                    sp.dma_start(gr[:], gain.partition_broadcast(P)).then_inc(gain_in, 16)
                wv = w_dram.rearrange("(k p) n -> p k n", p=P)
                for k in range(KD):
                    sp.dma_start(w[:, k, :], wv[:, k, :]).then_inc(w_in, 16)

            @block.tensor
            def _(pe):
                pe.wait_ge(w_in, 16 * KD)
                for n in range(NT):
                    if n >= 2:
                        pe.wait_ge(freed, n - 1)
                    for h in range(2):
                        for k in range(KD):
                            o = pe.matmul(ps[:, n % 2, h * HALF:(h + 1) * HALF], src_t[:, k, n * P:(n + 1) * P],
                                          w[:, k, h * HALF:(h + 1) * HALF], start=(k == 0), stop=(k == KD - 1))
                    o.then_inc(done, 1)

            if gain is not None:
                @block.scalar
                def _(act):
                    for n in range(NT):
                        act.wait_ge(done, n + 1)
                        if n >= 2:
                            act.wait_ge(squared, n - 1)
                        act.activation(junk[:, n % 2, :], ps[:, n % 2, :], ACT.Square, accum_out=ss[:, 0, n:n + 1]).then_inc(squared, 1)
                        act.wait_ge(squared, n + 1)
                        act.activation(ss[:, 1, n:n + 1], ss[:, 0, n:n + 1], ACT.Sqrt, bias=g.eps[:], scale=1.0 / D).then_inc(rooted, 1)

            @block.vector
            def _(dve):
                row = gate
                if gain is not None:
                    dve.wait_ge(gain_in, 16)
                    dve.tensor_tensor(gr[:], gr[:], gate, ALU.mult).then_inc(gg, 1)
                    dve.wait_ge(gg, 1)
                    row = gr[:]
                for n in range(NT):
                    if n >= 2:
                        dve.wait_ge(added, n - 1)
                    if gain is None:
                        dve.wait_ge(done, n + 1)
                        dve.tensor_tensor(t[:, n % 2, :], ps[:, n % 2, :], row, ALU.mult).then_inc(scaled, 1)
                    else:
                        dve.wait_ge(rooted, n + 1)
                        dve.reciprocal(ss[:, 2, n:n + 1], ss[:, 1, n:n + 1]).then_inc(inv, 1)
                        dve.wait_ge(inv, n + 1)
                        dve.scalar_tensor_tensor(out=t[:, n % 2, :], in0=ps[:, n % 2, :], scalar=ss[:, 2, n:n + 1], in1=row,
                                                 op0=ALU.mult, op1=ALU.mult).then_inc(scaled, 1)
                    dve.wait_ge(scaled, n + 1)
                    dve.sem_inc(freed, 1)

            @block.gpsimd
            def _(pool):
                for n in range(NT):
                    pool.wait_ge(scaled, n + 1)
                    pool.tensor_tensor(g.x[:, n, :], g.x[:, n, :], t[:, n % 2, :], ALU.add).then_inc(added, 1)


def route(nc, g, a):
    with ExitStack() as ctx:
        w_in, b_in, c_in, logit, pads, step, ex, prefix, scattered, zeroed, table_in, table_t, done = sems(nc, g, "r_w_in r_b_in r_c_in r_logit r_pads r_step r_ex r_prefix r_scattered r_zeroed r_table_in r_table_t r_done")

        def sb(name, shape, dt=F32):
            return ctx.enter_context(nc.sbuf_tensor("r_" + name, shape, dt))

        NL = GROUPS + EXPERTS
        wr = sb("wr", [P, KD, NL])
        br = sb("br", [P, NL])
        iota = sb("iota", [P, MAX_BLOCKS])
        tri = sb("tri", [P, P])
        tok = sb("tok", [P, NT])
        lg = sb("lg", [P, NT, NL])
        gl = sb("gl", [P, NT, 8])
        gm = sb("gm", [P, NT, 8])
        gi = sb("gi", [P, NT, 8], U32)
        gif = sb("gif", [P, NT])
        gd = sb("gd", [P, NT, GROUPS])
        gp = sb("gp", [P, NT])
        oh = sb("oh", [P, NT, GROUPS])
        em = sb("em", [P, NT, EXPERTS])
        tm = sb("tm", [P, NT, 8])
        ti = sb("ti", [P, NT, 8], U32)
        tif = sb("tif", [P, NT, 2])
        dl = sb("dl", [P, NT])
        hot = sb("hot", [P, 2, NT, EXPERTS])
        both = sb("both", [P, NT, EXPERTS])
        pos = sb("pos", [P, NT, EXPERTS])
        off = sb("off", [P, NT + 1, EXPERTS])
        nb = sb("nb", [P, EXPERTS])
        inc = sb("inc", [P, EXPERTS])
        one = sb("one", [P, EXPERTS])
        sel = sb("sel", [P, NT, EXPERTS])
        dst = sb("dst", [P, 2, NT])
        cmp = sb("cmp", [1, MAX_BLOCKS, EXPERTS])
        blk = sb("blk", [1, MAX_BLOCKS + 1])
        zero = sb("zero", [P, MAX_BLOCKS])
        rt = sb("rt", [MAX_BLOCKS, P])
        pl = ctx.enter_context(nc.psum_tensor("r_pl", [P, NT, 64], F32))
        pp = ctx.enter_context(nc.psum_tensor("r_pp", [P, HALF], F32))
        pn = ctx.enter_context(nc.psum_tensor("r_pn", [P, HALF], F32))
        prt = ctx.enter_context(nc.psum_tensor("r_prt", [P, MAX_BLOCKS], F32))
        NE = NT * EXPERTS
        with nc.Block() as block:

            @block.sync
            def _(sp):
                sp.dma_start(wr[:, :, 0:GROUPS], a["w_router_group"][0].rearrange("(k p) n -> p k n", p=P)).then_inc(w_in, 16)
                sp.dma_start(wr[:, :, GROUPS:], a["w_router_expert"][0].rearrange("(k p) n -> p k n", p=P)).then_inc(w_in, 16)
                sp.dma_start(br[:, 0:GROUPS], a["b_router_group"][0].partition_broadcast(P)).then_inc(b_in, 16)
                sp.dma_start(br[:, GROUPS:], a["b_router_expert"][0].partition_broadcast(P)).then_inc(b_in, 16)
                sp.dma_start(iota[:], a["const_iota"][0].partition_broadcast(P)).then_inc(c_in, 16)
                sp.dma_start(tri[:], a["const_before"]).then_inc(c_in, 16)
                sp.dma_start(tok[:], a["const_token"]).then_inc(c_in, 16)
                sp.wait_ge(pads, 1)
                sp.dma_start(g.row_token.rearrange("(p n) a -> p (n a)", p=P), zero[:]).then_inc(zeroed, 16)
                sp.wait_ge(scattered, 16 * 2 * NT)
                sp.dma_start(rt[:], g.row_token.rearrange("(n p) a -> n (p a)", p=P)).then_inc(table_in, 16)
                sp.wait_ge(table_in, 16)

            @block.tensor
            def _(pe):
                pe.wait_ge(w_in, 32)
                for n in range(NT):
                    for k in range(KD):
                        o = pe.matmul(pl[:, n, 0:NL], g.ht[:, k, n * P:(n + 1) * P], wr[:, k, :], start=(k == 0), stop=(k == KD - 1))
                o.then_inc(logit, 1)
                pe.wait_ge(ex, 2)
                pe.wait_ge(c_in, 48)
                bv = both[:].rearrange("p n e -> p (n e)")
                pe.matmul(pp[:, 0:NE], tri[:], bv, start=True, stop=True).then_inc(prefix, 1)
                pe.matmul(pn[:, 0:NE], g.ones[:], bv, start=True, stop=True).then_inc(prefix, 1)
                pe.wait_ge(table_in, 16)
                pe.transpose(prt[:], rt[:], g.ident[0:MAX_BLOCKS, 0:MAX_BLOCKS]).then_inc(table_t, 1)

            @block.scalar
            def _(act):
                act.wait_ge(ex, 1)
                act.activation(gd[:], gd[:], ACT.Exp).then_inc(done, 1)
                act.activation(dl[:], dl[:], ACT.Exp).then_inc(done, 1)

            @block.vector
            def _(dve):
                count = [0]

                def seq(o):
                    count[0] += 1
                    o.then_inc(step, 1)
                    dve.wait_ge(step, count[0])

                def bc(x, n):
                    return x.unsqueeze(2).broadcast_to([P, NT, n])

                dve.memset(zero[:], 0.0).then_inc(pads, 1)
                dve.memset(one[:], 1.0)
                dve.memset(off[:, 0, :], 0.0)
                seq(dve.memset(gl[:], -BIG))
                dve.wait_ge(logit, 1)
                dve.wait_ge(b_in, 32)
                dve.wait_ge(c_in, 48)
                seq(dve.tensor_tensor(lg[:], pl[:, :, 0:NL], br[:].unsqueeze(1).broadcast_to([P, NT, NL]), ALU.add))
                seq(dve.tensor_copy(gl[:, :, 0:GROUPS], lg[:, :, 0:GROUPS]))
                for n in range(NT):
                    o = dve.max(gm[:, n, :], gl[:, n, :])
                seq(o)
                for n in range(NT):
                    o = dve.max_index(gi[:, n, :], gm[:, n, :], gl[:, n, :])
                seq(o)
                seq(dve.tensor_copy(gif[:], gi[:, :, 0]))
                seq(dve.tensor_tensor(oh[:], iota[:, 0:GROUPS].unsqueeze(1).broadcast_to([P, NT, GROUPS]), bc(gif[:], GROUPS), ALU.is_equal))
                for n in range(NT):
                    o = dve.tensor_tensor(em[:, n, :].rearrange("p (a b) -> p a b", a=GROUPS),
                                          lg[:, n, GROUPS:].rearrange("p (a b) -> p a b", a=GROUPS),
                                          oh[:, n, :].unsqueeze(2).broadcast_to([P, GROUPS, PER_GROUP]), ALU.mult)
                seq(o)
                seq(dve.tensor_scalar(oh[:], oh[:], -1.0, BIG, ALU.add, ALU.mult))
                for n in range(NT):
                    o = dve.tensor_tensor(em[:, n, :].rearrange("p (a b) -> p a b", a=GROUPS),
                                          em[:, n, :].rearrange("p (a b) -> p a b", a=GROUPS),
                                          oh[:, n, :].unsqueeze(2).broadcast_to([P, GROUPS, PER_GROUP]), ALU.add)
                seq(o)
                for n in range(NT):
                    o = dve.max(tm[:, n, :], em[:, n, :])
                seq(o)
                for n in range(NT):
                    o = dve.max_index(ti[:, n, :], tm[:, n, :], em[:, n, :])
                seq(o)
                seq(dve.tensor_copy(tif[:], ti[:, :, 0:2]))
                seq(dve.tensor_tensor(gd[:], lg[:, :, 0:GROUPS], bc(gm[:, :, 0], GROUPS), ALU.subtract))
                dve.tensor_tensor(dl[:], tm[:, :, 1], tm[:, :, 0], ALU.subtract).then_inc(ex, 1)
                for s in range(2):
                    o = dve.tensor_tensor(hot[:, s, :, :], iota[:, 0:EXPERTS].unsqueeze(1).broadcast_to([P, NT, EXPERTS]),
                                          bc(tif[:, :, s], EXPERTS), ALU.is_equal)
                seq(o)
                dve.tensor_tensor(both[:], hot[:, 0], hot[:, 1], ALU.add).then_inc(ex, 1)
                dve.wait_ge(done, 2)
                seq(dve.tensor_reduce(gp[:], gd[:], AX_X, ALU.add))
                seq(dve.scalar_tensor_tensor(out=gp[:], in0=dl[:], scalar=1.0, in1=gp[:], op0=ALU.add, op1=ALU.mult))
                seq(dve.reciprocal(g.wt[:, 0, :], gp[:]))
                seq(dve.tensor_tensor(g.wt[:, 1, :], g.wt[:, 0, :], dl[:], ALU.mult))
                dve.wait_ge(prefix, 2)
                for n in range(NT):
                    seq(dve.tensor_tensor(off[:, n + 1, :], off[:, n, :], pn[:, n * EXPERTS:(n + 1) * EXPERTS], ALU.add))
                seq(dve.tensor_scalar(nb[:], off[:, NT, :], 0.0, None, ALU.is_gt))
                for j in range(1, NT):
                    seq(dve.scalar_tensor_tensor(out=nb[:], in0=off[:, NT, :], scalar=float(j * P), in1=nb[:], op0=ALU.is_gt, op1=ALU.add))
                seq(dve.tensor_tensor_scan(inc[:], one[:], nb[:], 0.0, ALU.mult, ALU.add))
                seq(dve.tensor_tensor(nb[:], inc[:], nb[:], ALU.subtract))
                seq(dve.tensor_scalar(nb[:], nb[:], float(P), None, ALU.mult))
                seq(dve.tensor_tensor(pos[:].rearrange("p n e -> p (n e)"), pp[:, 0:NE], off[:, 0:NT, :].rearrange("p n e -> p (n e)"), ALU.add))
                seq(dve.tensor_tensor(pos[:], pos[:], nb[:].unsqueeze(1).broadcast_to([P, NT, EXPERTS]), ALU.add))
                for s in range(2):
                    seq(dve.tensor_tensor(sel[:], hot[:, s], pos[:], ALU.mult))
                    seq(dve.tensor_reduce(dst[:, s, :], sel[:], AX_X, ALU.add))
                dve.tensor_copy(g.dest[:], dst[:]).then_inc(pads, 1)
                seq(dve.tensor_tensor(cmp[:], inc[0:1, :].unsqueeze(1).broadcast_to([1, MAX_BLOCKS, EXPERTS]),
                                      iota[0:1, :].unsqueeze(2).broadcast_to([1, MAX_BLOCKS, EXPERTS]), ALU.is_le))
                seq(dve.tensor_reduce(blk[:, 0:MAX_BLOCKS], cmp[:], AX_X, ALU.add))
                seq(dve.tensor_scalar(blk[:, 0:MAX_BLOCKS], blk[:, 0:MAX_BLOCKS], float(EXPERTS - 1), None, ALU.min))
                seq(dve.tensor_scalar(cmp[:, 0, 0:MAX_BLOCKS // 2], iota[0:1, 0:MAX_BLOCKS // 2], 2.0, None, ALU.mult))
                seq(dve.tensor_scalar(cmp[:, 1, 0:MAX_BLOCKS // 2], cmp[:, 0, 0:MAX_BLOCKS // 2], inc[0:1, EXPERTS - 1:EXPERTS], None, ALU.is_lt))
                seq(dve.tensor_reduce(blk[:, MAX_BLOCKS:], cmp[:, 1, 0:MAX_BLOCKS // 2], AX_X, ALU.add))
                seq(dve.tensor_copy(g.blocks[:], blk[:]))
                dve.wait_ge(table_t, 1)
                seq(dve.tensor_copy(g.rows[:], prt[:]))

            @block.gpsimd
            def _(pool):
                pool.wait_ge(c_in, 48)
                pool.wait_ge(pads, 2)
                pool.wait_ge(zeroed, 16)
                for s in range(2):
                    for n in range(NT):
                        pool.indirect_dma_start(g.row_token, bass.IndirectOffsetOnAxis(ap=g.dest[:, s, n:n + 1], axis=0),
                                                tok[:, n:n + 1], None).then_inc(scattered, 16)
                pool.wait_ge(scattered, 16 * 2 * NT)


def experts(nc, g, a):
    with ExitStack() as ctx:
        names = ("g_in0 g_in1 u_in0 u_in1 d_in0 d_in1 gu_used d_used idx got got1 x_turned x_mul x_mod x_used act_in act_ready a_turned a_copied "
                 "y_done y_out0 y_out1 y_copied gu_free silu idx_seen cleared y_zeroed")
        (g_in0, g_in1, u_in0, u_in1, d_in0, d_in1, gu_used, d_used, idx_ready, got, got1, x_turned, x_mul, x_mod, x_used, act_in, act_ready, a_turned,
         a_copied, y_done, y_out0, y_out1, y_copied, gu_free, silu_done, idx_seen, cleared, y_zeroed) = sems(nc, g, " ".join("e_" + s for s in names.split()))
        g_in, u_in, d_in, y_out, got = (g_in0, g_in1), (u_in0, u_in1), (d_in0, d_in1), (y_out0, y_out1), (got, got1)

        def sb(name, shape, dt=F32):
            return ctx.enter_context(nc.sbuf_tensor("e_" + name, shape, dt))

        wg = sb("wg", [P, 2, KD, FE])
        wu = sb("wu", [P, 2, KD, FE])
        wd = sb("wd", [P, 2, KE, D])
        idx = [sb(f"idx{b}", [P, 1], U32) for b in range(2)]
        xg = [sb(f"xg{b}", [P, D]) for b in range(2)]
        xt = sb("xt", [P, 2, KD, P])
        sg = sb("sg", [P, 2, FE])
        at = sb("at", [P, 2, FE])
        att = sb("att", [P, 2, KE, P])
        yo = sb("yo", [P, 2, D])
        zrow = sb("zrow", [P, D])
        px = ctx.enter_context(nc.psum_tensor("e_px", [P, KD, P], F32))
        pgu = ctx.enter_context(nc.psum_tensor("e_pgu", [P, 2, 2, FE], F32))
        py = ctx.enter_context(nc.psum_tensor("e_py", [P, D], F32))
        wg_d = a["w_expert_gate"][0].rearrange("e (k p) n -> e p k n", p=P)
        wu_d = a["w_expert_up"][0].rearrange("e (k p) n -> e p k n", p=P)
        wd_d = a["w_expert_down"][0].rearrange("e (k p) n -> e p k n", p=P)
        y_rows = g.y_dram.rearrange("(n p) d -> n p d", p=P)

        def pairs(eng):
            return eng.value_load(g.blocks[0:1, MAX_BLOCKS:MAX_BLOCKS + 1], min_val=1, max_val=MAX_BLOCKS // 2)

        with nc.Block() as block:

            @block.sync
            def _(sp):
                n = pairs(sp)
                with sp.Fori(0, n) as i:
                    for b in range(2):
                        ex = sp.value_load(g.blocks[0:1, ds(2 * i + b, 1)], min_val=0, max_val=EXPERTS - 1)
                        sp.wait_ge(gu_used, 2 * i + b + 1)
                        sp.dma_start(wg[:, b, :, :], wg_d[ds(ex, 1)].squeeze(0)).then_inc(g_in[b], 16)
                        sp.dma_start(wu[:, b, :, :], wu_d[ds(ex, 1)].squeeze(0)).then_inc(u_in[b], 16)
                        sp.wait_ge(d_used, 2 * i + b + 1)
                        sp.dma_start(wd[:, b, :, :], wd_d[ds(ex, 1)].squeeze(0)).then_inc(d_in[b], 16)

            @block.gpsimd
            def _(pool):
                n = pairs(pool)
                pool.sem_inc(x_used, 2)
                with pool.Fori(0, n) as i:
                    for b in range(2):
                        pool.wait_ge(x_used, 2 * i + b + 1)
                        pool.tensor_copy(idx[b][:], g.rows[:, ds(2 * i + b, 1)]).then_inc(idx_ready, 1)
                        pool.wait_ge(idx_ready, 2 * i + b + 1)
                        pool.sem_inc(idx_seen, 1)
                        pool.indirect_dma_start(xg[b][:], None, g.xn_dram, bass.IndirectOffsetOnAxis(ap=idx[b][:], axis=0)).then_inc(got[b], 16)

            @block.tensor
            def _(pe):
                n = pairs(pe)
                pe.sem_inc(gu_used, 2)
                pe.sem_inc(d_used, 2)
                with pe.Fori(0, n) as i:
                    for b in range(2):
                        pe.wait_ge(got[b], 16 * i + 16)
                        if b == 0:
                            pe.wait_ge(a_copied, 2 * i + 1)
                        else:
                            pe.wait_ge(x_mul, 2 * i + 1)
                        for k in range(KD):
                            o = pe.transpose(px[:, k, :], xg[b][:, k * P:(k + 1) * P], g.ident[:])
                        o.then_inc(x_turned, 1)
                        pe.wait_ge(x_turned, 2 * i + b + 1)
                        pe.sem_inc(x_used, 1)
                    for b in range(2):
                        pe.wait_ge(x_mod, 2 * i + b + 1)
                        pe.wait_ge(gu_free, 2 * i + 1)
                        pe.wait_ge(g_in[b], 16 * i + 16)
                        for k in range(KD):
                            pe.matmul(pgu[:, b, 0, :], xt[:, b, k, :], wg[:, b, k, :], start=(k == 0), stop=(k == KD - 1))
                        pe.wait_ge(u_in[b], 16 * i + 16)
                        for k in range(KD):
                            o = pe.matmul(pgu[:, b, 1, :], xt[:, b, k, :], wu[:, b, k, :], start=(k == 0), stop=(k == KD - 1))
                        o.then_inc(act_in, 1)
                        pe.wait_ge(act_in, 2 * i + b + 1)
                        pe.sem_inc(gu_used, 1)
                    for b in range(2):
                        pe.wait_ge(act_ready, 2 * i + b + 1)
                        if b == 1:
                            pe.wait_ge(a_copied, 2 * i + 2)
                        for k in range(KE):
                            o = pe.transpose(px[:, k, :], at[:, b, k * P:(k + 1) * P], g.ident[:])
                        o.then_inc(a_turned, 1)
                        pe.wait_ge(a_copied, 2 * i + b + 2)
                        pe.wait_ge(d_in[b], 16 * i + 16)
                        pe.wait_ge(y_copied, 2 * i + b + 1)
                        for h in range(2):
                            for k in range(KE):
                                o = pe.matmul(py[:, h * HALF:(h + 1) * HALF], att[:, b, k, :], wd[:, b, k, h * HALF:(h + 1) * HALF],
                                              start=(k == 0), stop=(k == KE - 1))
                        o.then_inc(y_done, 1)
                        pe.wait_ge(y_done, 2 * i + b + 1)
                        pe.sem_inc(d_used, 1)

            @block.vector
            def _(dve):
                dve.memset(zrow[:], 0.0).then_inc(cleared, 1)
                dve.sem_inc(gu_free, 1)
                dve.sem_inc(y_copied, 1)
                n = pairs(dve)
                with dve.Fori(0, n) as i:
                    for b in range(2):
                        dve.wait_ge(x_turned, 2 * i + b + 1)
                        dve.tensor_tensor(xt[:, b], px[:], g.a_col[:].unsqueeze(2).broadcast_to([P, KD, P]), ALU.mult).then_inc(x_mul, 1)
                        dve.wait_ge(x_mul, 2 * i + b + 1)
                        dve.tensor_tensor(xt[:, b], xt[:, b], g.b_col[:].unsqueeze(2).broadcast_to([P, KD, P]), ALU.add).then_inc(x_mod, 1)
                    for b in range(2):
                        dve.wait_ge(silu_done, 2 * i + b + 1)
                        dve.tensor_tensor(at[:, b, :], sg[:, b, :], pgu[:, b, 1, :], ALU.mult).then_inc(act_ready, 1)
                        dve.wait_ge(act_ready, 2 * i + b + 1)
                        dve.sem_inc(gu_free, 1)
                    for b in range(2):
                        dve.wait_ge(y_done, 2 * i + b + 1)
                        dve.wait_ge(y_out[b], 16 * i + 16)
                        dve.tensor_copy(yo[:, b, :], py[:]).then_inc(y_copied, 1)

            @block.scalar
            def _(act):
                n = pairs(act)
                act.sem_inc(a_copied, 1)
                act.sem_inc(y_out0, 16)
                act.sem_inc(y_out1, 16)
                act.wait_ge(cleared, 1)
                with act.Fori(n, Y_BLOCKS // 2) as i:
                    for b in range(2):
                        act.dma_start(y_rows[ds(2 * i + b, 1)].squeeze(0), zrow[:]).then_inc(y_zeroed, 16)
                with act.Fori(0, n) as i:
                    act.sem_inc(y_zeroed, 32)
                    for b in range(2):
                        act.wait_ge(act_in, 2 * i + b + 1)
                        act.activation(sg[:, b, :], pgu[:, b, 0, :], ACT.Silu).then_inc(silu_done, 1)
                    for b in range(2):
                        act.wait_ge(a_turned, 2 * i + b + 1)
                        act.activation(att[:, b], px[:, 0:KE, :], ACT.Copy).then_inc(a_copied, 1)
                        act.wait_ge(y_copied, 2 * i + b + 2)
                        act.dma_start(y_rows[ds(2 * i + b, 1)].squeeze(0), yo[:, b, :]).then_inc(y_out[b], 16)
                act.wait_ge(y_out0, 16 * n + 16)
                act.sem_inc(silu_done, 1)
                act.wait_ge(y_out1, 16 * n + 16)
                act.sem_inc(silu_done, 1)
                act.wait_ge(y_zeroed, 16 * Y_BLOCKS)
                act.sem_inc(silu_done, 1)


def combine(nc, g, a):
    with ExitStack() as ctx:
        fg_in, rows_in0, rows_in1, rows_in2, rows_in3, w1, mixed, scaled, added, squared, rooted, inv, normed, used = sems(nc, g, "c_fg_in c_rows_in0 c_rows_in1 c_rows_in2 c_rows_in3 c_w1 c_mixed c_scaled c_added c_squared c_rooted c_inv c_normed c_used")
        rows_in = (rows_in0, rows_in1, rows_in2, rows_in3)
        y = ctx.enter_context(nc.sbuf_tensor("c_y", [P, 4, 2, D], F32))
        fg = ctx.enter_context(nc.sbuf_tensor("c_fg", [P, D], F32))
        junk = ctx.enter_context(nc.sbuf_tensor("c_junk", [P, D], F32))
        ss = ctx.enter_context(nc.sbuf_tensor("c_ss", [P, 3, NT], F32))
        with nc.Block() as block:

            @block.sync
            def _(sp):
                sp.dma_start(fg[:], a["final_norm_g"].partition_broadcast(P)).then_inc(fg_in, 16)

            @block.gpsimd
            def _(pool):
                for n in range(NT):
                    if n >= 4:
                        pool.wait_ge(added, n - 3)
                    for s in range(2):
                        pool.indirect_dma_start(y[:, n % 4, s, :], None, g.y_dram,
                                                bass.IndirectOffsetOnAxis(ap=g.dest[:, s, n:n + 1], axis=0)).then_inc(rows_in[n % 4], 16)

            @block.vector
            def _(dve):
                for n in range(NT):
                    dve.wait_ge(rows_in[n % 4], 32 * (n // 4 + 1))
                    dve.tensor_scalar(y[:, n % 4, 0, :], y[:, n % 4, 0, :], g.wt[:, 0, n:n + 1], None, ALU.mult).then_inc(w1, 1)
                    dve.wait_ge(w1, n + 1)
                    dve.scalar_tensor_tensor(out=y[:, n % 4, 0, :], in0=y[:, n % 4, 1, :], scalar=g.wt[:, 1, n:n + 1],
                                             in1=y[:, n % 4, 0, :], op0=ALU.mult, op1=ALU.add).then_inc(mixed, 1)
                    dve.wait_ge(mixed, n + 1)
                    dve.tensor_tensor(y[:, n % 4, 0, :], y[:, n % 4, 0, :], g.gate[:, 1, :], ALU.mult).then_inc(scaled, 1)
                    dve.wait_ge(scaled, n + 1)
                    dve.tensor_tensor(g.x[:, n, :], g.x[:, n, :], y[:, n % 4, 0, :], ALU.add).then_inc(added, 1)
                dve.wait_ge(fg_in, 16)
                for n in range(NT):
                    dve.wait_ge(rooted, n + 1)
                    dve.reciprocal(ss[:, 2, n:n + 1], ss[:, 1, n:n + 1]).then_inc(inv, 1)
                    dve.wait_ge(inv, n + 1)
                    dve.scalar_tensor_tensor(out=g.x[:, n, :], in0=g.x[:, n, :], scalar=ss[:, 2, n:n + 1], in1=fg[:],
                                             op0=ALU.mult, op1=ALU.mult).then_inc(normed, 1)

            @block.scalar
            def _(act):
                for n in range(NT):
                    act.wait_ge(added, n + 1)
                    if n:
                        act.wait_ge(squared, n)
                    act.activation(junk[:], g.x[:, n, :], ACT.Square, accum_out=ss[:, 0, n:n + 1]).then_inc(squared, 1)
                    act.wait_ge(squared, n + 1)
                    act.activation(ss[:, 1, n:n + 1], ss[:, 0, n:n + 1], ACT.Sqrt, bias=g.eps[:], scale=1.0 / D).then_inc(rooted, 1)


def short_conv(nc, g, a):
    with ExitStack() as ctx:
        w_in0, w_in1, w_used, ps_done, c_out, u_done, t1, t2, t3, freed, halo = sems(nc, g, "s_w_in0 s_w_in1 s_w_used s_ps_done s_c_out s_u_done s_t1 s_t2 s_t3 s_freed s_halo")
        w_in = (w_in0, w_in1)
        w = ctx.enter_context(nc.sbuf_tensor("s_w", [P, 2, KD, 3, P], F32))
        cc = ctx.enter_context(nc.sbuf_tensor("s_cc", [P, 2, HALF], F32))
        u = ctx.enter_context(nc.sbuf_tensor("s_u", [P, 2, T + 2], F32))
        t = ctx.enter_context(nc.sbuf_tensor("s_t", [P, 2, 3, HALF], F32))
        ps = [ctx.enter_context(nc.psum_tensor(f"s_ps{i}", [P, 3, HALF], F32)) for i in range(2)]
        w_v = a["conv_w_in_2"][0].rearrange("(k p) (s n) -> p k s n", p=P, s=3)
        cw = g.col["conv_w"]
        with nc.Block() as block:

            @block.sync
            def _(sp):
                with sp.Fori(0, KD // 2) as i:
                    for b in range(2):
                        sp.wait_ge(w_used, 2 * i + b + 1)
                        for s in range(3):
                            sp.dma_start(w[:, b, :, s, :], w_v[:, :, s, ds((2 * i + b) * P, P)]).then_inc(w_in[b], 16)

            @block.tensor
            def _(pe):
                pe.sem_inc(w_used, 2)
                pe.sem_inc(freed, 2)
                with pe.Fori(0, KD // 2) as i:
                    for b in range(2):
                        pe.wait_ge(w_in[b], 48 * i + 48)
                        for h in range(2):
                            pe.wait_ge(freed, 4 * i + 2 * b + h + 1)
                            for s in (1, 2, 0):
                                for k in range(KD):
                                    o = pe.matmul(ps[h][:, s, :], w[:, b, k, s, :], g.ht[:, k, h * HALF:(h + 1) * HALF],
                                                  start=(k == 0), stop=(k == KD - 1))
                            o.then_inc(ps_done, 1)
                        pe.wait_ge(ps_done, 4 * i + 2 * b + 2)
                        pe.sem_inc(w_used, 1)

            @block.scalar
            def _(act):
                with act.Fori(0, KD // 2) as i:
                    for b in range(2):
                        for h in range(2):
                            act.wait_ge(ps_done, 4 * i + 2 * b + h + 1)
                            act.wait_ge(u_done, 4 * i + 2 * b + h + 1)
                            act.activation(cc[:, h, :], ps[h][:, 1, :], ACT.Copy).then_inc(c_out, 1)

            @block.vector
            def _(dve):
                dve.memset(u[:, :, 0:2], 0.0).then_inc(halo, 1)
                dve.wait_ge(halo, 1)
                dve.sem_inc(u_done, 1)
                with dve.Fori(0, KD // 2) as i:
                    for b in range(2):
                        for h in range(2):
                            j = 4 * i + 2 * b + h
                            f = 2 * i + b
                            lo = h * HALF
                            dve.wait_ge(c_out, j + 1)
                            dve.tensor_tensor(u[:, b, 2 + lo:2 + lo + HALF], cc[:, h, :], ps[h][:, 2, :], ALU.mult).then_inc(u_done, 1)
                            dve.wait_ge(u_done, j + 2)
                            dve.tensor_scalar(t[:, h, 0, :], u[:, b, lo:lo + HALF], cw[:, ds(f, 1)], None, ALU.mult).then_inc(t1, 1)
                            dve.wait_ge(t1, j + 1)
                            dve.scalar_tensor_tensor(out=t[:, h, 1, :], in0=u[:, b, lo + 1:lo + 1 + HALF], scalar=cw[:, ds(KD + f, 1)],
                                                     in1=t[:, h, 0, :], op0=ALU.mult, op1=ALU.add).then_inc(t2, 1)
                            dve.wait_ge(t2, j + 1)
                            dve.scalar_tensor_tensor(out=t[:, h, 2, :], in0=u[:, b, lo + 2:lo + 2 + HALF], scalar=cw[:, ds(2 * KD + f, 1)],
                                                     in1=t[:, h, 1, :], op0=ALU.mult, op1=ALU.add).then_inc(t3, 1)
                            dve.wait_ge(t3, j + 1)
                            dve.tensor_tensor(g.mix[:, ds(f, 1), lo:lo + HALF], t[:, h, 2:3, :], ps[h][:, 0:1, :], ALU.mult).then_inc(freed, 1)


def feed_forward(nc, g, a, out):
    with ExitStack() as outer:
        act_t = outer.enter_context(nc.sbuf_tensor("f_act", [P, KF, T], F32))
        with ExitStack() as ctx:
            w_in0, w_in1, w_used, ps_done, silu, freed = sems(nc, g, "f_w_in0 f_w_in1 f_w_used f_ps_done f_silu f_freed")
            w_in = (w_in0, w_in1)
            w = ctx.enter_context(nc.sbuf_tensor("f_w", [P, 2, KD, 2, P], F32))
            sg = ctx.enter_context(nc.sbuf_tensor("f_sg", [P, 2, T], F32))
            ps = [ctx.enter_context(nc.psum_tensor(f"f_ps{i}", [P, 2, T], F32)) for i in range(2)]
            w_v = a["ffn_w_gate_up_2"][0].rearrange("(k p) (s n) -> p k s n", p=P, s=2)
            with nc.Block() as block:

                @block.sync
                def _(sp):
                    with sp.Fori(0, KF // 2) as i:
                        for b in range(2):
                            sp.wait_ge(w_used, 2 * i + b + 1)
                            for s in range(2):
                                sp.dma_start(w[:, b, :, s, :], w_v[:, :, s, ds((2 * i + b) * P, P)]).then_inc(w_in[b], 16)

                @block.tensor
                def _(pe):
                    pe.sem_inc(w_used, 2)
                    pe.sem_inc(freed, 2)
                    with pe.Fori(0, KF // 2) as i:
                        for b in range(2):
                            pe.wait_ge(w_in[b], 32 * i + 32)
                            pe.wait_ge(freed, 2 * i + b + 1)
                            for s in range(2):
                                for h in range(2):
                                    for k in range(KD):
                                        o = pe.matmul(ps[b][:, s, h * HALF:(h + 1) * HALF], w[:, b, k, s, :], g.ht[:, k, h * HALF:(h + 1) * HALF],
                                                      start=(k == 0), stop=(k == KD - 1))
                            o.then_inc(ps_done, 1)
                            pe.wait_ge(ps_done, 2 * i + b + 1)
                            pe.sem_inc(w_used, 1)

                @block.scalar
                def _(act):
                    with act.Fori(0, KF // 2) as i:
                        for b in range(2):
                            act.wait_ge(ps_done, 2 * i + b + 1)
                            act.wait_ge(freed, 2 * i + b + 1)
                            act.activation(sg[:, b, :], ps[b][:, 0, :], ACT.Silu).then_inc(silu, 1)

                @block.vector
                def _(dve):
                    with dve.Fori(0, KF // 2) as i:
                        for b in range(2):
                            dve.wait_ge(silu, 2 * i + b + 1)
                            dve.tensor_tensor(act_t[:, ds(2 * i + b, 1), :], sg[:, b:b + 1, :], ps[b][:, 1:2, :], ALU.mult).then_inc(freed, 1)
        with ExitStack() as ctx:
            w_in0, w_in1, w_used, done, banks_free, gain_in, gg, squared, rooted, inv, scaled, added, stored = sems(nc, g, "d_w_in0 d_w_in1 d_w_used d_done d_banks_free d_gain_in d_gg d_squared d_rooted d_inv d_scaled d_added d_stored")
            w_in = (w_in0, w_in1)
            KG = KF // 2
            QW = 256
            w = ctx.enter_context(nc.sbuf_tensor("d_w", [P, 2, KG, QW], F32))
            gr = ctx.enter_context(nc.sbuf_tensor("d_gr", [P, D], F32))
            ss = ctx.enter_context(nc.sbuf_tensor("d_ss", [P, 3, NT], F32))
            junk = ctx.enter_context(nc.sbuf_tensor("d_junk", [P, D], F32))
            ps = [ctx.enter_context(nc.psum_tensor(f"d_ps{i}", [P, HALF], F32)) for i in range(NT)]
            w_v = a["ffn_w_down_2"][0].rearrange("(q k p) n -> q p k n", p=P, q=2)
            rows = g.ht
            with nc.Block() as block:

                @block.sync
                def _(sp):
                    sp.dma_start(gr[:], a["norm_gains_2"][0, 3].partition_broadcast(P)).then_inc(gain_in, 16)
                    with sp.Fori(0, D // QW) as h:
                        for q in range(2):
                            sp.wait_ge(w_used, 2 * h + q + 1)
                            sp.dma_start(w[:, q, :, :], w_v[q][:, :, ds(h * QW, QW)]).then_inc(w_in[q], 16)
                    for n in range(NT):
                        sp.wait_ge(added, n + 1)
                        sp.dma_start(out[0, n * P:(n + 1) * P, :], g.x[:, n, :]).then_inc(stored, 16)
                    sp.wait_ge(stored, 16 * NT)

                @block.tensor
                def _(pe):
                    pe.sem_inc(w_used, 2)
                    with pe.Fori(0, D // QW) as h:
                        for q in range(2):
                            pe.wait_ge(w_in[q], 16 * h + 16)
                            for n in range(NT):
                                if q == 0:
                                    pe.wait_ge(banks_free, 8 * h + 1)
                                for k in range(KG):
                                    o = pe.matmul(ps[n][:, 0:QW], act_t[:, q * KG + k, n * P:(n + 1) * P], w[:, q, k, :],
                                                  start=(q == 0 and k == 0), stop=(q == 1 and k == KG - 1))
                                if q == 1:
                                    o.then_inc(done, 1)
                            if q == 1:
                                pe.wait_ge(done, 8 * h + 8)
                                pe.sem_inc(w_used, 2)

                @block.scalar
                def _(act):
                    act.sem_inc(banks_free, 1)
                    with act.Fori(0, D // QW) as h:
                        for n in range(NT):
                            act.wait_ge(done, 8 * h + n + 1)
                            act.activation(rows[:, n:n + 1, ds(h * QW, QW)], ps[n][:, 0:QW].unsqueeze(1), ACT.Copy).then_inc(banks_free, 1)
                    for n in range(NT):
                        act.wait_ge(banks_free, 8 * (D // QW - 1) + n + 2)
                        if n:
                            act.wait_ge(squared, n)
                        act.activation(junk[:], rows[:, n, :], ACT.Square, accum_out=ss[:, 0, n:n + 1]).then_inc(squared, 1)
                        act.wait_ge(squared, n + 1)
                        act.activation(ss[:, 1, n:n + 1], ss[:, 0, n:n + 1], ACT.Sqrt, bias=g.eps[:], scale=1.0 / D).then_inc(rooted, 1)

                @block.vector
                def _(dve):
                    dve.wait_ge(gain_in, 16)
                    dve.tensor_tensor(gr[:], gr[:], g.gate2[:, 1, :], ALU.mult).then_inc(gg, 1)
                    dve.wait_ge(gg, 1)
                    for n in range(NT):
                        dve.wait_ge(rooted, n + 1)
                        dve.reciprocal(ss[:, 2, n:n + 1], ss[:, 1, n:n + 1]).then_inc(inv, 1)
                        dve.wait_ge(inv, n + 1)
                        dve.scalar_tensor_tensor(out=rows[:, n, :], in0=rows[:, n, :], scalar=ss[:, 2, n:n + 1], in1=gr[:],
                                                 op0=ALU.mult, op1=ALU.mult).then_inc(scaled, 1)
                        dve.wait_ge(scaled, n + 1)
                        dve.tensor_tensor(g.x[:, n, :], g.x[:, n, :], rows[:, n, :], ALU.add).then_inc(added, 1)


def build(nc, a, out, stop=None):
    g = Program()
    with ExitStack() as ctx:
        g.sems = []

        def sb(name, shape, dt=F32):
            return ctx.enter_context(nc.sbuf_tensor(name, shape, dt))

        g.x = sb("x_rows", [P, NT, D])
        g.ident = sb("ident", [P, P])
        g.ones = sb("ones", [P, P])
        g.eps = sb("eps", [P, 1])
        g.vcol = sb("vcol", [P, 2, P])
        g.neg_lam = sb("neg_lam", [P, 1])
        g.mod = sb("mod", [P, 2, 16])
        g.mod2 = sb("mod2", [P, 2, 16])
        g.gate = sb("gate", [P, 2, D])
        g.gate2 = sb("gate2", [P, 2, D])
        g.a_col = sb("a_col", [P, KD])
        g.b_col = sb("b_col", [P, KD])
        g.wt = sb("wt", [P, 2, NT])
        g.dest = sb("dest", [P, 2, NT], U32)
        g.blocks = sb("blocks", [1, MAX_BLOCKS + 1], U32)
        g.rows = sb("rows", [P, MAX_BLOCKS], U32)
        g.row_token = nc.dram_tensor("row_token", [MAX_BLOCKS * P, 1], F32, kind="Internal").ap()
        g.xn_dram = nc.dram_tensor("xn_rows", [T, D], F32, kind="Internal").ap()
        g.y_dram = nc.dram_tensor("y_rows", [Y_BLOCKS * P, D], F32, kind="Internal").ap()
        with ExitStack() as early:
            g.cs = early.enter_context(nc.sbuf_tensor("cos_sin", [P, 2, T], F32))
            load_constants(nc, g, a)
            modulation(nc, g, "m1_", a["c"], a["w_ada"], a["b_ada"], g.col["b_ada"], g.mod, g.gate)
            modulation(nc, g, "m2_", a["c_2"], a["ada_w_2"], a["ada_b_2"], g.col["b_ada2"], g.mod2, g.gate2)
            g.mix = early.enter_context(nc.sbuf_tensor("mix", [P, 2 * HEADS, T], F32))
            g.ht = early.enter_context(nc.sbuf_tensor("ht", [P, KD, T], F32))
            norm_transposed(nc, g, "n1_", g.col["norm1_g"], g.mod[:, 0, :], g.ht)
            with ExitStack() as mla:
                g.lat = mla.enter_context(nc.sbuf_tensor("lat", [P, 4, T], F32))
                g.kpe = mla.enter_context(nc.sbuf_tensor("kpe", [ROPE, T], F32))
                latents(nc, g, a)
                attention(nc, g, a, "am_", False)
            attention(nc, g, a, "ad_", True)
            head_norm(nc, g)
            project_rows(nc, g, "po_", g.mix, a["w_out"][0], g.gate[:, 0, :])
            norm_transposed(nc, g, "n2_", g.col["norm2_g"], g.mod[:, 1, :], g.ht, keep=g.xn_dram)
            route(nc, g, a)
        clear_sems(nc, g)
        experts(nc, g, a)
        combine(nc, g, a)
        with ExitStack() as late:
            g.ht = late.enter_context(nc.sbuf_tensor("ht2", [P, KD, T], F32))
            norm_transposed(nc, g, "n3_", g.col["g0"], g.mod2[:, 0, :], g.ht)
            with ExitStack() as conv:
                g.mix = conv.enter_context(nc.sbuf_tensor("mix2", [P, KD, T], F32))
                short_conv(nc, g, a)
                project_rows(nc, g, "pc_", g.mix, a["conv_w_out_2"][0], g.gate2[:, 0, :], gain=a["norm_gains_2"][0, 1])
            norm_transposed(nc, g, "n4_", g.col["g2"], g.mod2[:, 1, :], g.ht)
            feed_forward(nc, g, a, out)


def constants():
    half = ROPE // 2
    inv = np.float32(10000.0) ** (-np.arange(0, ROPE, 2, dtype=np.float32) / np.float32(ROPE))
    ang = inv.astype(np.float32)[:, None] * np.arange(T, dtype=np.float32)[None, :]
    cos, sin = np.cos(ang).astype(np.float32), np.sin(ang).astype(np.float32)
    rope = np.zeros((2, P, T), np.float32)
    for q in range(P // half):
        rope[0, q * half:(q + 1) * half] = cos
        rope[1, q * half:(q + 1) * half] = sin if q % 2 else -sin
    return {
        "const_rope": rope,
        "const_ident": np.eye(P, dtype=np.float32),
        "const_before": np.triu(np.ones((P, P), np.float32), 1),
        "const_iota": np.arange(MAX_BLOCKS, dtype=np.float32)[None, :],
        "const_token": np.arange(T, dtype=np.float32).reshape(NT, P).T.copy(),
    }


_INS = ["x", "c", "w_ada", "b_ada", "norm1_g", "w_in", "q_a_norm_g", "w_q_up", "kv_a_norm_g", "w_kv_up", "lambda_q1",
        "lambda_k1", "lambda_q2", "lambda_k2", "subln_g", "w_out", "norm2_g", "w_router_group", "b_router_group",
        "w_router_expert", "b_router_expert", "w_expert_gate", "w_expert_up", "w_expert_down", "final_norm_g",
        "c_2", "ada_w_2", "ada_b_2", "norm_gains_2", "conv_w_in_2", "conv_w_2", "conv_w_out_2",
        "ffn_w_gate_up_2", "ffn_w_down_2"]


def kernel(**inputs):
    import numpy as _np
    import concourse.bacc as _bacc
    from concourse import mybir as _mybir
    from concourse.bass_utils import run_bass_kernel_spmd as _run

    nc = _bacc.Bacc("TRN2", target_bir_lowering=False, num_devices=1)
    arrays, aps = {}, {}
    given = {name: _np.ascontiguousarray(inputs[name]) for name in _INS}
    given.update(constants())
    for name, value in given.items():
        arrays[f"in_{name}_dram"] = value
        aps[name] = nc.dram_tensor(f"in_{name}_dram", value.shape, _mybir.dt.from_np(value.dtype), kind="ExternalInput").ap()
    out = nc.dram_tensor("out_0_dram", (1, T, D), _mybir.dt.float32, kind="ExternalOutput").ap()
    build(nc, aps, out)
    r = _run(nc, [arrays], core_ids=[0])
    return r.results[0]["out_0_dram"]
```

```python
from contextlib import ExitStack

import numpy as np

import concourse.bass as bass
from concourse import mybir

ALU = mybir.AluOpType
ACT = mybir.ActivationFunctionType
F32 = mybir.dt.float32
F32R = mybir.dt.float32r
U32 = mybir.dt.uint32
AX_X = mybir.AxisListType.X
ds = bass.ds

P = 128
T = 1024
D = 1024
NT = T // P
KD = D // P
HALF = 512
EPS = 1e-6
QR, KVR, NOPE, ROPE, VD = 256, 256, 128, 64, 128
HEADS = 4
DQK = 64
QH = NOPE + ROPE
KVH = NOPE + VD
DQ0 = QR + KVR + ROPE
DK0 = DQ0 + HEADS * 2 * DQK
DV0 = DK0 + HEADS * 2 * DQK
GROUPS, PER_GROUP = 4, 8
EXPERTS = GROUPS * PER_GROUP
FE = 512
KE = FE // P
Y_BLOCKS = 50
MAX_BLOCKS = 48
FF = 2816
KF = FF // P
LAMBDA_INIT = 0.2
BIG = 3.0e38


class Program:
    pass


def sems(nc, g, names):
    made = [nc.alloc_semaphore(n) for n in names.split()]
    g.sems += made
    return made


def clear_sems(nc, g):
    nc.clear_and_free_semaphores(g.sems)
    nc.all_engine_barrier()
    g.sems = []


def load_constants(nc, g, a):
    rows = [[("norm1_g", a["norm1_g"], 8), ("norm2_g", a["norm2_g"], 8), ("q_g", a["q_a_norm_g"], 2),
             ("kv_g", a["kv_a_norm_g"], 2), ("sub_g", a["subln_g"], 1),
             ("g0", a["norm_gains_2"][0, 0:1, :], 8), ("g2", a["norm_gains_2"][0, 2:3, :], 8),
             ("b_ada", a["b_ada"], 48)],
            [("b_ada2", a["ada_b_2"], 48), ("conv_w", a["conv_w_2"][0, :, :], 24)]]
    with ExitStack() as ctx:
        const_in, rows_in, lam_in, rows_clear, turned, vec_ready, prod, lam_sum, lam_exp, ones_ready = sems(nc, g, "const_in rows_in lam_in rows_clear turned vec_ready prod lam_sum lam_exp ones_ready")
        vrow = ctx.enter_context(nc.sbuf_tensor("vrow", [P, 2, P], F32))
        lamv = ctx.enter_context(nc.sbuf_tensor("lamv", [P, 4, DQK], F32))
        lamp = ctx.enter_context(nc.sbuf_tensor("lamp", [P, 2, DQK], F32))
        lams = ctx.enter_context(nc.sbuf_tensor("lams", [P, 2], F32))
        lame = ctx.enter_context(nc.sbuf_tensor("lame", [P, 2], F32))
        pv = ctx.enter_context(nc.psum_tensor("pv", [P, 2, P], F32))
        g.col = {}
        n_rows = 0
        with nc.Block() as block:

            @block.sync
            def _(sp):
                nonlocal n_rows
                sp.dma_start(g.ident[:], a["const_ident"]).then_inc(const_in, 16)
                sp.dma_start(g.cs[:], a["const_rope"].rearrange("s p t -> p s t")).then_inc(const_in, 16)
                sp.wait_ge(rows_clear, 1)
                for j, group in enumerate(rows):
                    at = 0
                    for name, src, n in group:
                        pat = "a (r q) -> (a r) q"
                        sp.dma_start(vrow[at:at + n, j, :], src.rearrange(pat, q=P)).then_inc(rows_in, 16)
                        g.col[name] = g.vcol[:, j, at:at + n]
                        at += n
                        n_rows += 1

            @block.scalar
            def _(act):
                for i, name in enumerate(("lambda_q1", "lambda_k1", "lambda_q2", "lambda_k2")):
                    act.dma_start(lamv[:, i, :], a[name][0].partition_broadcast(P)).then_inc(lam_in, 16)
                act.wait_ge(lam_sum, 2)
                act.activation(lame[:], lams[:], ACT.Exp).then_inc(lam_exp, 1)

            @block.tensor
            def _(pe):
                pe.wait_ge(const_in, 32)
                pe.wait_ge(rows_in, 16 * sum(len(r) for r in rows))
                for j in range(2):
                    pe.transpose(pv[:, j, :], vrow[:, j, :], g.ident[:]).then_inc(turned, 1)

            @block.vector
            def _(dve):
                dve.memset(vrow[:], 0.0).then_inc(rows_clear, 1)
                dve.memset(g.ones[:], 1.0).then_inc(ones_ready, 1)
                dve.memset(g.eps[:], EPS).then_inc(ones_ready, 1)
                dve.wait_ge(lam_in, 64)
                for i in range(2):
                    dve.tensor_tensor(lamp[:, i, :], lamv[:, 2 * i, :], lamv[:, 2 * i + 1, :], ALU.mult).then_inc(prod, 1)
                dve.wait_ge(prod, 2)
                for i in range(2):
                    dve.tensor_reduce(lams[:, i:i + 1], lamp[:, i, :], AX_X, ALU.add).then_inc(lam_sum, 1)
                dve.wait_ge(lam_exp, 1)
                dve.scalar_tensor_tensor(out=g.neg_lam[:], in0=lame[:, 1:2], scalar=-LAMBDA_INIT,
                                         in1=lame[:, 0:1], op0=ALU.add, op1=ALU.subtract).then_inc(lam_sum, 1)
                dve.wait_ge(turned, 2)
                dve.tensor_copy(g.vcol[:], pv[:]).then_inc(vec_ready, 1)


def modulation(nc, g, tag, c, w, bias, bias_col, mod_col, gate_row):
    with ExitStack() as ctx:
        c_in, bias_in, c_ready, sec_in0, sec_in1, sec_in2, sec_free, part, summed, acc_free, col_ps, row_ps, col_free, row_free = sems(nc, g, " ".join(tag + s for s in "c_in bias_in c_ready sec_in0 sec_in1 sec_in2 sec_free part summed acc_free col_ps row_ps col_free row_free".split()))
        sec_in = (sec_in0, sec_in1, sec_in2)
        ct = ctx.enter_context(nc.sbuf_tensor(tag + "ct", [P, KD], F32))
        cs = ctx.enter_context(nc.sbuf_tensor(tag + "cs", [P, KD], F32))
        sec = ctx.enter_context(nc.sbuf_tensor(tag + "sec", [P, 3, KD, D], F32))
        acc = ctx.enter_context(nc.sbuf_tensor(tag + "acc", [P, 3, D], F32))
        pcol = ctx.enter_context(nc.psum_tensor(tag + "pcol", [P, 16], F32))
        prow = ctx.enter_context(nc.psum_tensor(tag + "prow", [P, D], F32))
        w_v = w[0].rearrange("(p k) n -> p k n", k=KD)
        with nc.Block() as block:

            @block.sync
            def _(sp):
                sp.dma_start(ct[:], c[0].rearrange("(p k) -> p k", k=KD)).then_inc(c_in, 16)
                for i in range(2):
                    sp.dma_start(gate_row[:, i, :], bias[0, (3 * i + 2) * D:(3 * i + 3) * D].partition_broadcast(P)).then_inc(bias_in, 16)
                with sp.Fori(0, 2) as i:
                    for s in range(3):
                        sp.wait_ge(sec_free, 3 * i + s + 1)
                        sp.dma_start(sec[:, s, :, :], w_v[:, :, ds((3 * i + s) * D, D)]).then_inc(sec_in[s], 16)

            @block.scalar
            def _(act):
                act.wait_ge(c_in, 16)
                act.activation(cs[:], ct[:], ACT.Silu).then_inc(c_ready, 1)

            @block.vector
            def _(dve):
                dve.sem_inc(sec_free, 3)
                dve.sem_inc(col_free, 1)
                dve.sem_inc(row_free, 1)
                dve.wait_ge(c_ready, 1)
                dve.wait_ge(bias_in, 32)
                with dve.Fori(0, 2) as i:
                    for s in range(3):
                        dve.wait_ge(sec_in[s], 16 * i + 16)
                        if s == 0:
                            dve.wait_ge(acc_free, i + 1)
                        for k in range(KD):
                            if k == 0:
                                o = dve.tensor_scalar(acc[:, s, :], sec[:, s, k, :], cs[:, 0:1], None, ALU.mult)
                            else:
                                dve.wait_ge(part, 21 * i + 7 * s + k)
                                o = dve.scalar_tensor_tensor(out=acc[:, s, :], in0=sec[:, s, k, :], scalar=cs[:, k:k + 1],
                                                             in1=acc[:, s, :], op0=ALU.mult, op1=ALU.add)
                            if k < KD - 1:
                                o.then_inc(part, 1)
                        o.then_inc(summed, 1)
                        dve.wait_ge(summed, 3 * i + s + 1)
                        dve.sem_inc(sec_free, 1)
                    dve.wait_ge(col_ps, i + 1)
                    dve.tensor_tensor(mod_col[:, ds(i, 1), :], pcol[:].unsqueeze(1),
                                      bias_col[:, ds(24 * i, 16)].unsqueeze(1), ALU.add).then_inc(col_free, 1)
                    dve.wait_ge(row_ps, i + 1)
                    dve.tensor_tensor(gate_row[:, ds(i, 1), :], prow[:].unsqueeze(1), gate_row[:, ds(i, 1), :], ALU.add).then_inc(row_free, 1)

            @block.tensor
            def _(pe):
                pe.sem_inc(acc_free, 1)
                with pe.Fori(0, 2) as i:
                    pe.wait_ge(summed, 3 * i + 2)
                    pe.wait_ge(col_free, i + 1)
                    for j in range(16):
                        o = pe.matmul(pcol[:, j:j + 1], acc[:, j // KD, (j % KD) * P:(j % KD + 1) * P], g.ones[:, 0:1],
                                      start=True, stop=True)
                    o.then_inc(col_ps, 1)
                    pe.wait_ge(summed, 3 * i + 3)
                    pe.wait_ge(row_free, i + 1)
                    for h in range(2):
                        o = pe.matmul(prow[:, h * HALF:(h + 1) * HALF], g.ones[:], acc[:, 2, h * HALF:(h + 1) * HALF], start=True, stop=True)
                    o.then_inc(row_ps, 1)
                    pe.wait_ge(row_ps, i + 1)
                    pe.sem_inc(acc_free, 1)


def three_passes(pe, out, stat, mov, start, stop):
    for n, (i, j) in enumerate(((0, 0), (1, 0), (0, 1))):
        o = pe.matmul(out, stat[i], mov[j], start=start and n == 0, stop=stop and n == 2)
    return o


def norm_transposed(nc, g, tag, gain, mod, out_t=None, split=None, keep=None, load=None):
    with ExitStack() as ctx:
        x_in, sq, root, rstd_ready, ab, staged, turned, turned_free, row_ready, row_out0, row_out1, high, low = sems(
            nc, g, " ".join(tag + s for s in "x_in sq root rstd_ready ab staged turned turned_free row_ready row_out0 row_out1 high low".split()))
        row_out = (row_out0, row_out1)
        junk = ctx.enter_context(nc.sbuf_tensor(tag + "junk", [P, D], F32))
        ss = ctx.enter_context(nc.sbuf_tensor(tag + "ss", [P, NT], F32))
        rs = ctx.enter_context(nc.sbuf_tensor(tag + "rs", [P, NT], F32))
        rstd = ctx.enter_context(nc.sbuf_tensor(tag + "rstd", [P, NT], F32))
        stage = ctx.enter_context(nc.sbuf_tensor(tag + "stage", [P, 2, NT, P], F32))
        rows = ctx.enter_context(nc.sbuf_tensor(tag + "rows", [P, 2, D], F32)) if keep is not None else None
        full = ctx.enter_context(nc.sbuf_tensor(tag + "full", [P, 2, T], F32)) if split is not None else None
        pt = ctx.enter_context(nc.psum_tensor(tag + "pt", [P, 2, T], F32))
        with nc.Block() as block:

            @block.scalar
            def _(act):
                if load is not None:
                    act.wait_ge(x_in, 16)
                for n in range(NT):
                    if n:
                        act.wait_ge(sq, n)
                    act.activation(junk[:], g.x[:, n, :], ACT.Square, accum_out=ss[:, n:n + 1]).then_inc(sq, 1)
                act.wait_ge(sq, NT)
                act.activation(rs[:], ss[:], ACT.Sqrt, bias=g.eps[:], scale=1.0 / D).then_inc(root, 1)
                act.wait_ge(ab, 1)
                act.sem_inc(turned_free, 2)
                with act.Fori(0, KD // 2) as i:
                    for b in range(2):
                        act.wait_ge(turned, 2 * i + b + 3)
                        if split is not None:
                            act.wait_ge(low, 2 * i + b + 1)
                        to = full[:, b:b + 1, :] if split is not None else out_t[:, ds(2 * i + b, 1), :]
                        act.activation(to, pt[:, b:b + 1, :], ACT.Identity,
                                       bias=g.b_col[:, ds(2 * i + b, 1)], scale=g.a_col[:, ds(2 * i + b, 1)]).then_inc(turned_free, 1)

            @block.vector
            def _(dve):
                dve.scalar_tensor_tensor(out=g.a_col[:], in0=mod[:, 8:16], scalar=1.0, in1=gain, op0=ALU.add, op1=ALU.mult)
                dve.tensor_copy(g.b_col[:], mod[:, 0:8]).then_inc(ab, 1)
                dve.wait_ge(root, 1)
                dve.reciprocal(rstd[:], rs[:]).then_inc(rstd_ready, 1)
                dve.wait_ge(rstd_ready, 1)
                dve.sem_inc(low, 2)

                def scale_chunk(k, b):
                    dve.wait_ge(turned, k + 1)
                    dve.tensor_tensor(stage[:, b, :, :], g.x[:, :, ds(k * P, P)],
                                      rstd[:].unsqueeze(2).broadcast_to([P, NT, P]), ALU.mult).then_inc(staged, 1)

                def split_chunk(k, b):
                    dve.wait_ge(turned_free, k + 3)
                    dve.tensor_copy(split[0][:, ds(k, 1), :], full[:, b:b + 1, :]).then_inc(high, 1)
                    dve.wait_ge(high, k + 1)
                    dve.tensor_tensor(split[1][:, ds(k, 1), :], full[:, b:b + 1, :], split[0][:, ds(k, 1), :].bitcast(F32),
                                      ALU.subtract).then_inc(low, 1)

                if split is None:
                    with dve.Fori(0, KD // 2) as i:
                        for b in range(2):
                            scale_chunk(2 * i + b, b)
                else:
                    scale_chunk(0, 0)
                    scale_chunk(1, 1)
                    with dve.Fori(1, KD // 2) as i:
                        for b in range(2):
                            scale_chunk(2 * i + b, b)
                            split_chunk(2 * i + b - 2, b)
                    split_chunk(KD - 2, 0)
                    split_chunk(KD - 1, 1)
                if keep is not None:
                    for n in range(NT):
                        if n >= 2:
                            dve.wait_ge(row_out[n % 2], 16 * (n // 2))
                        dve.tensor_scalar(rows[:, n % 2, :], g.x[:, n, :], rstd[:, n:n + 1], None, ALU.mult).then_inc(row_ready, 1)

            @block.tensor
            def _(pe):
                pe.sem_inc(turned, 2)
                with pe.Fori(0, KD // 2) as i:
                    for b in range(2):
                        pe.wait_ge(staged, 2 * i + b + 1)
                        pe.wait_ge(turned_free, 2 * i + b + 1)
                        for n in range(NT):
                            o = pe.transpose(pt[:, b, n * P:(n + 1) * P], stage[:, b, n, :], g.ident[:])
                        o.then_inc(turned, 1)

            if keep is not None or load is not None:
                @block.sync
                def _(sp):
                    if load is not None:
                        sp.dma_start(g.x[:], load.rearrange("(n p) d -> p n d", p=P)).then_inc(x_in, 16)
                    if keep is not None:
                        for n in range(NT):
                            sp.wait_ge(row_ready, n + 1)
                            sp.dma_start(keep[n * P:(n + 1) * P, :], rows[:, n % 2, :]).then_inc(row_out[n % 2], 16)
                        for b in range(2):
                            sp.wait_ge(row_out[b], 8 * NT)


def rope_rotate(dve, out, ps, g, tmp, rows, step, k0):
    dve.tensor_tensor(tmp[0:rows, 0, :], ps[0:rows, :], g.cs[0:rows, 0, :], ALU.mult)
    for q in range(rows // 32):
        o = dve.tensor_tensor(tmp[32 * q:32 * q + 32, 1, :], ps[32 * (q ^ 1):32 * (q ^ 1) + 32, :],
                              g.cs[32 * q:32 * q + 32, 1, :], ALU.mult)
    o.then_inc(step, 1)
    dve.wait_ge(step, k0 + 1)
    return dve.tensor_tensor(out, tmp[0:rows, 0, :], tmp[0:rows, 1, :], ALU.add)


def latents(nc, g, a):
    with ExitStack() as ctx:
        w_in, proj, raw, squared, ssq, rooted, recip_r, lat_done, ps_free, rope_step = sems(nc, g, "l_w_in l_proj l_raw l_squared l_ssq l_rooted l_recip l_done l_ps_free l_rope")
        w = ctx.enter_context(nc.sbuf_tensor("l_w", [P, KD, DQ0], F32))
        raws = ctx.enter_context(nc.sbuf_tensor("l_raw", [P, 4, T], F32))
        sqs = g.dmix
        root = ctx.enter_context(nc.sbuf_tensor("l_root", [P, 2, T], F32))
        rinv = ctx.enter_context(nc.sbuf_tensor("l_rinv", [P, 2, T], F32))
        tmp = ctx.enter_context(nc.sbuf_tensor("l_tmp", [P, 2, T], F32))
        ps = ctx.enter_context(nc.psum_tensor("l_ps", [P, 2, T], F32))
        pss = ctx.enter_context(nc.psum_tensor("l_pss", [P, 2, T], F32))
        with nc.Block() as block:

            @block.sync
            def _(sp):
                sp.dma_start(w[:], a["w_in"][0].rearrange("(k p) n -> p k n", p=P)[:, :, 0:DQ0]).then_inc(w_in, 16)

            @block.tensor
            def _(pe):
                pe.wait_ge(w_in, 16)
                for c in range(5):
                    m = P if c < 4 else ROPE
                    if c >= 2:
                        pe.wait_ge(ps_free, c - 1)
                    for h in range(2):
                        for k in range(KD):
                            o = pe.matmul(ps[0:m, c % 2, h * HALF:(h + 1) * HALF], w[:, k, c * P:c * P + m],
                                          g.ht[:, k, h * HALF:(h + 1) * HALF], start=(k == 0), stop=(k == KD - 1))
                    o.then_inc(proj, 1)
                for j in range(2):
                    pe.wait_ge(squared, 2 * j + 2)
                    for h in range(2):
                        for c in range(2):
                            o = pe.matmul(pss[:, j, h * HALF:(h + 1) * HALF], g.ones[:], sqs[:, 2 * j + c, h * HALF:(h + 1) * HALF],
                                          start=(c == 0), stop=(c == 1))
                    o.then_inc(ssq, 1)

            @block.scalar
            def _(act):
                for c in range(4):
                    act.wait_ge(proj, c + 1)
                    act.activation(raws[:, c, :], ps[:, c % 2, :], ACT.Copy).then_inc(raw, 1)
                    act.wait_ge(raw, c + 1)
                    act.sem_inc(ps_free, 1)
                    act.activation(sqs[:, c, :], raws[:, c, :], ACT.Square).then_inc(squared, 1)
                for j in range(2):
                    act.wait_ge(ssq, j + 1)
                    act.activation(root[:, j, :], pss[:, j, :], ACT.Sqrt, bias=g.eps[:], scale=1.0 / QR).then_inc(rooted, 1)

            @block.vector
            def _(dve):
                dve.wait_ge(proj, 5)
                rope_rotate(dve, g.kpe[:], ps[:, 0, :], g, tmp, ROPE, rope_step, 0).then_inc(lat_done, 1)
                for j, gain in enumerate(("q_g", "kv_g")):
                    dve.wait_ge(rooted, j + 1)
                    dve.reciprocal(rinv[:, j, :], root[:, j, :]).then_inc(recip_r, 1)
                    dve.wait_ge(recip_r, j + 1)
                    for c in range(2):
                        dve.scalar_tensor_tensor(out=g.lat[:, 2 * j + c, :], in0=raws[:, 2 * j + c, :], scalar=g.col[gain][:, c:c + 1],
                                                 in1=rinv[:, j, :], op0=ALU.mult, op1=ALU.mult).then_inc(lat_done, 1)


def attention(nc, g, a, tag, diff):
    maps = 2 if diff else 1
    scale = float(DQK if diff else QH) ** -0.5
    kin = KD if diff else QR // P
    wcols = 3 * P if diff else QH + KVH
    uses = (2 + NT, 1 + NT) if diff else (2 + NT // 2, 2 + NT // 2)
    n_proj = 3 if diff else 4
    with ExitStack() as ctx:
        names = ("w_in w_used proj q_ready qpe_ready k_ready v_ready rope_step free0 free1 scored maxed nmax expd sumr "
                 "probs turned copied pt_free pv mixed t_free combined p_free leading")
        (w_in, w_used, proj, q_ready, qpe_ready, k_ready, v_ready, rope_step, free0, free1, scored, maxed, nmax, expd, sumr,
         probs, turned, copied, pt_free, pv, mixed, t_free, combined, p_free, leading) = sems(nc, g, " ".join(tag + s for s in names.split()))
        free = (free0, free1)

        def sb(name, shape):
            return ctx.enter_context(nc.sbuf_tensor(tag + name, shape, F32))

        w = sb("w", [P, kin, wcols])
        qt = sb("qt", [P, T])
        kt = sb("kt", [P, T])
        qpe = sb("qpe", [ROPE, T]) if not diff else None
        v = sb("v", [P, NT, P])
        e = sb("e", [P, 2, maps, T])
        pr = sb("pr", [P, 2, T]) if diff else None
        tmp = pr if diff else e[:, :, 0, :]
        pt = sb("pt", [P, NT, HALF])
        mx = sb("mx", [P, 2, maps])
        nm = sb("nm", [P, 2, maps])
        sm = sb("sm", [P, 2, maps])
        ri = sb("ri", [P, 2, maps])
        r2 = sb("r2", [P, 2])
        ps = [ctx.enter_context(nc.psum_tensor(tag + f"ps{i}", [P, T], F32)) for i in range(2)]
        ptr = ctx.enter_context(nc.psum_tensor(tag + "ptr", [P, NT, P], F32))
        po = ctx.enter_context(nc.psum_tensor(tag + "po", [P, HALF], F32))

        def slot(i, m):
            return (m, i + 2 - m) if diff else (i % 2, 2 + i // 2)

        if diff:
            win = a["w_in"][0].rearrange("(k p) n -> p k n", p=P)
        else:
            wq = a["w_q_up"][0].rearrange("(k p) n -> p k n", p=P)
            wkv = a["w_kv_up"][0].rearrange("(k p) n -> p k n", p=P)
        n_w = 3 if diff else 2

        with nc.Block() as block:

            @block.sync
            def _(sp):
                with sp.Fori(0, HEADS) as h:
                    sp.wait_ge(w_used, h + 1)
                    if diff:
                        for j, c0 in enumerate((DQ0, DK0, DV0)):
                            sp.dma_start(w[:, :, j * P:(j + 1) * P], win[:, :, ds(c0 + h * P, P)]).then_inc(w_in, 16)
                    else:
                        sp.dma_start(w[:, :, 0:QH], wq[:, :, ds(h * QH, QH)]).then_inc(w_in, 16)
                        sp.dma_start(w[:, :, QH:], wkv[:, :, ds(h * KVH, KVH)]).then_inc(w_in, 16)

            @block.tensor
            def _(pe):
                pe.sem_inc(free0, 1)
                pe.sem_inc(free1, 1)
                pe.sem_inc(w_used, 1)
                pe.sem_inc(pv, 1)
                with pe.Fori(0, HEADS) as h:
                    pe.wait_ge(w_in, 16 * n_w * (h + 1))

                    def project(buf, use, c0, m, src, c_src):
                        pe.wait_ge(free[buf], uses[buf] * h + use + 1)
                        for hf in range(2):
                            for k in range(kin):
                                o = pe.matmul(ps[buf][0:m, hf * HALF:(hf + 1) * HALF], w[:, k, c0:c0 + m],
                                              src[:, c_src + k, hf * HALF:(hf + 1) * HALF], start=(k == 0), stop=(k == kin - 1))
                        o.then_inc(proj, 1)

                    def values(buf, use, c0, src, c_src):
                        pe.wait_ge(free[buf], uses[buf] * h + use + 1)
                        for n in range(NT):
                            for k in range(kin):
                                o = pe.matmul(ps[buf][:, n * P:(n + 1) * P], src[:, c_src + k, n * P:(n + 1) * P],
                                              w[:, k, c0:c0 + P], start=(k == 0), stop=(k == kin - 1))
                        o.then_inc(proj, 1)

                    if diff:
                        project(0, 0, 0, P, g.ht, 0)
                        project(1, 0, P, P, g.ht, 0)
                        values(0, 1, 2 * P, g.ht, 0)
                    else:
                        project(0, 0, NOPE, ROPE, g.lat, 0)
                        project(1, 0, 0, NOPE, g.lat, 0)
                        project(0, 1, QH, NOPE, g.lat, 2)
                        values(1, 1, QH + NOPE, g.lat, 2)
                    pe.wait_ge(proj, n_proj * (h + 1))
                    pe.sem_inc(w_used, 1)
                    pe.wait_ge(q_ready, h + 1)
                    if not diff:
                        pe.wait_ge(qpe_ready, h + 1)
                    pe.wait_ge(k_ready, h + 1)

                    def scores(i):
                        for m in range(maps):
                            buf, use = slot(i, m)
                            pe.wait_ge(free[buf], uses[buf] * h + use + 1)
                            lo = m * DQK
                            hi = lo + DQK if diff else P
                            for hf in range(2):
                                cols = slice(hf * HALF, (hf + 1) * HALF)
                                o = pe.matmul(ps[buf][:, cols], qt[lo:hi, i * P:(i + 1) * P], kt[lo:hi, cols], start=True, stop=diff)
                                if not diff:
                                    o = pe.matmul(ps[buf][:, cols], qpe[:, i * P:(i + 1) * P], g.kpe[:, cols], start=False, stop=True)
                            o.then_inc(scored, 1)

                    def turn(i):
                        pe.wait_ge(probs, NT * h + i + 1)
                        pe.wait_ge(t_free, NT * h + i + 1)
                        src = pr[:, i % 2, :] if diff else e[:, i % 2, 0, :]
                        for n in range(NT):
                            o = pe.transpose(ptr[:, n, :], src[:, n * P:(n + 1) * P], g.ident[:])
                        o.then_inc(turned, 1)

                    def weigh(j):
                        pe.wait_ge(copied, NT * h + 4 * j + 4)
                        pe.wait_ge(v_ready, h + 1)
                        pe.wait_ge(mixed, 2 * h + j + 1)
                        for n in range(NT):
                            o = pe.matmul(po[:], v[:, n, :], pt[:, n, :], start=(n == 0), stop=(n == NT - 1))
                        o.then_inc(pv, 1)

                    for i in range(NT + 1):
                        if i < NT:
                            scores(i)
                        if i >= 1:
                            turn(i - 1)
                        if i == 5:
                            weigh(0)
                    weigh(1)

            @block.scalar
            def _(act):
                act.sem_inc(t_free, 1)
                with act.Fori(0, HEADS) as h:
                    if diff:
                        act.wait_ge(proj, 3 * h + 3)
                        act.wait_ge(pv, 2 * h + 1)
                        act.activation(v[:].rearrange("p n d -> p (n d)"), ps[0][:], ACT.Copy).then_inc(v_ready, 1)
                        act.wait_ge(v_ready, h + 1)
                        act.sem_inc(free0, 1)
                    else:
                        act.wait_ge(proj, 4 * h + 2)
                        act.activation(qt[:], ps[1][:], ACT.Copy).then_inc(q_ready, 1)
                        act.wait_ge(q_ready, h + 1)
                        act.sem_inc(free1, 1)
                        act.wait_ge(proj, 4 * h + 3)
                        act.activation(kt[:], ps[0][:], ACT.Copy).then_inc(k_ready, 1)
                        act.wait_ge(k_ready, h + 1)
                        act.sem_inc(free0, 1)
                        act.wait_ge(proj, 4 * h + 4)
                        act.wait_ge(pv, 2 * h + 1)
                        act.activation(v[:].rearrange("p n d -> p (n d)"), ps[1][:], ACT.Copy).then_inc(v_ready, 1)
                        act.wait_ge(v_ready, h + 1)
                        act.sem_inc(free1, 1)

                    def copy_turned(i):
                        act.wait_ge(turned, NT * h + i + 1)
                        if i % 4 == 0:
                            act.wait_ge(pv, 2 * h + i // 4 + 1)
                        act.activation(pt[:, :, (i % 4) * P:(i % 4 + 1) * P], ptr[:], ACT.Copy).then_inc(copied, 1)
                        act.wait_ge(copied, NT * h + i + 1)
                        act.sem_inc(t_free, 1)

                    for i in range(NT):
                        for m in range(maps):
                            buf, use = slot(i, m)
                            act.wait_ge(nmax, maps * (NT * h + i) + m + 1)
                            if m == 0:
                                act.wait_ge(p_free, NT * h + i + 1)
                            act.activation(e[:, i % 2, m, :], ps[buf][:], ACT.Exp, bias=nm[:, i % 2, m:m + 1], scale=scale,
                                           accum_out=sm[:, i % 2, m:m + 1]).then_inc(expd, 1)
                            act.wait_ge(expd, maps * (NT * h + i) + m + 1)
                            act.sem_inc(free[buf], 1)
                        if i >= 1:
                            copy_turned(i - 1)
                    copy_turned(NT - 1)

            @block.vector
            def _(dve):
                dve.sem_inc(p_free, 2)
                dve.sem_inc(mixed, 1)
                with dve.Fori(0, HEADS) as h:
                    if diff:
                        dve.wait_ge(proj, 3 * h + 1)
                        rope_rotate(dve, qt[:], ps[0], g, tmp, P, rope_step, 2 * h).then_inc(q_ready, 1)
                        dve.wait_ge(q_ready, h + 1)
                        dve.sem_inc(free0, 1)
                        dve.wait_ge(proj, 3 * h + 2)
                        rope_rotate(dve, kt[:], ps[1], g, tmp, P, rope_step, 2 * h + 1).then_inc(k_ready, 1)
                        dve.wait_ge(k_ready, h + 1)
                        dve.sem_inc(free1, 1)
                    else:
                        dve.wait_ge(proj, 4 * h + 1)
                        rope_rotate(dve, qpe[:], ps[0], g, tmp, ROPE, rope_step, h).then_inc(qpe_ready, 1)
                        dve.sem_inc(free0, 1)

                    def find_max(i):
                        for m in range(maps):
                            n = maps * (NT * h + i) + m
                            dve.wait_ge(scored, n + 1)
                            dve.tensor_reduce(mx[:, i % 2, m:m + 1], ps[slot(i, m)[0]][:], AX_X, ALU.max).then_inc(maxed, 1)
                            dve.wait_ge(maxed, n + 1)
                            dve.tensor_scalar(nm[:, i % 2, m:m + 1], mx[:, i % 2, m:m + 1], -scale, None, ALU.mult).then_inc(nmax, 1)

                    def finish(i):
                        b = i % 2
                        dve.wait_ge(expd, maps * (NT * h + i + 1))
                        dve.reciprocal(ri[:, b, :], sm[:, b, :]).then_inc(sumr, 1)
                        if not diff:
                            dve.wait_ge(sumr, NT * h + i + 1)
                            dve.tensor_scalar(e[:, b, 0, :], e[:, b, 0, :], ri[:, b, 0:1], None, ALU.mult).then_inc(probs, 1)
                            return
                        dve.wait_ge(sumr, 2 * (NT * h + i) + 1)
                        dve.tensor_scalar(r2[:, b:b + 1], ri[:, b, 1:2], g.neg_lam[:], None, ALU.mult).then_inc(sumr, 1)
                        dve.wait_ge(sumr, 2 * (NT * h + i) + 2)
                        dve.tensor_scalar(e[:, b, 1, :], e[:, b, 1, :], r2[:, b:b + 1], None, ALU.mult).then_inc(combined, 1)
                        dve.wait_ge(combined, NT * h + i + 1)
                        dve.scalar_tensor_tensor(out=pr[:, b, :], in0=e[:, b, 0, :], scalar=ri[:, b, 0:1], in1=e[:, b, 1, :],
                                                 op0=ALU.mult, op1=ALU.add).then_inc(probs, 1)

                    def take(j):
                        cols = slice(j * HALF, (j + 1) * HALF)
                        dve.wait_ge(pv, 2 * h + j + 2)
                        if diff:
                            dve.tensor_copy(g.dmix[:, ds(h, 1), cols], po[:].unsqueeze(1)).then_inc(mixed, 1)
                        else:
                            dve.tensor_copy(g.mix_a[0][:, ds(h, 1), cols], po[:].unsqueeze(1)).then_inc(leading, 1)
                            dve.wait_ge(leading, 2 * h + j + 1)
                            dve.tensor_tensor(g.mix_a[1][:, ds(h, 1), cols], po[:].unsqueeze(1),
                                              g.mix_a[0][:, ds(h, 1), cols].bitcast(F32), ALU.subtract).then_inc(mixed, 1)

                    def release(i):
                        dve.wait_ge(turned, NT * h + i + 1)
                        dve.sem_inc(p_free, 1)

                    for i in range(NT):
                        if i >= 2:
                            release(i - 2)
                        find_max(i)
                        finish(i)
                        if i == 6:
                            take(0)
                    release(NT - 2)
                    release(NT - 1)
                    take(1)


def head_norm(nc, g, mix_b):
    with ExitStack() as ctx:
        squared, summed, rooted, inv, done, high, low = sems(nc, g, "hn_squared hn_summed hn_rooted hn_inv hn_done hn_high hn_low")
        sq = ctx.enter_context(nc.sbuf_tensor("hn_sq", [P, HEADS, T], F32))
        root = ctx.enter_context(nc.sbuf_tensor("hn_root", [P, HEADS, T], F32))
        gs = ctx.enter_context(nc.sbuf_tensor("hn_gs", [P, 1], F32))
        ps = ctx.enter_context(nc.psum_tensor("hn_ps", [P, HEADS, T], F32))
        with nc.Block() as block:

            @block.scalar
            def _(act):
                for h in range(HEADS):
                    act.activation(sq[:, h, :], g.dmix[:, h, :], ACT.Square).then_inc(squared, 1)
                for h in range(HEADS):
                    act.wait_ge(summed, h + 1)
                    act.activation(root[:, h, :], ps[:, h, :], ACT.Sqrt, bias=g.eps[:], scale=1.0 / P).then_inc(rooted, 1)
                for h in range(HEADS):
                    act.wait_ge(done, h + 1)
                    act.activation(mix_b[0][:, h, :], g.dmix[:, h, :], ACT.Copy).then_inc(high, 1)

            @block.tensor
            def _(pe):
                for h in range(HEADS):
                    pe.wait_ge(squared, h + 1)
                    for hf in range(2):
                        o = pe.matmul(ps[:, h, hf * HALF:(hf + 1) * HALF], g.ones[:], sq[:, h, hf * HALF:(hf + 1) * HALF], start=True, stop=True)
                    o.then_inc(summed, 1)

            @block.vector
            def _(dve):
                dve.tensor_scalar(gs[:], g.col["sub_g"], 1.0 - LAMBDA_INIT, None, ALU.mult).then_inc(inv, 1)
                for h in range(HEADS):
                    dve.wait_ge(rooted, h + 1)
                    dve.reciprocal(root[:, h, :], root[:, h, :]).then_inc(inv, 1)
                    dve.wait_ge(inv, h + 2)
                    dve.scalar_tensor_tensor(out=g.dmix[:, h, :], in0=g.dmix[:, h, :], scalar=gs[:], in1=root[:, h, :],
                                             op0=ALU.mult, op1=ALU.mult).then_inc(done, 1)
                for h in range(HEADS):
                    dve.wait_ge(high, h + 1)
                    dve.tensor_tensor(mix_b[1][:, h, :], g.dmix[:, h, :], mix_b[0][:, h, :].bitcast(F32), ALU.subtract).then_inc(low, 1)


def project_rows(nc, g, tag, src, w_dram, gate, x_from, x_to, x_keep=None, gain=None):
    with ExitStack() as ctx:
        raw_in0, raw_in1, x_in0, x_in1, x_out0, x_out1, gain_in, gg, high, low, done, squared, rooted, inv, scaled, added = sems(
            nc, g, " ".join(tag + s for s in ("raw_in0 raw_in1 x_in0 x_in1 x_out0 x_out1 gain_in gg high low done squared rooted inv "
                                              "scaled added").split()))
        raw_in, x_in, x_out = (raw_in0, raw_in1), (x_in0, x_in1), (x_out0, x_out1)
        raw = ctx.enter_context(nc.sbuf_tensor(tag + "raw", [P, 2, D], F32))
        w = [ctx.enter_context(nc.sbuf_tensor(tag + f"w{j}", [P, KD, D], F32R)) for j in range(2)]
        gr = ctx.enter_context(nc.sbuf_tensor(tag + "gr", [P, D], F32)) if gain is not None else None
        junk = ctx.enter_context(nc.sbuf_tensor(tag + "junk", [P, D], F32)) if gain is not None else None
        ss = ctx.enter_context(nc.sbuf_tensor(tag + "ss", [P, 3, NT], F32))
        t = ctx.enter_context(nc.sbuf_tensor(tag + "t", [P, 2, D], F32))
        xr = None if x_keep is not None else ctx.enter_context(nc.sbuf_tensor(tag + "xr", [P, 2, D], F32))
        ps = ctx.enter_context(nc.psum_tensor(tag + "ps", [P, 4, D], F32))

        def x_tile(n):
            return x_keep[:, n, :] if x_keep is not None else xr[:, n % 2, :]

        with nc.Block() as block:

            @block.sync
            def _(sp):
                for k in range(KD):
                    if k >= 2:
                        sp.wait_ge(low, k - 1)
                    sp.dma_start(raw[:, k % 2, :], w_dram[k * P:(k + 1) * P, :]).then_inc(raw_in[k % 2], 16)
                if gain is not None:
                    sp.dma_start(gr[:], gain.partition_broadcast(P)).then_inc(gain_in, 16)
                for n in range(NT):
                    if n >= 2:
                        sp.wait_ge(x_out[n % 2], 16 * (n // 2))
                    sp.dma_start(x_tile(n), x_from[n * P:(n + 1) * P, :]).then_inc(x_in[n % 2], 16)
                    if n >= 1:
                        sp.wait_ge(added, n)
                        sp.dma_start(x_to[(n - 1) * P:n * P, :], x_tile(n - 1)).then_inc(x_out[(n - 1) % 2], 16)
                sp.wait_ge(added, NT)
                sp.dma_start(x_to[(NT - 1) * P:, :], x_tile(NT - 1)).then_inc(x_out[(NT - 1) % 2], 16)
                for b in range(2):
                    sp.wait_ge(x_out[b], 8 * NT)

            @block.tensor
            def _(pe):
                for r in range(2):
                    for k in range(KD):
                        if r == 0:
                            pe.wait_ge(low, k + 1)
                        for m in range(4):
                            n = 4 * r + m
                            if r == 1 and k == 0:
                                pe.wait_ge(scaled, m + 1)
                            for h in range(2):
                                cols = slice(h * HALF, (h + 1) * HALF)
                                o = three_passes(pe, ps[:, m, cols], [x[:, n * P:(n + 1) * P] for x in src(k)],
                                                 [x[:, k, cols] for x in w], k == 0, k == KD - 1)
                            if k == KD - 1:
                                o.then_inc(done, 1)

            @block.scalar
            def _(act):
                for k in range(KD):
                    act.wait_ge(raw_in[k % 2], 16 * (k // 2 + 1))
                    act.activation(w[0][:, k, :], raw[:, k % 2, :], ACT.Copy).then_inc(high, 1)
                if gain is not None:
                    for n in range(NT):
                        act.wait_ge(done, n + 1)
                        if n:
                            act.wait_ge(squared, n)
                        act.activation(junk[:], ps[:, n % 4, :], ACT.Square, accum_out=ss[:, 0, n:n + 1]).then_inc(squared, 1)
                        act.wait_ge(squared, n + 1)
                        act.activation(ss[:, 1, n:n + 1], ss[:, 0, n:n + 1], ACT.Sqrt, bias=g.eps[:], scale=1.0 / D).then_inc(rooted, 1)

            @block.vector
            def _(dve):
                for k in range(KD):
                    dve.wait_ge(high, k + 1)
                    dve.tensor_tensor(w[1][:, k, :], raw[:, k % 2, :], w[0][:, k, :].bitcast(F32), ALU.subtract).then_inc(low, 1)
                row = gate
                if gain is not None:
                    dve.wait_ge(gain_in, 16)
                    dve.tensor_tensor(gr[:], gr[:], gate, ALU.mult).then_inc(gg, 1)
                    dve.wait_ge(gg, 1)
                    row = gr[:]
                for n in range(NT):
                    if gain is None:
                        dve.wait_ge(done, n + 1)
                        dve.tensor_tensor(t[:, n % 2, :], ps[:, n % 4, :], row, ALU.mult).then_inc(scaled, 1)
                    else:
                        dve.wait_ge(rooted, n + 1)
                        dve.reciprocal(ss[:, 2, n:n + 1], ss[:, 1, n:n + 1]).then_inc(inv, 1)
                        dve.wait_ge(inv, n + 1)
                        dve.scalar_tensor_tensor(out=t[:, n % 2, :], in0=ps[:, n % 4, :], scalar=ss[:, 2, n:n + 1], in1=row,
                                                 op0=ALU.mult, op1=ALU.mult).then_inc(scaled, 1)
                    dve.wait_ge(scaled, n + 1)
                    dve.wait_ge(x_in[n % 2], 16 * (n // 2 + 1))
                    dve.tensor_tensor(x_tile(n), x_tile(n), t[:, n % 2, :], ALU.add).then_inc(added, 1)


def route(nc, g, a):
    with ExitStack() as ctx:
        w_in, b_in, c_in, logit, pads, step, ex, prefix, scattered, zeroed, table_in, table_t, done = sems(nc, g, "r_w_in r_b_in r_c_in r_logit r_pads r_step r_ex r_prefix r_scattered r_zeroed r_table_in r_table_t r_done")

        def sb(name, shape, dt=F32):
            return ctx.enter_context(nc.sbuf_tensor("r_" + name, shape, dt))

        NL = GROUPS + EXPERTS
        wr = sb("wr", [P, KD, NL])
        br = sb("br", [P, NL])
        iota = sb("iota", [P, MAX_BLOCKS])
        tri = sb("tri", [P, P])
        tok = sb("tok", [P, NT])
        lg = sb("lg", [P, NT, NL])
        gl = sb("gl", [P, NT, 8])
        gm = sb("gm", [P, NT, 8])
        gi = sb("gi", [P, NT, 8], U32)
        gif = sb("gif", [P, NT])
        gd = sb("gd", [P, NT, GROUPS])
        gp = sb("gp", [P, NT])
        oh = sb("oh", [P, NT, GROUPS])
        em = sb("em", [P, NT, EXPERTS])
        tm = sb("tm", [P, NT, 8])
        ti = sb("ti", [P, NT, 8], U32)
        tif = sb("tif", [P, NT, 2])
        dl = sb("dl", [P, NT])
        hot = sb("hot", [P, 2, NT, EXPERTS])
        both = sb("both", [P, NT, EXPERTS])
        pos = sb("pos", [P, NT, EXPERTS])
        off = sb("off", [P, NT + 1, EXPERTS])
        nb = sb("nb", [P, EXPERTS])
        inc = sb("inc", [P, EXPERTS])
        one = sb("one", [P, EXPERTS])
        sel = sb("sel", [P, NT, EXPERTS])
        dst = sb("dst", [P, 2, NT])
        cmp = sb("cmp", [1, MAX_BLOCKS, EXPERTS])
        blk = sb("blk", [1, MAX_BLOCKS + 1])
        zero = sb("zero", [P, MAX_BLOCKS])
        rt = sb("rt", [MAX_BLOCKS, P])
        pl = ctx.enter_context(nc.psum_tensor("r_pl", [P, NT, 64], F32))
        pp = ctx.enter_context(nc.psum_tensor("r_pp", [P, HALF], F32))
        pn = ctx.enter_context(nc.psum_tensor("r_pn", [P, HALF], F32))
        prt = ctx.enter_context(nc.psum_tensor("r_prt", [P, MAX_BLOCKS], F32))
        NE = NT * EXPERTS
        with nc.Block() as block:

            @block.sync
            def _(sp):
                sp.dma_start(wr[:, :, 0:GROUPS], a["w_router_group"][0].rearrange("(k p) n -> p k n", p=P)).then_inc(w_in, 16)
                sp.dma_start(wr[:, :, GROUPS:], a["w_router_expert"][0].rearrange("(k p) n -> p k n", p=P)).then_inc(w_in, 16)
                sp.dma_start(br[:, 0:GROUPS], a["b_router_group"][0].partition_broadcast(P)).then_inc(b_in, 16)
                sp.dma_start(br[:, GROUPS:], a["b_router_expert"][0].partition_broadcast(P)).then_inc(b_in, 16)
                sp.dma_start(iota[:], a["const_iota"][0].partition_broadcast(P)).then_inc(c_in, 16)
                sp.dma_start(tri[:], a["const_before"]).then_inc(c_in, 16)
                sp.dma_start(tok[:], a["const_token"]).then_inc(c_in, 16)
                sp.wait_ge(pads, 1)
                sp.dma_start(g.row_token.rearrange("(p n) a -> p (n a)", p=P), zero[:]).then_inc(zeroed, 16)
                sp.wait_ge(scattered, 16 * 2 * NT)
                sp.dma_start(rt[:], g.row_token.rearrange("(n p) a -> n (p a)", p=P)).then_inc(table_in, 16)
                sp.wait_ge(table_in, 16)

            @block.tensor
            def _(pe):
                pe.wait_ge(w_in, 32)
                for n in range(NT):
                    for k in range(KD):
                        o = pe.matmul(pl[:, n, 0:NL], g.ht[:, k, n * P:(n + 1) * P], wr[:, k, :], start=(k == 0), stop=(k == KD - 1))
                o.then_inc(logit, 1)
                pe.wait_ge(ex, 2)
                pe.wait_ge(c_in, 48)
                bv = both[:].rearrange("p n e -> p (n e)")
                pe.matmul(pp[:, 0:NE], tri[:], bv, start=True, stop=True).then_inc(prefix, 1)
                pe.matmul(pn[:, 0:NE], g.ones[:], bv, start=True, stop=True).then_inc(prefix, 1)
                pe.wait_ge(table_in, 16)
                pe.transpose(prt[:], rt[:], g.ident[0:MAX_BLOCKS, 0:MAX_BLOCKS]).then_inc(table_t, 1)

            @block.scalar
            def _(act):
                act.wait_ge(ex, 1)
                act.activation(gd[:], gd[:], ACT.Exp).then_inc(done, 1)
                act.activation(dl[:], dl[:], ACT.Exp).then_inc(done, 1)

            @block.vector
            def _(dve):
                count = [0]

                def seq(o):
                    count[0] += 1
                    o.then_inc(step, 1)
                    dve.wait_ge(step, count[0])

                def bc(x, n):
                    return x.unsqueeze(2).broadcast_to([P, NT, n])

                dve.memset(zero[:], 0.0).then_inc(pads, 1)
                dve.memset(one[:], 1.0)
                dve.memset(off[:, 0, :], 0.0)
                seq(dve.memset(gl[:], -BIG))
                dve.wait_ge(logit, 1)
                dve.wait_ge(b_in, 32)
                dve.wait_ge(c_in, 48)
                seq(dve.tensor_tensor(lg[:], pl[:, :, 0:NL], br[:].unsqueeze(1).broadcast_to([P, NT, NL]), ALU.add))
                seq(dve.tensor_copy(gl[:, :, 0:GROUPS], lg[:, :, 0:GROUPS]))
                for n in range(NT):
                    o = dve.max(gm[:, n, :], gl[:, n, :])
                seq(o)
                for n in range(NT):
                    o = dve.max_index(gi[:, n, :], gm[:, n, :], gl[:, n, :])
                seq(o)
                seq(dve.tensor_copy(gif[:], gi[:, :, 0]))
                seq(dve.tensor_tensor(oh[:], iota[:, 0:GROUPS].unsqueeze(1).broadcast_to([P, NT, GROUPS]), bc(gif[:], GROUPS), ALU.is_equal))
                for n in range(NT):
                    o = dve.tensor_tensor(em[:, n, :].rearrange("p (a b) -> p a b", a=GROUPS),
                                          lg[:, n, GROUPS:].rearrange("p (a b) -> p a b", a=GROUPS),
                                          oh[:, n, :].unsqueeze(2).broadcast_to([P, GROUPS, PER_GROUP]), ALU.mult)
                seq(o)
                seq(dve.tensor_scalar(oh[:], oh[:], -1.0, BIG, ALU.add, ALU.mult))
                for n in range(NT):
                    o = dve.tensor_tensor(em[:, n, :].rearrange("p (a b) -> p a b", a=GROUPS),
                                          em[:, n, :].rearrange("p (a b) -> p a b", a=GROUPS),
                                          oh[:, n, :].unsqueeze(2).broadcast_to([P, GROUPS, PER_GROUP]), ALU.add)
                seq(o)
                for n in range(NT):
                    o = dve.max(tm[:, n, :], em[:, n, :])
                seq(o)
                for n in range(NT):
                    o = dve.max_index(ti[:, n, :], tm[:, n, :], em[:, n, :])
                seq(o)
                seq(dve.tensor_copy(tif[:], ti[:, :, 0:2]))
                seq(dve.tensor_tensor(gd[:], lg[:, :, 0:GROUPS], bc(gm[:, :, 0], GROUPS), ALU.subtract))
                dve.tensor_tensor(dl[:], tm[:, :, 1], tm[:, :, 0], ALU.subtract).then_inc(ex, 1)
                for s in range(2):
                    o = dve.tensor_tensor(hot[:, s, :, :], iota[:, 0:EXPERTS].unsqueeze(1).broadcast_to([P, NT, EXPERTS]),
                                          bc(tif[:, :, s], EXPERTS), ALU.is_equal)
                seq(o)
                dve.tensor_tensor(both[:], hot[:, 0], hot[:, 1], ALU.add).then_inc(ex, 1)
                dve.wait_ge(done, 2)
                seq(dve.tensor_reduce(gp[:], gd[:], AX_X, ALU.add))
                seq(dve.scalar_tensor_tensor(out=gp[:], in0=dl[:], scalar=1.0, in1=gp[:], op0=ALU.add, op1=ALU.mult))
                seq(dve.reciprocal(g.wt[:, 0, :], gp[:]))
                seq(dve.tensor_tensor(g.wt[:, 1, :], g.wt[:, 0, :], dl[:], ALU.mult))
                dve.wait_ge(prefix, 2)
                for n in range(NT):
                    seq(dve.tensor_tensor(off[:, n + 1, :], off[:, n, :], pn[:, n * EXPERTS:(n + 1) * EXPERTS], ALU.add))
                seq(dve.tensor_scalar(nb[:], off[:, NT, :], 0.0, None, ALU.is_gt))
                for j in range(1, NT):
                    seq(dve.scalar_tensor_tensor(out=nb[:], in0=off[:, NT, :], scalar=float(j * P), in1=nb[:], op0=ALU.is_gt, op1=ALU.add))
                seq(dve.tensor_tensor_scan(inc[:], one[:], nb[:], 0.0, ALU.mult, ALU.add))
                seq(dve.tensor_tensor(nb[:], inc[:], nb[:], ALU.subtract))
                seq(dve.tensor_scalar(nb[:], nb[:], float(P), None, ALU.mult))
                seq(dve.tensor_tensor(pos[:].rearrange("p n e -> p (n e)"), pp[:, 0:NE], off[:, 0:NT, :].rearrange("p n e -> p (n e)"), ALU.add))
                seq(dve.tensor_tensor(pos[:], pos[:], nb[:].unsqueeze(1).broadcast_to([P, NT, EXPERTS]), ALU.add))
                for s in range(2):
                    seq(dve.tensor_tensor(sel[:], hot[:, s], pos[:], ALU.mult))
                    seq(dve.tensor_reduce(dst[:, s, :], sel[:], AX_X, ALU.add))
                dve.tensor_copy(g.dest[:], dst[:]).then_inc(pads, 1)
                seq(dve.tensor_tensor(cmp[:], inc[0:1, :].unsqueeze(1).broadcast_to([1, MAX_BLOCKS, EXPERTS]),
                                      iota[0:1, :].unsqueeze(2).broadcast_to([1, MAX_BLOCKS, EXPERTS]), ALU.is_le))
                seq(dve.tensor_reduce(blk[:, 0:MAX_BLOCKS], cmp[:], AX_X, ALU.add))
                seq(dve.tensor_scalar(blk[:, 0:MAX_BLOCKS], blk[:, 0:MAX_BLOCKS], float(EXPERTS - 1), None, ALU.min))
                seq(dve.tensor_scalar(cmp[:, 0, 0:MAX_BLOCKS // 2], iota[0:1, 0:MAX_BLOCKS // 2], 2.0, None, ALU.mult))
                seq(dve.tensor_scalar(cmp[:, 1, 0:MAX_BLOCKS // 2], cmp[:, 0, 0:MAX_BLOCKS // 2], inc[0:1, EXPERTS - 1:EXPERTS], None, ALU.is_lt))
                seq(dve.tensor_reduce(blk[:, MAX_BLOCKS:], cmp[:, 1, 0:MAX_BLOCKS // 2], AX_X, ALU.add))
                seq(dve.tensor_copy(g.blocks[:], blk[:]))
                dve.wait_ge(table_t, 1)
                seq(dve.tensor_copy(g.rows[:], prt[:]))

            @block.gpsimd
            def _(pool):
                pool.wait_ge(c_in, 48)
                pool.wait_ge(pads, 2)
                pool.wait_ge(zeroed, 16)
                for s in range(2):
                    for n in range(NT):
                        pool.indirect_dma_start(g.row_token, bass.IndirectOffsetOnAxis(ap=g.dest[:, s, n:n + 1], axis=0),
                                                tok[:, n:n + 1], None).then_inc(scattered, 16)
                pool.wait_ge(scattered, 16 * 2 * NT)


def experts(nc, g, a):
    with ExitStack() as ctx:
        names = ("g_in0 g_in1 u_in0 u_in1 d_in0 d_in1 gu_used d_used idx got got1 x_turned x_mul x_mod x_used act_in act_ready a_turned a_copied "
                 "y_done y_out0 y_out1 y_copied gu_free silu idx_seen cleared y_zeroed")
        (g_in0, g_in1, u_in0, u_in1, d_in0, d_in1, gu_used, d_used, idx_ready, got, got1, x_turned, x_mul, x_mod, x_used, act_in, act_ready, a_turned,
         a_copied, y_done, y_out0, y_out1, y_copied, gu_free, silu_done, idx_seen, cleared, y_zeroed) = sems(nc, g, " ".join("e_" + s for s in names.split()))
        g_in, u_in, d_in, y_out, got = (g_in0, g_in1), (u_in0, u_in1), (d_in0, d_in1), (y_out0, y_out1), (got, got1)

        def sb(name, shape, dt=F32):
            return ctx.enter_context(nc.sbuf_tensor("e_" + name, shape, dt))

        wg = sb("wg", [P, 2, KD, FE])
        wu = sb("wu", [P, 2, KD, FE])
        wd = sb("wd", [P, 2, KE, D])
        idx = [sb(f"idx{b}", [P, 1], U32) for b in range(2)]
        xg = [sb(f"xg{b}", [P, D]) for b in range(2)]
        xt = sb("xt", [P, 2, KD, P])
        sg = sb("sg", [P, 2, FE])
        at = sb("at", [P, 2, FE])
        att = sb("att", [P, 2, KE, P])
        yo = sb("yo", [P, 2, D])
        zrow = sb("zrow", [P, D])
        px = ctx.enter_context(nc.psum_tensor("e_px", [P, KD, P], F32))
        pgu = ctx.enter_context(nc.psum_tensor("e_pgu", [P, 2, 2, FE], F32))
        py = ctx.enter_context(nc.psum_tensor("e_py", [P, D], F32))
        wg_d = a["w_expert_gate"][0].rearrange("e (k p) n -> e p k n", p=P)
        wu_d = a["w_expert_up"][0].rearrange("e (k p) n -> e p k n", p=P)
        wd_d = a["w_expert_down"][0].rearrange("e (k p) n -> e p k n", p=P)
        y_rows = g.y_dram.rearrange("(n p) d -> n p d", p=P)

        def pairs(eng):
            return eng.value_load(g.blocks[0:1, MAX_BLOCKS:MAX_BLOCKS + 1], min_val=1, max_val=MAX_BLOCKS // 2)

        with nc.Block() as block:

            @block.sync
            def _(sp):
                n = pairs(sp)
                with sp.Fori(0, n) as i:
                    for b in range(2):
                        ex = sp.value_load(g.blocks[0:1, ds(2 * i + b, 1)], min_val=0, max_val=EXPERTS - 1)
                        sp.wait_ge(gu_used, 2 * i + b + 1)
                        sp.dma_start(wg[:, b, :, :], wg_d[ds(ex, 1)].squeeze(0)).then_inc(g_in[b], 16)
                        sp.dma_start(wu[:, b, :, :], wu_d[ds(ex, 1)].squeeze(0)).then_inc(u_in[b], 16)
                        sp.wait_ge(d_used, 2 * i + b + 1)
                        sp.dma_start(wd[:, b, :, :], wd_d[ds(ex, 1)].squeeze(0)).then_inc(d_in[b], 16)

            @block.gpsimd
            def _(pool):
                n = pairs(pool)
                pool.sem_inc(x_used, 2)
                with pool.Fori(0, n) as i:
                    for b in range(2):
                        pool.wait_ge(x_used, 2 * i + b + 1)
                        pool.tensor_copy(idx[b][:], g.rows[:, ds(2 * i + b, 1)]).then_inc(idx_ready, 1)
                        pool.wait_ge(idx_ready, 2 * i + b + 1)
                        pool.sem_inc(idx_seen, 1)
                        pool.indirect_dma_start(xg[b][:], None, g.xn_dram, bass.IndirectOffsetOnAxis(ap=idx[b][:], axis=0)).then_inc(got[b], 16)

            @block.tensor
            def _(pe):
                n = pairs(pe)
                pe.sem_inc(gu_used, 2)
                pe.sem_inc(d_used, 2)
                with pe.Fori(0, n) as i:
                    for b in range(2):
                        pe.wait_ge(got[b], 16 * i + 16)
                        if b == 0:
                            pe.wait_ge(a_copied, 2 * i + 1)
                        else:
                            pe.wait_ge(x_mul, 2 * i + 1)
                        for k in range(KD):
                            o = pe.transpose(px[:, k, :], xg[b][:, k * P:(k + 1) * P], g.ident[:])
                        o.then_inc(x_turned, 1)
                        pe.wait_ge(x_turned, 2 * i + b + 1)
                        pe.sem_inc(x_used, 1)
                    for b in range(2):
                        pe.wait_ge(x_mod, 2 * i + b + 1)
                        pe.wait_ge(gu_free, 2 * i + 1)
                        pe.wait_ge(g_in[b], 16 * i + 16)
                        for k in range(KD):
                            pe.matmul(pgu[:, b, 0, :], xt[:, b, k, :], wg[:, b, k, :], start=(k == 0), stop=(k == KD - 1))
                        pe.wait_ge(u_in[b], 16 * i + 16)
                        for k in range(KD):
                            o = pe.matmul(pgu[:, b, 1, :], xt[:, b, k, :], wu[:, b, k, :], start=(k == 0), stop=(k == KD - 1))
                        o.then_inc(act_in, 1)
                        pe.wait_ge(act_in, 2 * i + b + 1)
                        pe.sem_inc(gu_used, 1)
                    for b in range(2):
                        pe.wait_ge(act_ready, 2 * i + b + 1)
                        if b == 1:
                            pe.wait_ge(a_copied, 2 * i + 2)
                        for k in range(KE):
                            o = pe.transpose(px[:, k, :], at[:, b, k * P:(k + 1) * P], g.ident[:])
                        o.then_inc(a_turned, 1)
                        pe.wait_ge(a_copied, 2 * i + b + 2)
                        pe.wait_ge(d_in[b], 16 * i + 16)
                        pe.wait_ge(y_copied, 2 * i + b + 1)
                        for h in range(2):
                            for k in range(KE):
                                o = pe.matmul(py[:, h * HALF:(h + 1) * HALF], att[:, b, k, :], wd[:, b, k, h * HALF:(h + 1) * HALF],
                                              start=(k == 0), stop=(k == KE - 1))
                        o.then_inc(y_done, 1)
                        pe.wait_ge(y_done, 2 * i + b + 1)
                        pe.sem_inc(d_used, 1)

            @block.vector
            def _(dve):
                dve.memset(zrow[:], 0.0).then_inc(cleared, 1)
                dve.sem_inc(gu_free, 1)
                dve.sem_inc(y_copied, 1)
                n = pairs(dve)
                with dve.Fori(0, n) as i:
                    for b in range(2):
                        dve.wait_ge(x_turned, 2 * i + b + 1)
                        dve.tensor_tensor(xt[:, b], px[:], g.a_col[:].unsqueeze(2).broadcast_to([P, KD, P]), ALU.mult).then_inc(x_mul, 1)
                        dve.wait_ge(x_mul, 2 * i + b + 1)
                        dve.tensor_tensor(xt[:, b], xt[:, b], g.b_col[:].unsqueeze(2).broadcast_to([P, KD, P]), ALU.add).then_inc(x_mod, 1)
                    for b in range(2):
                        dve.wait_ge(silu_done, 2 * i + b + 1)
                        dve.tensor_tensor(at[:, b, :], sg[:, b, :], pgu[:, b, 1, :], ALU.mult).then_inc(act_ready, 1)
                        dve.wait_ge(act_ready, 2 * i + b + 1)
                        dve.sem_inc(gu_free, 1)
                    for b in range(2):
                        dve.wait_ge(y_done, 2 * i + b + 1)
                        dve.wait_ge(y_out[b], 16 * i + 16)
                        dve.tensor_copy(yo[:, b, :], py[:]).then_inc(y_copied, 1)

            @block.scalar
            def _(act):
                n = pairs(act)
                act.sem_inc(a_copied, 1)
                act.sem_inc(y_out0, 16)
                act.sem_inc(y_out1, 16)
                act.wait_ge(cleared, 1)
                with act.Fori(n, Y_BLOCKS // 2) as i:
                    for b in range(2):
                        act.dma_start(y_rows[ds(2 * i + b, 1)].squeeze(0), zrow[:]).then_inc(y_zeroed, 16)
                with act.Fori(0, n) as i:
                    act.sem_inc(y_zeroed, 32)
                    for b in range(2):
                        act.wait_ge(act_in, 2 * i + b + 1)
                        act.activation(sg[:, b, :], pgu[:, b, 0, :], ACT.Silu).then_inc(silu_done, 1)
                    for b in range(2):
                        act.wait_ge(a_turned, 2 * i + b + 1)
                        act.activation(att[:, b], px[:, 0:KE, :], ACT.Copy).then_inc(a_copied, 1)
                        act.wait_ge(y_copied, 2 * i + b + 2)
                        act.dma_start(y_rows[ds(2 * i + b, 1)].squeeze(0), yo[:, b, :]).then_inc(y_out[b], 16)
                act.wait_ge(y_out0, 16 * n + 16)
                act.sem_inc(silu_done, 1)
                act.wait_ge(y_out1, 16 * n + 16)
                act.sem_inc(silu_done, 1)
                act.wait_ge(y_zeroed, 16 * Y_BLOCKS)
                act.sem_inc(silu_done, 1)


def combine(nc, g, a):
    with ExitStack() as ctx:
        x_in, x_out = sems(nc, g, "c_x_in c_x_out")
        fg_in, rows_in0, rows_in1, rows_in2, rows_in3, w1, mixed, scaled, added, squared, rooted, inv, normed, used = sems(nc, g, "c_fg_in c_rows_in0 c_rows_in1 c_rows_in2 c_rows_in3 c_w1 c_mixed c_scaled c_added c_squared c_rooted c_inv c_normed c_used")
        rows_in = (rows_in0, rows_in1, rows_in2, rows_in3)
        y = ctx.enter_context(nc.sbuf_tensor("c_y", [P, 4, 2, D], F32))
        fg = ctx.enter_context(nc.sbuf_tensor("c_fg", [P, D], F32))
        junk = ctx.enter_context(nc.sbuf_tensor("c_junk", [P, D], F32))
        ss = ctx.enter_context(nc.sbuf_tensor("c_ss", [P, 3, NT], F32))
        with nc.Block() as block:

            @block.sync
            def _(sp):
                sp.dma_start(g.x[:], g.x_dram.rearrange("(n p) d -> p n d", p=P)).then_inc(x_in, 16)
                sp.dma_start(fg[:], a["final_norm_g"].partition_broadcast(P)).then_inc(fg_in, 16)
                for n in range(NT):
                    sp.wait_ge(normed, n + 1)
                    sp.dma_start(g.x_dram[n * P:(n + 1) * P, :], g.x[:, n, :]).then_inc(x_out, 16)
                sp.wait_ge(x_out, 16 * NT)

            @block.gpsimd
            def _(pool):
                for n in range(NT):
                    if n >= 4:
                        pool.wait_ge(added, n - 3)
                    for s in range(2):
                        pool.indirect_dma_start(y[:, n % 4, s, :], None, g.y_dram,
                                                bass.IndirectOffsetOnAxis(ap=g.dest[:, s, n:n + 1], axis=0)).then_inc(rows_in[n % 4], 16)

            @block.vector
            def _(dve):
                dve.wait_ge(x_in, 16)
                for n in range(NT):
                    dve.wait_ge(rows_in[n % 4], 32 * (n // 4 + 1))
                    dve.tensor_scalar(y[:, n % 4, 0, :], y[:, n % 4, 0, :], g.wt[:, 0, n:n + 1], None, ALU.mult).then_inc(w1, 1)
                    dve.wait_ge(w1, n + 1)
                    dve.scalar_tensor_tensor(out=y[:, n % 4, 0, :], in0=y[:, n % 4, 1, :], scalar=g.wt[:, 1, n:n + 1],
                                             in1=y[:, n % 4, 0, :], op0=ALU.mult, op1=ALU.add).then_inc(mixed, 1)
                    dve.wait_ge(mixed, n + 1)
                    dve.tensor_tensor(y[:, n % 4, 0, :], y[:, n % 4, 0, :], g.gate[:, 1, :], ALU.mult).then_inc(scaled, 1)
                    dve.wait_ge(scaled, n + 1)
                    dve.tensor_tensor(g.x[:, n, :], g.x[:, n, :], y[:, n % 4, 0, :], ALU.add).then_inc(added, 1)
                dve.wait_ge(fg_in, 16)
                for n in range(NT):
                    dve.wait_ge(rooted, n + 1)
                    dve.reciprocal(ss[:, 2, n:n + 1], ss[:, 1, n:n + 1]).then_inc(inv, 1)
                    dve.wait_ge(inv, n + 1)
                    dve.scalar_tensor_tensor(out=g.x[:, n, :], in0=g.x[:, n, :], scalar=ss[:, 2, n:n + 1], in1=fg[:],
                                             op0=ALU.mult, op1=ALU.mult).then_inc(normed, 1)

            @block.scalar
            def _(act):
                for n in range(NT):
                    act.wait_ge(added, n + 1)
                    if n:
                        act.wait_ge(squared, n)
                    act.activation(junk[:], g.x[:, n, :], ACT.Square, accum_out=ss[:, 0, n:n + 1]).then_inc(squared, 1)
                    act.wait_ge(squared, n + 1)
                    act.activation(ss[:, 1, n:n + 1], ss[:, 0, n:n + 1], ACT.Sqrt, bias=g.eps[:], scale=1.0 / D).then_inc(rooted, 1)


def short_conv(nc, g, a, h_t, y_t):
    with ExitStack() as ctx:
        asked, raw_in0, raw_in1, raw_in2, high, low, used, c_out, u_done, t1, t2, t3, freed, y_high, y_low, halo = sems(
            nc, g, "s_asked s_raw_in0 s_raw_in1 s_raw_in2 s_high s_low s_used s_c_out s_u_done s_t1 s_t2 s_t3 s_freed s_y_high s_y_low s_halo")
        raw_in = (raw_in0, raw_in1, raw_in2)
        raw = ctx.enter_context(nc.sbuf_tensor("s_raw", [P, 3, KD, P], F32))
        w = [ctx.enter_context(nc.sbuf_tensor(f"s_w{j}", [P, 3, KD, P], F32R)) for j in range(2)]
        cc = ctx.enter_context(nc.sbuf_tensor("s_cc", [P, T], F32))
        u = ctx.enter_context(nc.sbuf_tensor("s_u", [P, T + 2], F32))
        t = ctx.enter_context(nc.sbuf_tensor("s_t", [P, 2, T], F32))
        ps = [ctx.enter_context(nc.psum_tensor(f"s_ps{i}", [P, 1, T], F32)) for i in range(3)]
        w_v = a["conv_w_in_2"][0].rearrange("(k p) (s n) -> p k s n", p=P, s=3)
        cw = g.col["conv_w"]
        order = (1, 2, 0)
        with nc.Block() as block:

            @block.sync
            def _(sp):
                with sp.Fori(0, KD) as f:
                    for j, s in enumerate(order):
                        sp.wait_ge(low, 3 * f + j + 1)
                        sp.sem_inc(asked, 1)
                        sp.dma_start(raw[:, j], w_v[:, :, s, ds(f * P, P)]).then_inc(raw_in[j], 16)

            @block.tensor
            def _(pe):
                pe.sem_inc(used, 3)
                with pe.Fori(0, KD) as f:
                    for j in range(3):
                        pe.wait_ge(low, 3 * f + j + 4)
                        if j == 0:
                            pe.wait_ge(c_out, f + 1)
                        elif j == 1:
                            pe.wait_ge(u_done, f + 1)
                        else:
                            pe.wait_ge(freed, f + 1)
                        for h in range(2):
                            cols = slice(h * HALF, (h + 1) * HALF)
                            for k in range(KD):
                                o = three_passes(pe, ps[j][:, 0, cols], [x[:, j, k, :] for x in w], [x[:, k, cols] for x in h_t],
                                                 k == 0, k == KD - 1)
                        o.then_inc(used, 1)

            @block.scalar
            def _(act):
                act.sem_inc(c_out, 1)

                def leading(f, j):
                    act.wait_ge(raw_in[j], 16 * f + 16)
                    act.wait_ge(used, 3 * f + j + 1)
                    act.activation(w[0][:, j], raw[:, j], ACT.Copy).then_inc(high, 1)

                def chunk(f, last):
                    act.wait_ge(used, 3 * f + 4)
                    act.wait_ge(u_done, f + 1)
                    act.activation(cc[:], ps[0][:, 0, :], ACT.Copy).then_inc(c_out, 1)
                    if not last:
                        for j in range(3):
                            leading(f + 1, j)

                for j in range(3):
                    leading(0, j)
                with act.Fori(0, KD - 1) as f:
                    chunk(f, False)
                chunk(KD - 1, True)

            @block.vector
            def _(dve):
                dve.sem_inc(low, 3)
                dve.sem_inc(u_done, 1)
                dve.sem_inc(freed, 1)
                dve.memset(u[:, 0:2], 0.0).then_inc(halo, 1)
                dve.wait_ge(halo, 1)

                def rest(f, j):
                    dve.wait_ge(high, 3 * f + j + 1)
                    dve.tensor_tensor(w[1][:, j], raw[:, j], w[0][:, j].bitcast(F32), ALU.subtract).then_inc(low, 1)

                def chunk(f, last):
                    dve.wait_ge(c_out, f + 2)
                    if not last:
                        rest(f + 1, 0)
                    dve.wait_ge(used, 3 * f + 5)
                    dve.tensor_tensor(u[:, 2:], cc[:], ps[1][:, 0, :], ALU.mult).then_inc(u_done, 1)
                    dve.wait_ge(u_done, f + 2)
                    dve.tensor_scalar(t[:, 0, :], u[:, 0:T], cw[:, ds(f, 1)], None, ALU.mult).then_inc(t1, 1)
                    dve.wait_ge(t1, f + 1)
                    dve.scalar_tensor_tensor(out=t[:, 1, :], in0=u[:, 1:T + 1], scalar=cw[:, ds(KD + f, 1)],
                                             in1=t[:, 0, :], op0=ALU.mult, op1=ALU.add).then_inc(t2, 1)
                    dve.wait_ge(t2, f + 1)
                    dve.scalar_tensor_tensor(out=t[:, 0, :], in0=u[:, 2:T + 2], scalar=cw[:, ds(2 * KD + f, 1)],
                                             in1=t[:, 1, :], op0=ALU.mult, op1=ALU.add).then_inc(t3, 1)
                    dve.wait_ge(t3, f + 1)
                    if not last:
                        rest(f + 1, 1)
                    dve.wait_ge(used, 3 * f + 6)
                    dve.tensor_tensor(t[:, 1, :], t[:, 0, :], ps[2][:, 0, :], ALU.mult).then_inc(freed, 1)
                    dve.wait_ge(freed, f + 2)
                    if not last:
                        rest(f + 1, 2)
                    dve.tensor_copy(y_t[0][:, ds(f, 1), :], t[:, 1:2, :]).then_inc(y_high, 1)
                    dve.wait_ge(y_high, f + 1)
                    dve.tensor_tensor(y_t[1][:, ds(f, 1), :], t[:, 1:2, :], y_t[0][:, ds(f, 1), :].bitcast(F32), ALU.subtract).then_inc(y_low, 1)
                    dve.wait_ge(y_low, f + 1)

                for j in range(3):
                    rest(0, j)
                with dve.Fori(0, KD - 1) as f:
                    chunk(f, False)
                chunk(KD - 1, True)


def feed_forward(nc, g, a, out):
    NH = NT // 2
    TH = T // 2
    PIECES = 3 * KF
    with ExitStack() as ctx:
        names = ("raw_in0 raw_in1 high low used x_in x_out gain_in gg sq root inv staged turned full_done h_high h_low silu acted a_high "
                 "a_low down squared rooted inv2 scaled added ab")
        (raw_in0, raw_in1, high, low, used, x_in, x_out, gain_in, gg, sq, root, inv, staged, turned, full_done, h_high, h_low, silu, acted,
         a_high, a_low, down, squared, rooted, inv2, scaled, added, ab) = sems(nc, g, " ".join("f_" + s for s in names.split()))
        raw_in = (raw_in0, raw_in1)

        def sb(name, shape, dt=F32):
            return ctx.enter_context(nc.sbuf_tensor("f_" + name, shape, dt))

        x = sb("x", [P, NH, D])
        h_t = [sb(f"h{j}", [P, KD, TH], F32R) for j in range(2)]
        a_t = [sb(f"a{j}", [P, KF, TH], F32R) for j in range(2)]
        raw = sb("raw", [P, 2, D])
        w = [sb(f"w{j}", [P, 2, D], F32R) for j in range(2)]
        sg = sb("sg", [P, 2, TH])
        y = sb("y", [P, 2, TH])
        r = sb("r", [P, 2, D])
        gr = sb("gr", [P, D])
        ss = sb("ss", [P, 6, NH])
        ps = ctx.enter_context(nc.psum_tensor("f_ps", [P, NH, 2, HALF], F32))
        pg, pu = ps[:, 0, 0, :], ps[:, 0, 1, :]
        w_up = a["ffn_w_gate_up_2"][0].rearrange("(k p) (s n) -> p k s n", p=P, s=2)
        w_down = a["ffn_w_down_2"][0].rearrange("(f p) n -> f p n", p=P)
        x_rows = g.x_dram.rearrange("(h n p) d -> h p n d", p=P, h=2)
        out_rows = out[0].rearrange("(h n p) d -> h p n d", p=P, h=2)
        with nc.Block() as block:

            @block.sync
            def _(sp):
                sp.dma_start(gr[:], a["norm_gains_2"][0, 3].partition_broadcast(P)).then_inc(gain_in, 16)
                sp.sem_inc(x_out, 16)
                with sp.Fori(0, 2) as h:
                    sp.wait_ge(x_out, 64 * h + 16)
                    sp.dma_start(x[:], x_rows[ds(h, 1)].squeeze(0)).then_inc(x_in, 16)
                    with sp.Fori(0, KF) as f:
                        for s in range(2):
                            sp.wait_ge(low, PIECES * h + 2 * f + s + 1)
                            sp.dma_start(raw[:, s, :].rearrange("p (k n) -> p k n", k=KD), w_up[:, :, s, ds(f * P, P)]).then_inc(raw_in[s], 16)
                    with sp.Fori(0, KF // 2) as f:
                        for s in range(2):
                            sp.wait_ge(low, PIECES * h + 2 * KF + 2 * f + s + 1)
                            sp.dma_start(raw[:, s, :], w_down[ds(2 * f + s, 1)].squeeze(0)).then_inc(raw_in[s], 16)
                    for n in range(NH):
                        sp.wait_ge(added, NH * h + n + 1)
                        sp.dma_start(out_rows[ds(h, 1), :, n, :].squeeze(0), x[:, n, :]).then_inc(x_out, 16)
                sp.wait_ge(x_out, 16 + 128)

            @block.tensor
            def _(pe):
                pe.sem_inc(used, 2)
                pe.sem_inc(turned, 2)
                with pe.Fori(0, 2) as h:
                    pe.wait_ge(scaled, NH * h + 1)
                    for k in range(KD):
                        pe.wait_ge(staged, KD * h + k + 1)
                        pe.wait_ge(full_done, KD * h + k + 1)
                        for n in range(NH):
                            o = pe.transpose(ps[:, 0, k % 2, n * P:(n + 1) * P], sg[:, k % 2, n * P:(n + 1) * P], g.ident[:])
                        o.then_inc(turned, 1)
                    with pe.Fori(0, KF) as f:
                        pe.wait_ge(h_low, KD * h + KD)
                        for s, bank in enumerate((pg, pu)):
                            pe.wait_ge(low, PIECES * h + 2 * f + s + 3)
                            if s == 0:
                                pe.wait_ge(silu, KF * h + f + 1)
                            else:
                                pe.wait_ge(acted, KF * h + f + 1)
                            for k in range(KD):
                                o = three_passes(pe, bank, [v[:, s, k * P:(k + 1) * P] for v in w], [v[:, k, :] for v in h_t],
                                                 k == 0, k == KD - 1)
                            o.then_inc(used, 1)
                    pe.wait_ge(a_low, KF * h + KF)
                    for f in range(KF):
                        pe.wait_ge(low, PIECES * h + 2 * KF + f + 3)
                        for n in range(NH):
                            for c in range(2):
                                cols = slice(c * HALF, (c + 1) * HALF)
                                o = three_passes(pe, ps[:, n, c, :], [v[:, f, n * P:(n + 1) * P] for v in a_t],
                                                 [v[:, f % 2, cols] for v in w], f == 0, f == KF - 1)
                            if f == KF - 1 and n < NH - 1:
                                o.then_inc(down, 1)
                        o.then_inc(used, 1)

            @block.scalar
            def _(act):
                act.sem_inc(silu, 1)
                act.sem_inc(full_done, 2)
                act.sem_inc(sq, 1)

                def leading(j_in_half, h, pair, s):
                    act.wait_ge(raw_in[s], 16 * (PIECES // 2 * h + pair) + 16)
                    act.wait_ge(used, PIECES * h + j_in_half + 1)
                    act.activation(w[0][:, s, :], raw[:, s, :], ACT.Copy).then_inc(high, 1)

                with act.Fori(0, 2) as h:
                    for s in range(2):
                        leading(s, h, 0, s)
                    act.wait_ge(x_in, 16 * h + 16)
                    for n in range(NH):
                        act.wait_ge(sq, NH * h + n + 1)
                        act.activation(r[:, 0, :], x[:, n, :], ACT.Square, accum_out=ss[:, 0, n:n + 1]).then_inc(sq, 1)
                    act.wait_ge(sq, NH * h + NH + 1)
                    act.activation(ss[:, 1, :], ss[:, 0, :], ACT.Sqrt, bias=g.eps[:], scale=1.0 / D).then_inc(root, 1)
                    act.wait_ge(ab, 1)
                    for k in range(KD):
                        act.wait_ge(turned, KD * h + k + 3)
                        if k >= 2:
                            act.wait_ge(h_low, KD * h + k - 1)
                        act.activation(y[:, k % 2, :], ps[:, 0, k % 2, :], ACT.Identity, bias=g.b_col[:, k:k + 1],
                                       scale=g.a_col[:, k:k + 1]).then_inc(full_done, 1)
                    with act.Fori(0, KF) as f:
                        act.wait_ge(used, PIECES * h + 2 * f + 3)
                        act.wait_ge(acted, KF * h + f + 1)
                        act.activation(sg[:, 0, :], pg, ACT.Silu).then_inc(silu, 1)
                        leading(2 * f + 2, h, f + 1, 0)
                        leading(2 * f + 3, h, f + 1, 1)
                    for f in range(KF - 2):
                        leading(2 * KF + f + 2, h, KF + f // 2 + 1, f % 2)
                    for n in range(NH):
                        if n < NH - 1:
                            act.wait_ge(down, (NH - 1) * h + n + 1)
                        else:
                            act.wait_ge(used, PIECES * (h + 1) + 2)
                        act.activation(r[:, 1, :], ps[:, n], ACT.Square, accum_out=ss[:, 3, n:n + 1]).then_inc(squared, 1)
                        act.wait_ge(squared, NH * h + n + 1)
                        act.activation(ss[:, 4, n:n + 1], ss[:, 3, n:n + 1], ACT.Sqrt, bias=g.eps[:], scale=1.0 / D).then_inc(rooted, 1)

            @block.vector
            def _(dve):
                dve.sem_inc(low, 2)
                dve.sem_inc(acted, 1)
                dve.sem_inc(scaled, 1)
                dve.scalar_tensor_tensor(out=g.a_col[:], in0=g.mod2[:, 1, 8:16], scalar=1.0, in1=g.col["g2"], op0=ALU.add, op1=ALU.mult)
                dve.tensor_copy(g.b_col[:], g.mod2[:, 1, 0:8]).then_inc(ab, 1)
                dve.wait_ge(gain_in, 16)
                dve.tensor_tensor(gr[:], gr[:], g.gate2[:, 1, :], ALU.mult).then_inc(gg, 1)
                dve.wait_ge(gg, 1)

                def rest(j_in_half, h, s):
                    dve.wait_ge(high, PIECES * h + j_in_half + 1)
                    dve.tensor_tensor(w[1][:, s, :], raw[:, s, :], w[0][:, s, :].bitcast(F32), ALU.subtract).then_inc(low, 1)

                with dve.Fori(0, 2) as h:
                    for s in range(2):
                        rest(s, h, s)
                    dve.wait_ge(root, h + 1)
                    dve.reciprocal(ss[:, 2, :], ss[:, 1, :]).then_inc(inv, 1)
                    dve.wait_ge(inv, h + 1)
                    for k in range(KD + 1):
                        if k < KD:
                            dve.wait_ge(turned, KD * h + k + 1)
                            dve.tensor_tensor(sg[:, k % 2, :].rearrange("p (n q) -> p n q", n=NH), x[:, :, k * P:(k + 1) * P],
                                              ss[:, 2, :].unsqueeze(2).broadcast_to([P, NH, P]), ALU.mult).then_inc(staged, 1)
                        if k >= 1:
                            dve.wait_ge(full_done, KD * h + k + 2)
                            dve.tensor_copy(h_t[0][:, k - 1, :], y[:, (k - 1) % 2, :]).then_inc(h_high, 1)
                            dve.wait_ge(h_high, KD * h + k)
                            dve.tensor_tensor(h_t[1][:, k - 1, :], y[:, (k - 1) % 2, :], h_t[0][:, k - 1, :].bitcast(F32),
                                              ALU.subtract).then_inc(h_low, 1)
                    with dve.Fori(0, KF) as f:
                        rest(2 * f + 2, h, 0)
                        dve.wait_ge(h_low, KD * h + KD)
                        dve.wait_ge(silu, KF * h + f + 2)
                        dve.wait_ge(used, PIECES * h + 2 * f + 4)
                        dve.tensor_tensor(y[:, 0, :], sg[:, 0, :], pu, ALU.mult).then_inc(acted, 1)
                        dve.wait_ge(acted, KF * h + f + 2)
                        rest(2 * f + 3, h, 1)
                        dve.tensor_copy(a_t[0][:, ds(f, 1), :], y[:, 0:1, :]).then_inc(a_high, 1)
                        dve.wait_ge(a_high, KF * h + f + 1)
                        dve.tensor_tensor(a_t[1][:, ds(f, 1), :], y[:, 0:1, :], a_t[0][:, ds(f, 1), :].bitcast(F32),
                                          ALU.subtract).then_inc(a_low, 1)
                        dve.wait_ge(a_low, KF * h + f + 1)
                    for f in range(KF - 2):
                        rest(2 * KF + f + 2, h, f % 2)
                    for n in range(NH):
                        dve.wait_ge(rooted, NH * h + n + 1)
                        dve.reciprocal(ss[:, 5, n:n + 1], ss[:, 4, n:n + 1]).then_inc(inv2, 1)
                        dve.wait_ge(inv2, NH * h + n + 1)
                        dve.scalar_tensor_tensor(out=r[:, 0, :].rearrange("p (c n) -> p c n", c=2), in0=ps[:, n], scalar=ss[:, 5, n:n + 1],
                                                 in1=gr[:].rearrange("p (c n) -> p c n", c=2), op0=ALU.mult, op1=ALU.mult).then_inc(scaled, 1)
                        dve.wait_ge(scaled, NH * h + n + 2)
                        dve.tensor_tensor(x[:, n, :], x[:, n, :], r[:, 0, :], ALU.add).then_inc(added, 1)
                        dve.wait_ge(added, NH * h + n + 1)


def build(nc, a, out, stop=None):
    g = Program()
    with ExitStack() as ctx:
        g.sems = []

        def sb(name, shape, dt=F32):
            return ctx.enter_context(nc.sbuf_tensor(name, shape, dt))

        g.ident = sb("ident", [P, P])
        g.ones = sb("ones", [P, P])
        g.eps = sb("eps", [P, 1])
        g.vcol = sb("vcol", [P, 2, P])
        g.neg_lam = sb("neg_lam", [P, 1])
        g.mod = sb("mod", [P, 2, 16])
        g.mod2 = sb("mod2", [P, 2, 16])
        g.a_col = sb("a_col", [P, KD])
        g.b_col = sb("b_col", [P, KD])
        g.wt = sb("wt", [P, 2, NT])
        g.dest = sb("dest", [P, 2, NT], U32)
        g.blocks = sb("blocks", [1, MAX_BLOCKS + 1], U32)
        g.rows = sb("rows", [P, MAX_BLOCKS], U32)
        g.gate2 = sb("gate2", [P, 2, D])
        g.row_token = nc.dram_tensor("row_token", [MAX_BLOCKS * P, 1], F32, kind="Internal").ap()
        g.xn_dram = nc.dram_tensor("xn_rows", [T, D], F32, kind="Internal").ap()
        g.x_dram = nc.dram_tensor("x_rows", [T, D], F32, kind="Internal").ap()
        g.y_dram = nc.dram_tensor("y_rows", [Y_BLOCKS * P, D], F32, kind="Internal").ap()

        def pair(where, name, chunks):
            return [where.enter_context(nc.sbuf_tensor(f"{name}{j}", [P, chunks, T], F32R)) for j in range(2)]

        with ExitStack() as first:
            g.gate = first.enter_context(nc.sbuf_tensor("gate", [P, 2, D], F32))
            with ExitStack() as mixed:
                with ExitStack() as early:
                    g.cs = early.enter_context(nc.sbuf_tensor("cos_sin", [P, 2, T], F32, side="right"))
                    load_constants(nc, g, a)
                    modulation(nc, g, "m1_", a["c"], a["w_ada"], a["b_ada"], g.col["b_ada"], g.mod, g.gate)
                    modulation(nc, g, "m2_", a["c_2"], a["ada_w_2"], a["ada_b_2"], g.col["b_ada2"], g.mod2, g.gate2)
                    g.dmix = early.enter_context(nc.sbuf_tensor("dmix", [P, HEADS, T], F32, side="right"))
                    g.ht = early.enter_context(nc.sbuf_tensor("ht", [P, KD, T], F32, side="right"))
                    with nc.sbuf_tensor("x_in_rows", [P, NT, D], F32) as g.x:
                        norm_transposed(nc, g, "n1_", g.col["norm1_g"], g.mod[:, 0, :], out_t=g.ht, load=a["x"][0])
                    g.mix_a = pair(mixed, "mix_a", HEADS)
                    with ExitStack() as mla:
                        g.lat = mla.enter_context(nc.sbuf_tensor("lat", [P, 4, T], F32))
                        g.kpe = mla.enter_context(nc.sbuf_tensor("kpe", [ROPE, T], F32))
                        latents(nc, g, a)
                        attention(nc, g, a, "am_", False)
                    attention(nc, g, a, "ad_", True)
                    mix_b = pair(mixed, "mix_b", HEADS)
                    head_norm(nc, g, mix_b)
                    clear_sems(nc, g)
                x1 = ExitStack()
                g.x = x1.enter_context(nc.sbuf_tensor("x1_rows", [P, NT, D], F32, side="right"))
                project_rows(nc, g, "po_", lambda k: [x[:, k % HEADS, :] for x in (g.mix_a if k < HEADS else mix_b)],
                             a["w_out"][0], g.gate[:, 0, :], a["x"][0], g.x_dram, x_keep=g.x)
            with x1:
                g.ht = x1.enter_context(nc.sbuf_tensor("ht_moe", [P, KD, T], F32, side="right"))
                norm_transposed(nc, g, "n2_", g.col["norm2_g"], g.mod[:, 1, :], out_t=g.ht, keep=g.xn_dram)
                route(nc, g, a)
            clear_sems(nc, g)
            experts(nc, g, a)
            hidden = ExitStack()
            h_t = [hidden.enter_context(nc.sbuf_tensor(f"h2_{j}", [P, KD, T], F32R, side="right")) for j in range(2)]
            with nc.sbuf_tensor("x2_rows", [P, NT, D], F32) as g.x:
                combine(nc, g, a)
                norm_transposed(nc, g, "n3_", g.col["g0"], g.mod2[:, 0, :], split=h_t)
        with ExitStack() as conv:
            y_t = pair(conv, "y2_", KD)
            with hidden:
                short_conv(nc, g, a, h_t, y_t)
            project_rows(nc, g, "pc_", lambda k: [x[:, k, :] for x in y_t], a["conv_w_out_2"][0], g.gate2[:, 0, :],
                         g.x_dram, g.x_dram, gain=a["norm_gains_2"][0, 1])
        clear_sems(nc, g)
        feed_forward(nc, g, a, out)


def constants():
    half = ROPE // 2
    inv = np.float32(10000.0) ** (-np.arange(0, ROPE, 2, dtype=np.float32) / np.float32(ROPE))
    ang = inv.astype(np.float32)[:, None] * np.arange(T, dtype=np.float32)[None, :]
    cos, sin = np.cos(ang).astype(np.float32), np.sin(ang).astype(np.float32)
    rope = np.zeros((2, P, T), np.float32)
    for q in range(P // half):
        rope[0, q * half:(q + 1) * half] = cos
        rope[1, q * half:(q + 1) * half] = sin if q % 2 else -sin
    return {
        "const_rope": rope,
        "const_ident": np.eye(P, dtype=np.float32),
        "const_before": np.triu(np.ones((P, P), np.float32), 1),
        "const_iota": np.arange(MAX_BLOCKS, dtype=np.float32)[None, :],
        "const_token": np.arange(T, dtype=np.float32).reshape(NT, P).T.copy(),
    }


_INS = ["x", "c", "w_ada", "b_ada", "norm1_g", "w_in", "q_a_norm_g", "w_q_up", "kv_a_norm_g", "w_kv_up", "lambda_q1",
        "lambda_k1", "lambda_q2", "lambda_k2", "subln_g", "w_out", "norm2_g", "w_router_group", "b_router_group",
        "w_router_expert", "b_router_expert", "w_expert_gate", "w_expert_up", "w_expert_down", "final_norm_g",
        "c_2", "ada_w_2", "ada_b_2", "norm_gains_2", "conv_w_in_2", "conv_w_2", "conv_w_out_2",
        "ffn_w_gate_up_2", "ffn_w_down_2"]


def kernel(**inputs):
    import numpy as _np
    import concourse.bacc as _bacc
    from concourse import mybir as _mybir
    from concourse.bass_utils import run_bass_kernel_spmd as _run

    nc = _bacc.Bacc("TRN2", target_bir_lowering=False, num_devices=1)
    arrays, aps = {}, {}
    given = {name: _np.ascontiguousarray(inputs[name]) for name in _INS}
    given.update(constants())
    for name, value in given.items():
        arrays[f"in_{name}_dram"] = value
        aps[name] = nc.dram_tensor(f"in_{name}_dram", value.shape, _mybir.dt.from_np(value.dtype), kind="ExternalInput").ap()
    out = nc.dram_tensor("out_0_dram", (1, T, D), _mybir.dt.float32, kind="ExternalOutput").ap()
    build(nc, aps, out)
    r = _run(nc, [arrays], core_ids=[0])
    return r.results[0]["out_0_dram"]
```

```python
from contextlib import ExitStack

import numpy as np

import concourse.bass as bass
from concourse import mybir

ALU = mybir.AluOpType
ACT = mybir.ActivationFunctionType
F32 = mybir.dt.float32
F32R = mybir.dt.float32r
U32 = mybir.dt.uint32
AX_X = mybir.AxisListType.X
ds = bass.ds

P = 128
T = 1024
D = 1024
NT = T // P
KD = D // P
HALF = 512
EPS = 1e-6
QR, KVR, NOPE, ROPE, VD = 256, 256, 128, 64, 128
HEADS = 4
DQK = 64
QH = NOPE + ROPE
KVH = NOPE + VD
DQ0 = QR + KVR + ROPE
DK0 = DQ0 + HEADS * 2 * DQK
DV0 = DK0 + HEADS * 2 * DQK
GROUPS, PER_GROUP = 4, 8
EXPERTS = GROUPS * PER_GROUP
FE = 512
KE = FE // P
Y_BLOCKS = 50
MIN_BLOCKS = 2 * T // P
MAX_BLOCKS = 48
FF = 2816
KF = FF // P
LAMBDA_INIT = 0.2
BIG = 3.0e38


class Program:
    pass


def sems(nc, g, names):
    made = [nc.alloc_semaphore(n) for n in names.split()]
    g.sems += made
    return made


def clear_sems(nc, g):
    nc.clear_and_free_semaphores(g.sems)
    nc.all_engine_barrier()
    g.sems = []


def load_constants(nc, g, a):
    rows = [[("norm1_g", a["norm1_g"], 8), ("norm2_g", a["norm2_g"], 8), ("q_g", a["q_a_norm_g"], 2),
             ("kv_g", a["kv_a_norm_g"], 2), ("sub_g", a["subln_g"], 1),
             ("g0", a["norm_gains_2"][0, 0:1, :], 8), ("g2", a["norm_gains_2"][0, 2:3, :], 8)],
            [("conv_w", a["conv_w_2"][0, :, :], 24)]]
    with ExitStack() as ctx:
        const_in, rows_in, lam_in, rows_clear, turned, vec_ready, prod, lam_sum, lam_exp, ones_ready = sems(nc, g, "const_in rows_in lam_in rows_clear turned vec_ready prod lam_sum lam_exp ones_ready")
        vrow = ctx.enter_context(nc.sbuf_tensor("vrow", [P, 2, P], F32))
        lamv = ctx.enter_context(nc.sbuf_tensor("lamv", [P, 4, DQK], F32))
        lamp = ctx.enter_context(nc.sbuf_tensor("lamp", [P, 2, DQK], F32))
        lams = ctx.enter_context(nc.sbuf_tensor("lams", [P, 2], F32))
        lame = ctx.enter_context(nc.sbuf_tensor("lame", [P, 2], F32))
        pv = ctx.enter_context(nc.psum_tensor("pv", [P, 2, P], F32))
        g.col = {}
        n_rows = 0
        with nc.Block() as block:

            @block.sync
            def _(sp):
                nonlocal n_rows
                sp.dma_start(g.ident[:], a["const_ident"]).then_inc(const_in, 16)
                sp.dma_start(g.cs[:], a["const_rope"].rearrange("s p t -> p s t")).then_inc(const_in, 16)
                sp.wait_ge(rows_clear, 1)
                for j, group in enumerate(rows):
                    at = 0
                    for name, src, n in group:
                        pat = "a (r q) -> (a r) q"
                        sp.dma_start(vrow[at:at + n, j, :], src.rearrange(pat, q=P)).then_inc(rows_in, 16)
                        g.col[name] = g.vcol[:, j, at:at + n]
                        at += n
                        n_rows += 1

            @block.scalar
            def _(act):
                for i, name in enumerate(("lambda_q1", "lambda_k1", "lambda_q2", "lambda_k2")):
                    act.dma_start(lamv[:, i, :], a[name][0].partition_broadcast(P)).then_inc(lam_in, 16)
                act.wait_ge(lam_sum, 2)
                act.activation(lame[:], lams[:], ACT.Exp).then_inc(lam_exp, 1)

            @block.tensor
            def _(pe):
                pe.wait_ge(const_in, 32)
                pe.wait_ge(rows_in, 16 * sum(len(r) for r in rows))
                for j in range(2):
                    pe.transpose(pv[:, j, :], vrow[:, j, :], g.ident[:]).then_inc(turned, 1)

            @block.vector
            def _(dve):
                dve.memset(vrow[:], 0.0).then_inc(rows_clear, 1)
                dve.memset(g.ones[:], 1.0).then_inc(ones_ready, 1)
                dve.memset(g.eps[:], EPS).then_inc(ones_ready, 1)
                dve.wait_ge(lam_in, 64)
                for i in range(2):
                    dve.tensor_tensor(lamp[:, i, :], lamv[:, 2 * i, :], lamv[:, 2 * i + 1, :], ALU.mult).then_inc(prod, 1)
                dve.wait_ge(prod, 2)
                for i in range(2):
                    dve.tensor_reduce(lams[:, i:i + 1], lamp[:, i, :], AX_X, ALU.add).then_inc(lam_sum, 1)
                dve.wait_ge(lam_exp, 1)
                dve.scalar_tensor_tensor(out=g.neg_lam[:], in0=lame[:, 1:2], scalar=-LAMBDA_INIT,
                                         in1=lame[:, 0:1], op0=ALU.add, op1=ALU.subtract).then_inc(lam_sum, 1)
                dve.wait_ge(turned, 2)
                dve.tensor_copy(g.vcol[:], pv[:]).then_inc(vec_ready, 1)


def sum_columns(pe, out, acc, ones):
    for j in range(KD):
        o = pe.matmul(out[:, j:j + 1], acc[:, j * P:(j + 1) * P], ones[:, 0:1], start=True, stop=True)
    return o


def sum_rows(pe, out, acc, ones):
    for h in range(2):
        cols = slice(h * HALF, (h + 1) * HALF)
        o = pe.matmul(out[:, cols], ones[:], acc[:, cols], start=True, stop=True)
    return o


def first_modulation(nc, g, a):
    with ExitStack() as ctx:
        x_in0, x_in1, x_in2, x_in3, sq, c_in, bias_in, c_ready, sec_in0, sec_in1, sec_in2, sec_in3, part, summed, col_ps, col_out = sems(
            nc, g, "m_x_in0 m_x_in1 m_x_in2 m_x_in3 m_sq m_c_in m_bias_in m_c_ready m_sec_in0 m_sec_in1 m_sec_in2 m_sec_in3 m_part m_summed m_col_ps m_col_out")
        sec_in, x_in = (sec_in0, sec_in1, sec_in2, sec_in3), (x_in0, x_in1, x_in2, x_in3)
        ct = ctx.enter_context(nc.sbuf_tensor("m_ct", [P, 2, KD], F32))
        sec = ctx.enter_context(nc.sbuf_tensor("m_sec", [P, 2, KD, D], F32))
        bias, acc = g.dmix[0:1, 0:2, :], g.dmix[:, 2:4, :]
        junk = ctx.enter_context(nc.sbuf_tensor("m_junk", [P, D], F32))
        pcol = ctx.enter_context(nc.psum_tensor("m_pcol", [P, 2 * KD], F32))
        w_v = a["w_ada"][0].rearrange("(p k) n -> p k n", k=KD)
        with nc.Block() as block:

            @block.sync
            def _(sp):
                for i, c in enumerate((a["c"], a["c_2"])):
                    sp.dma_start(ct[:, i, :], c[0].rearrange("(p k) -> p k", k=KD)).then_inc(c_in, 16)
                for q in range(4):
                    s, k = q // 2, q % 2 * (KD // 2)
                    sp.dma_start(sec[:, s, k:k + KD // 2, :], w_v[:, k:k + KD // 2, s * D:(s + 1) * D]).then_inc(sec_in[q], 16)
                sp.dma_start(bias, a["b_ada"][0:1, 0:2 * D].rearrange("a (s n) -> a s n", s=2)).then_inc(bias_in, 16)
                x_v = a["x"][0].rearrange("(n p) d -> p n d", p=P)
                for q in range(4):
                    sp.dma_start(g.x[:, 2 * q:2 * q + 2, :], x_v[:, 2 * q:2 * q + 2, :]).then_inc(x_in[q], 16)

            @block.scalar
            def _(act):
                act.wait_ge(c_in, 32)
                act.activation(g.cond[:], ct[:], ACT.Silu).then_inc(c_ready, 1)
                for n in range(NT):
                    act.wait_ge(x_in[n // 2], 16)
                    if n:
                        act.wait_ge(sq, n)
                    act.activation(junk[:], g.x[:, n, :], ACT.Square, accum_out=g.ss[:, n:n + 1]).then_inc(sq, 1)
                act.wait_ge(col_ps, 1)
                act.activation(g.mod[:, 0, :], pcol[:], ACT.Copy).then_inc(col_out, 1)

            @block.vector
            def _(dve):
                dve.wait_ge(c_ready, 1)
                for s in range(2):
                    for k in range(KD):
                        if k % (KD // 2) == 0:
                            dve.wait_ge(sec_in[2 * s + k // (KD // 2)], 16)
                        if k == 0:
                            dve.tensor_scalar(acc[:, s, :], sec[:, s, k, :], g.cond[:, 0, 0:1], None, ALU.mult).then_inc(part, 1)
                        else:
                            dve.wait_ge(part, KD * s + k)
                            dve.scalar_tensor_tensor(out=acc[:, s, :], in0=sec[:, s, k, :], scalar=g.cond[:, 0, k:k + 1],
                                                     in1=acc[:, s, :], op0=ALU.mult, op1=ALU.add).then_inc(part, 1)
                    dve.wait_ge(part, KD * (s + 1))
                    if s == 0:
                        dve.wait_ge(bias_in, 16)
                    dve.tensor_tensor(acc[0:1, s, :], acc[0:1, s, :], bias[:, s, :], ALU.add).then_inc(summed, 1)

            @block.tensor
            def _(pe):
                for s in range(2):
                    pe.wait_ge(summed, s + 1)
                    o = sum_columns(pe, pcol[:, s * KD:(s + 1) * KD], acc[:, s, :], g.ones)
                o.then_inc(col_ps, 1)


def partial_modulation(nc, g, block, ctx, tag, w, b, cond, first, count, at, spare=()):
    part_in0, part_in1, part_in2, part_in3, bias_in, part, scaled, seen, biased, acc_out = sems(
        nc, g, " ".join(tag + s for s in "part_in0 part_in1 part_in2 part_in3 bias_in part scaled seen biased acc_out".split()))
    part_in = (part_in0, part_in1, part_in2, part_in3)
    ring = 4 if spare else 2
    rows = [ctx.enter_context(nc.sbuf_tensor(tag + f"mrows{q}", [P, D], F32))[:] for q in range(ring - len(spare))] + list(spare)
    acc = ctx.enter_context(nc.sbuf_tensor(tag + "macc", [P, 2, D], F32))
    bias = ctx.enter_context(nc.sbuf_tensor(tag + "mbias", [1, D], F32))
    w_v = w[0].rearrange("(p k) n -> p k n", k=KD)

    @block.gpsimd
    def _(pool):
        def load(i, k):
            pool.dma_start(rows[k % ring], w_v[:, k, ds((i + first) * D, D)]).then_inc(part_in[k % ring], 16)

        def section(i, first_one=False, last=False):
            pool.dma_start(bias[:], b[0:1, ds((i + first) * D, D)]).then_inc(bias_in, 16)
            for k in range(KD):
                pool.wait_ge(part_in[k % ring], (KD // ring) * 16 * i + 16 * (k // ring + 1))
                pool.sem_inc(seen, 1)
                to = acc[:, 0, :] if k == 0 else rows[k % ring]
                pool.tensor_scalar(to, rows[k % ring], cond[:, k:k + 1], None, ALU.mult).then_inc(scaled if k else part, 1)
                if k >= 1:
                    pool.wait_ge(scaled, (KD - 1) * i + k)
                    if k == 1 and not first_one:
                        pool.wait_ge(acc_out, 16 * i)
                    pool.tensor_tensor(acc[:, k % 2, :], rows[k % ring], acc[:, 1 - k % 2, :], ALU.add).then_inc(part, 1)
                pool.wait_ge(part, KD * i + k + 1)
                pool.sem_inc(seen, 1)
                if k + ring < KD:
                    load(i, k + ring)
                elif not last:
                    load(i + 1, k + ring - KD)
            pool.wait_ge(bias_in, 16 * i + 16)
            pool.tensor_tensor(acc[0:1, 1, :], acc[0:1, 1, :], bias[:], ALU.add).then_inc(biased, 1)
            pool.wait_ge(biased, i + 1)
            pool.sem_inc(seen, 1)
            pool.dma_start(g.acc_dram[ds(i + at, 1)].squeeze(0), acc[:, 1, :]).then_inc(acc_out, 16)

        for k in range(ring):
            load(0, k)
        section(0, first_one=True)
        with pool.Fori(1, count - 1) as i:
            section(i)
        section(count - 1, last=True)
        pool.wait_ge(acc_out, 16 * count)


def three_passes(pe, out, stat, mov, start, stop):
    for n, (i, j) in enumerate(((0, 0), (1, 0), (0, 1))):
        o = pe.matmul(out, stat[i], mov[j], start=start and n == 0, stop=stop and n == 2)
    return o


def norm_transposed(nc, g, tag, gain, mod, out_t=None, split=None, keep=None, ahead=None):
    with ExitStack() as ctx:
        root, rstd_ready, ab, staged, turned, turned_free, row_ready, row_out0, row_out1, high, low = sems(
            nc, g, " ".join(tag + s for s in "root rstd_ready ab staged turned turned_free row_ready row_out0 row_out1 high low".split()))
        row_out = (row_out0, row_out1)
        rs = ctx.enter_context(nc.sbuf_tensor(tag + "rs", [P, NT], F32))
        rstd = ctx.enter_context(nc.sbuf_tensor(tag + "rstd", [P, NT], F32))
        stage = ctx.enter_context(nc.sbuf_tensor(tag + "stage", [P, 2, NT, P], F32))
        rows = ctx.enter_context(nc.sbuf_tensor(tag + "rows", [P, 2, D], F32)) if keep is not None else None
        full = ctx.enter_context(nc.sbuf_tensor(tag + "full", [P, 2, T], F32)) if split is not None else None
        pt = ctx.enter_context(nc.psum_tensor(tag + "pt", [P, 2, T], F32))
        with nc.Block() as block:

            @block.scalar
            def _(act):
                act.activation(rs[:], g.ss[:], ACT.Sqrt, bias=g.eps[:], scale=1.0 / D).then_inc(root, 1)
                act.wait_ge(ab, 1)
                act.sem_inc(turned_free, 2)
                with act.Fori(0, KD // 2) as i:
                    for b in range(2):
                        act.wait_ge(turned, 2 * i + b + 3)
                        if split is not None:
                            act.wait_ge(low, 2 * i + b + 1)
                        to = full[:, b:b + 1, :] if split is not None else out_t[:, ds(2 * i + b, 1), :]
                        act.activation(to, pt[:, b:b + 1, :], ACT.Identity,
                                       bias=g.b_col[:, ds(2 * i + b, 1)], scale=g.a_col[:, ds(2 * i + b, 1)]).then_inc(turned_free, 1)

            @block.vector
            def _(dve):
                dve.scalar_tensor_tensor(out=g.a_col[:], in0=mod[:, 8:16], scalar=1.0, in1=gain, op0=ALU.add, op1=ALU.mult)
                dve.tensor_copy(g.b_col[:], mod[:, 0:8]).then_inc(ab, 1)
                dve.wait_ge(root, 1)
                dve.reciprocal(rstd[:], rs[:]).then_inc(rstd_ready, 1)
                dve.wait_ge(rstd_ready, 1)
                dve.sem_inc(low, 2)

                def scale_chunk(k, b):
                    dve.wait_ge(turned, k + 1)
                    dve.tensor_tensor(stage[:, b, :, :], g.x[:, :, ds(k * P, P)],
                                      rstd[:].unsqueeze(2).broadcast_to([P, NT, P]), ALU.mult).then_inc(staged, 1)

                def split_chunk(k, b):
                    dve.wait_ge(turned_free, k + 3)
                    dve.tensor_copy(split[0][:, ds(k, 1), :], full[:, b:b + 1, :]).then_inc(high, 1)
                    dve.wait_ge(high, k + 1)
                    dve.tensor_tensor(split[1][:, ds(k, 1), :], full[:, b:b + 1, :], split[0][:, ds(k, 1), :].bitcast(F32),
                                      ALU.subtract).then_inc(low, 1)

                if split is None:
                    with dve.Fori(0, KD // 2) as i:
                        for b in range(2):
                            scale_chunk(2 * i + b, b)
                else:
                    scale_chunk(0, 0)
                    scale_chunk(1, 1)
                    with dve.Fori(1, KD // 2) as i:
                        for b in range(2):
                            scale_chunk(2 * i + b, b)
                            split_chunk(2 * i + b - 2, b)
                    split_chunk(KD - 2, 0)
                    split_chunk(KD - 1, 1)
                if keep is not None:
                    for n in range(NT):
                        if n >= 2:
                            dve.wait_ge(row_out[n % 2], 16 * (n // 2))
                        dve.tensor_scalar(rows[:, n % 2, :], g.x[:, n, :], rstd[:, n:n + 1], None, ALU.mult).then_inc(row_ready, 1)

            @block.tensor
            def _(pe):
                pe.sem_inc(turned, 2)
                with pe.Fori(0, KD // 2) as i:
                    for b in range(2):
                        pe.wait_ge(staged, 2 * i + b + 1)
                        pe.wait_ge(turned_free, 2 * i + b + 1)
                        for n in range(NT):
                            o = pe.transpose(pt[:, b, n * P:(n + 1) * P], stage[:, b, n, :], g.ident[:])
                        o.then_inc(turned, 1)

            if keep is not None or ahead is not None:
                @block.sync
                def _(sp):
                    if ahead is not None:
                        ahead(sp)
                    if keep is not None:
                        for n in range(NT):
                            sp.wait_ge(row_ready, n + 1)
                            sp.dma_start(keep[n * P:(n + 1) * P, :], rows[:, n % 2, :]).then_inc(row_out[n % 2], 16)
                        for b in range(2):
                            sp.wait_ge(row_out[b], 8 * NT)


def rope_rotate(dve, out, ps, g, tmp, rows, step, k0):
    dve.tensor_tensor(tmp[0:rows, 0, :], ps[0:rows, :], g.cs[0:rows, 0, :], ALU.mult)
    for q in range(rows // 32):
        o = dve.tensor_tensor(tmp[32 * q:32 * q + 32, 1, :], ps[32 * (q ^ 1):32 * (q ^ 1) + 32, :],
                              g.cs[32 * q:32 * q + 32, 1, :], ALU.mult)
    o.then_inc(step, 1)
    dve.wait_ge(step, k0 + 1)
    return dve.tensor_tensor(out, tmp[0:rows, 0, :], tmp[0:rows, 1, :], ALU.add)


def latents(nc, g, a, w, w_in, ahead):
    with ExitStack() as ctx:
        kpe_high, proj, raw, squared, ssq, rooted, recip_r, lat_done, ps_free, rope_step = sems(nc, g, "l_kpe_high l_proj l_raw l_squared l_ssq l_rooted l_recip l_done l_ps_free l_rope")
        raws = ctx.enter_context(nc.sbuf_tensor("l_raw", [P, 4, T], F32))
        sqs = g.dmix
        root = ctx.enter_context(nc.sbuf_tensor("l_root", [P, 2, T], F32))
        rinv = ctx.enter_context(nc.sbuf_tensor("l_rinv", [P, 2, T], F32))
        kpe = root[0:ROPE, 0, :]
        tmp = ctx.enter_context(nc.sbuf_tensor("l_tmp", [P, 2, T], F32))
        ps = ctx.enter_context(nc.psum_tensor("l_ps", [P, 2, T], F32))
        pss = ctx.enter_context(nc.psum_tensor("l_pss", [P, 2, T], F32))
        with nc.Block() as block:

            @block.sync
            def _(sp):
                ahead(sp)

            @block.tensor
            def _(pe):
                pe.wait_ge(w_in, 16)
                def sum_squares(j):
                    pe.wait_ge(squared, 2 * j + 2)
                    for h in range(2):
                        for c in range(2):
                            o = pe.matmul(pss[:, j, h * HALF:(h + 1) * HALF], g.ones[:], sqs[:, 2 * j + c, h * HALF:(h + 1) * HALF],
                                          start=(c == 0), stop=(c == 1))
                    o.then_inc(ssq, 1)

                for c in range(5):
                    m = P if c < 4 else ROPE
                    if c >= 2:
                        pe.wait_ge(ps_free, c - 1)
                    for h in range(2):
                        for k in range(KD):
                            o = pe.matmul(ps[0:m, c % 2, h * HALF:(h + 1) * HALF], w[:, k, c * P:c * P + m],
                                          g.ht[:, k, h * HALF:(h + 1) * HALF], start=(k == 0), stop=(k == KD - 1))
                        if h == 0 and c % 2 == 0 and c >= 2:
                            sum_squares(c // 2 - 1)
                    o.then_inc(proj, 1)

            @block.scalar
            def _(act):
                for c in range(4):
                    act.wait_ge(proj, c + 1)
                    act.activation(raws[:, c, :], ps[:, c % 2, :], ACT.Copy).then_inc(raw, 1)
                    act.wait_ge(raw, c + 1)
                    act.sem_inc(ps_free, 1)
                    act.activation(sqs[:, c, :], raws[:, c, :], ACT.Square).then_inc(squared, 1)
                    if c == 2:
                        act.wait_ge(ssq, 1)
                        act.activation(root[:, 0, :], pss[:, 0, :], ACT.Sqrt, bias=g.eps[:], scale=1.0 / QR).then_inc(rooted, 1)
                act.wait_ge(ssq, 2)
                act.activation(root[:, 1, :], pss[:, 1, :], ACT.Sqrt, bias=g.eps[:], scale=1.0 / QR).then_inc(rooted, 1)

            @block.vector
            def _(dve):
                for j, gain in enumerate(("q_g", "kv_g")):
                    dve.wait_ge(rooted, j + 1)
                    dve.reciprocal(rinv[:, j, :], root[:, j, :]).then_inc(recip_r, 1)
                    dve.wait_ge(recip_r, j + 1)
                    for c in range(2):
                        dve.scalar_tensor_tensor(out=g.lat[:, 2 * j + c, :], in0=raws[:, 2 * j + c, :], scalar=g.col[gain][:, c:c + 1],
                                                 in1=rinv[:, j, :], op0=ALU.mult, op1=ALU.mult).then_inc(lat_done, 1)
                dve.wait_ge(proj, 5)
                rope_rotate(dve, kpe, ps[:, 0, :], g, tmp, ROPE, rope_step, 0).then_inc(lat_done, 1)
                dve.wait_ge(lat_done, 5)
                for p in range(2):
                    dve.tensor_copy(g.kpe[0][p * ROPE:(p + 1) * ROPE, :], kpe).then_inc(kpe_high, 1)
                dve.wait_ge(kpe_high, 2)
                for p in range(2):
                    dve.tensor_tensor(g.kpe[1][p * ROPE:(p + 1) * ROPE, :], kpe, g.kpe[0][0:ROPE, :].bitcast(F32), ALU.subtract).then_inc(lat_done, 1)


def load_head(sp, a, w, w_in, diff, h):
    if diff:
        win = a["w_in"][0].rearrange("(k p) n -> p k n", p=P)
        for j, c0 in enumerate((DQ0, DK0, DV0)):
            sp.dma_start(w[:, :, j * P:(j + 1) * P], win[:, :, ds(c0 + h * P, P)]).then_inc(w_in, 16)
    else:
        wq = a["w_q_up"][0].rearrange("(k p) n -> p k n", p=P)
        wkv = a["w_kv_up"][0].rearrange("(k p) n -> p k n", p=P)
        sp.dma_start(w[:, :, 0:QH], wq[:, :, ds(h * QH, QH)]).then_inc(w_in, 16)
        sp.dma_start(w[:, :, QH:], wkv[:, :, ds(h * KVH, KVH)]).then_inc(w_in, 16)


def attention(nc, g, a, tag, diff, w, w_in, beside, ahead=None, staged=None):
    maps = 2 if diff else 1
    scale = float(DQK if diff else QH) ** -0.5
    kin = KD if diff else QR // P
    uses = (2 + NT, 1 + NT) if diff else (2 + NT // 2, 2 + NT // 2)
    n_proj = 3 if diff else 4
    with ExitStack() as ctx:
        names = ("w_used proj q_ready qpe_ready k_ready v_ready rope_step free0 free1 scored maxed nmax expd sumr "
                 "probs turned copied pv mixed t_free combined p_free leading cleared zeroed q_high k_high qpe_high turned_q w_copied")
        (w_used, proj, q_ready, qpe_ready, k_ready, v_ready, rope_step, free0, free1, scored, maxed, nmax, expd, sumr,
         probs, turned, copied, pv, mixed, t_free, combined, p_free, leading, cleared, zeroed,
         q_high, k_high, qpe_high, turned_q, w_copied) = sems(nc, g, " ".join(tag + s for s in names.split()))
        free = (free0, free1)

        def sb(name, shape):
            return ctx.enter_context(nc.sbuf_tensor(tag + name, shape, F32))

        if diff:
            qt, kt = sb("qt", [P, T]), sb("kt", [P, T])
        else:
            qt = [ctx.enter_context(nc.sbuf_tensor(tag + f"qt{j}", [P, T], F32R)) for j in range(2)]
            kt = [ctx.enter_context(nc.sbuf_tensor(tag + f"kt{j}", [P, T], F32R)) for j in range(2)]
            qpe = ctx.enter_context(nc.sbuf_tensor(tag + "qpe", [P, T], F32R))
        v = sb("v", [P, NT, P])
        e = sb("e", [P, 2, maps, T])
        pr = sb("pr", [P, 2, T]) if diff else None
        tmp = pr if diff else e[:, :, 0, :]
        pt = sb("pt", [P, NT, HALF])
        mx = sb("mx", [P, 2, maps])
        nm = sb("nm", [P, 2, maps])
        sm = sb("sm", [P, 2, maps])
        ri = sb("ri", [P, 2, maps])
        r2 = sb("r2", [P, 2])
        zrow = sb("zrow", [P, D // 4]) if not diff else None
        ps = [ctx.enter_context(nc.psum_tensor(tag + f"ps{i}", [P, T], F32)) for i in range(2)]
        ptr = ctx.enter_context(nc.psum_tensor(tag + "ptr", [P, NT, P], F32))
        po = ctx.enter_context(nc.psum_tensor(tag + "po", [P, HALF], F32))

        def slot(i, m):
            return (m, i + 2 - m) if diff else (i % 2, 2 + i // 2)

        n_w = 3 if diff else 2

        with nc.Block() as block:
            partial_modulation(nc, g, block, ctx, tag, *beside)

            @block.sync
            def _(sp):
                if ahead is not None:
                    ahead(sp)
                with sp.Fori(1, HEADS) as h:
                    sp.wait_ge(w_used, h + 1)
                    load_head(sp, a, w, w_in, diff, h)
                if not diff:
                    sp.wait_ge(zeroed, 64)

            @block.tensor
            def _(pe):
                pe.sem_inc(free0, 1)
                pe.sem_inc(free1, 1)
                pe.sem_inc(w_used, 1)
                pe.sem_inc(pv, 1)
                if staged is not None:
                    pe.wait_ge(w_copied, 1)
                with pe.Fori(0, HEADS) as h:
                    pe.wait_ge(w_in, 16 * n_w * (h + 1))

                    def project(buf, use, c0, m, src, c_src):
                        pe.wait_ge(free[buf], uses[buf] * h + use + 1)
                        for hf in range(2):
                            for k in range(kin):
                                o = pe.matmul(ps[buf][0:m, hf * HALF:(hf + 1) * HALF], w[:, k, c0:c0 + m],
                                              src[:, c_src + k, hf * HALF:(hf + 1) * HALF], start=(k == 0), stop=(k == kin - 1))
                        o.then_inc(proj, 1)

                    def values(buf, use, c0, src, c_src):
                        pe.wait_ge(free[buf], uses[buf] * h + use + 1)
                        for n in range(NT):
                            for k in range(kin):
                                o = pe.matmul(ps[buf][:, n * P:(n + 1) * P], src[:, c_src + k, n * P:(n + 1) * P],
                                              w[:, k, c0:c0 + P], start=(k == 0), stop=(k == kin - 1))
                        o.then_inc(proj, 1)

                    if diff:
                        project(0, 0, 0, P, g.ht, 0)
                        project(1, 0, P, P, g.ht, 0)
                        values(0, 1, 2 * P, g.ht, 0)
                    else:
                        project(0, 0, NOPE, ROPE, g.lat, 0)
                        project(1, 0, 0, NOPE, g.lat, 0)
                        project(0, 1, QH, NOPE, g.lat, 2)
                        values(1, 1, QH + NOPE, g.lat, 2)
                    pe.wait_ge(proj, n_proj * (h + 1))
                    pe.sem_inc(w_used, 1)
                    pe.wait_ge(q_ready, h + 1)
                    if not diff:
                        pe.wait_ge(qpe_ready, h + 1)
                    pe.wait_ge(k_ready, h + 1)

                    def scores(i):
                        for m in range(maps):
                            buf, use = slot(i, m)
                            pe.wait_ge(free[buf], uses[buf] * h + use + 1)
                            lo = m * DQK
                            hi = lo + DQK if diff else P
                            for hf in range(2):
                                cols = slice(hf * HALF, (hf + 1) * HALF)
                                if diff:
                                    o = pe.matmul(ps[buf][:, cols], qt[lo:hi, i * P:(i + 1) * P], kt[lo:hi, cols], start=True, stop=True)
                                    continue
                                three_passes(pe, ps[buf][:, cols], [x[:, i * P:(i + 1) * P] for x in qt], [x[:, cols] for x in kt], True, False)
                                for j in range(2):
                                    o = pe.matmul(ps[buf][:, cols], qpe[:, i * P:(i + 1) * P], g.kpe[j][:, cols], start=False, stop=(j == 1))
                            o.then_inc(scored, 1)

                    def turn(i):
                        pe.wait_ge(probs, NT * h + i + 1)
                        pe.wait_ge(t_free, NT * h + i + 1)
                        src = pr[:, i % 2, :] if diff else e[:, i % 2, 0, :]
                        for n in range(NT):
                            o = pe.transpose(ptr[:, n, :], src[:, n * P:(n + 1) * P], g.ident[:])
                        o.then_inc(turned, 1)

                    def weigh(j):
                        pe.wait_ge(copied, NT * h + 4 * j + 4)
                        pe.wait_ge(v_ready, h + 1)
                        pe.wait_ge(mixed, 2 * h + j + 1)
                        for n in range(NT):
                            o = pe.matmul(po[:], v[:, n, :], pt[:, n, :], start=(n == 0), stop=(n == NT - 1))
                        o.then_inc(pv, 1)

                    for i in range(NT + 1):
                        if i < NT:
                            scores(i)
                        if i >= 1:
                            turn(i - 1)
                        if i == 5:
                            weigh(0)
                    weigh(1)

            @block.scalar
            def _(act):
                if staged is not None:
                    act.wait_ge(w_in, 16 * n_w)
                    act.activation(w[:], staged, ACT.Copy).then_inc(w_copied, 1)
                act.sem_inc(t_free, 1)
                if not diff:
                    act.wait_ge(cleared, 1)
                    act.wait_ge(w_in, 16 * n_w)
                    for q in range(4):
                        act.dma_start(g.y_dram.rearrange("(n p) (c q) -> c p n q", p=P, c=4)[q, :, MIN_BLOCKS:],
                                      zrow[:].unsqueeze(1).broadcast_to([P, Y_BLOCKS - MIN_BLOCKS, D // 4])).then_inc(zeroed, 16)
                with act.Fori(0, HEADS) as h:
                    if diff:
                        act.wait_ge(proj, 3 * h + 3)
                        act.wait_ge(pv, 2 * h + 1)
                        act.activation(v[:].rearrange("p n d -> p (n d)"), ps[0][:], ACT.Copy).then_inc(v_ready, 1)
                        act.wait_ge(v_ready, h + 1)
                        act.sem_inc(free0, 1)
                    else:
                        act.wait_ge(proj, 4 * h + 2)
                        act.activation(qt[0][:], ps[1][:], ACT.Copy).then_inc(q_high, 1)
                        act.wait_ge(q_ready, h + 1)
                        act.sem_inc(free1, 1)
                        act.wait_ge(proj, 4 * h + 3)
                        act.activation(kt[0][:], ps[0][:], ACT.Copy).then_inc(k_high, 1)
                        act.wait_ge(k_ready, h + 1)
                        act.sem_inc(free0, 1)
                        act.wait_ge(proj, 4 * h + 4)
                        act.wait_ge(pv, 2 * h + 1)
                        act.activation(v[:].rearrange("p n d -> p (n d)"), ps[1][:], ACT.Copy).then_inc(v_ready, 1)
                        act.wait_ge(v_ready, h + 1)
                        act.sem_inc(free1, 1)

                    def copy_turned(i):
                        act.wait_ge(turned, NT * h + i + 1)
                        if i % 4 == 0:
                            act.wait_ge(pv, 2 * h + i // 4 + 1)
                        act.activation(pt[:, :, (i % 4) * P:(i % 4 + 1) * P], ptr[:], ACT.Copy).then_inc(copied, 1)
                        act.wait_ge(copied, NT * h + i + 1)
                        act.sem_inc(t_free, 1)

                    for i in range(NT):
                        for m in range(maps):
                            buf, use = slot(i, m)
                            act.wait_ge(nmax, maps * (NT * h + i) + m + 1)
                            if m == 0:
                                act.wait_ge(p_free, NT * h + i + 1)
                            act.activation(e[:, i % 2, m, :], ps[buf][:], ACT.Exp, bias=nm[:, i % 2, m:m + 1], scale=scale,
                                           accum_out=sm[:, i % 2, m:m + 1]).then_inc(expd, 1)
                            act.wait_ge(expd, maps * (NT * h + i) + m + 1)
                            act.sem_inc(free[buf], 1)
                        if i >= 1:
                            copy_turned(i - 1)
                    copy_turned(NT - 1)

            @block.vector
            def _(dve):
                if not diff:
                    dve.memset(zrow[:], 0.0).then_inc(cleared, 1)
                dve.sem_inc(p_free, 2)
                dve.sem_inc(mixed, 1)
                with dve.Fori(0, HEADS) as h:
                    if diff:
                        dve.wait_ge(proj, 3 * h + 1)
                        rope_rotate(dve, qt[:], ps[0], g, tmp, P, rope_step, 2 * h).then_inc(q_ready, 1)
                        dve.wait_ge(q_ready, h + 1)
                        dve.sem_inc(free0, 1)
                        dve.wait_ge(proj, 3 * h + 2)
                        rope_rotate(dve, kt[:], ps[1], g, tmp, P, rope_step, 2 * h + 1).then_inc(k_ready, 1)
                        dve.wait_ge(k_ready, h + 1)
                        dve.sem_inc(free1, 1)
                    else:
                        dve.wait_ge(proj, 4 * h + 1)
                        qpf = tmp[0:ROPE, 0, :]
                        rope_rotate(dve, qpf, ps[0], g, tmp, ROPE, rope_step, h).then_inc(turned_q, 1)
                        dve.sem_inc(free0, 1)
                        dve.wait_ge(q_high, h + 1)
                        dve.tensor_tensor(qt[1][:], ps[1][:], qt[0][:].bitcast(F32), ALU.subtract).then_inc(q_ready, 1)
                        dve.wait_ge(turned_q, h + 1)
                        dve.tensor_copy(qpe[0:ROPE, :], qpf).then_inc(qpe_high, 1)
                        dve.wait_ge(qpe_high, h + 1)
                        dve.tensor_tensor(qpe[ROPE:, :], qpf, qpe[0:ROPE, :].bitcast(F32), ALU.subtract).then_inc(qpe_ready, 1)
                        dve.wait_ge(k_high, h + 1)
                        dve.tensor_tensor(kt[1][:], ps[0][:], kt[0][:].bitcast(F32), ALU.subtract).then_inc(k_ready, 1)

                    def find_max(i):
                        for m in range(maps):
                            n = maps * (NT * h + i) + m
                            dve.wait_ge(scored, n + 1)
                            dve.tensor_reduce(mx[:, i % 2, m:m + 1], ps[slot(i, m)[0]][:], AX_X, ALU.max).then_inc(maxed, 1)
                            dve.wait_ge(maxed, n + 1)
                            dve.tensor_scalar(nm[:, i % 2, m:m + 1], mx[:, i % 2, m:m + 1], -scale, None, ALU.mult).then_inc(nmax, 1)

                    def finish(i):
                        b = i % 2
                        dve.wait_ge(expd, maps * (NT * h + i + 1))
                        dve.reciprocal(ri[:, b, :], sm[:, b, :]).then_inc(sumr, 1)
                        if not diff:
                            dve.wait_ge(sumr, NT * h + i + 1)
                            dve.tensor_scalar(e[:, b, 0, :], e[:, b, 0, :], ri[:, b, 0:1], None, ALU.mult).then_inc(probs, 1)
                            return
                        dve.wait_ge(sumr, 2 * (NT * h + i) + 1)
                        dve.tensor_scalar(r2[:, b:b + 1], ri[:, b, 1:2], g.neg_lam[:], None, ALU.mult).then_inc(sumr, 1)
                        dve.wait_ge(sumr, 2 * (NT * h + i) + 2)
                        dve.tensor_scalar(e[:, b, 1, :], e[:, b, 1, :], r2[:, b:b + 1], None, ALU.mult).then_inc(combined, 1)
                        dve.wait_ge(combined, NT * h + i + 1)
                        dve.scalar_tensor_tensor(out=pr[:, b, :], in0=e[:, b, 0, :], scalar=ri[:, b, 0:1], in1=e[:, b, 1, :],
                                                 op0=ALU.mult, op1=ALU.add).then_inc(probs, 1)

                    def take(j):
                        cols = slice(j * HALF, (j + 1) * HALF)
                        dve.wait_ge(pv, 2 * h + j + 2)
                        if diff:
                            dve.tensor_copy(g.dmix[:, ds(h, 1), cols], po[:].unsqueeze(1)).then_inc(mixed, 1)
                        else:
                            dve.tensor_copy(g.mix_a[0][:, ds(h, 1), cols], po[:].unsqueeze(1)).then_inc(leading, 1)
                            dve.wait_ge(leading, 2 * h + j + 1)
                            dve.tensor_tensor(g.mix_a[1][:, ds(h, 1), cols], po[:].unsqueeze(1),
                                              g.mix_a[0][:, ds(h, 1), cols].bitcast(F32), ALU.subtract).then_inc(mixed, 1)

                    def release(i):
                        dve.wait_ge(turned, NT * h + i + 1)
                        dve.sem_inc(p_free, 1)

                    for i in range(NT):
                        if i >= 2:
                            release(i - 2)
                        find_max(i)
                        finish(i)
                        if i == 6:
                            take(0)
                    release(NT - 2)
                    release(NT - 1)
                    take(1)


def head_norm(nc, g, mix_b):
    sections = [(g.gate[:, 0, :], True), (g.mod[:, 1, 0:KD], False), (g.mod[:, 1, KD:], False), (g.gate[:, 1, :], True)]
    for i in range(2):
        sections += [(g.mod2[:, i, 0:KD], False), (g.mod2[:, i, KD:], False), (g.gate2[:, i, :], True)]
    with ExitStack() as ctx:
        acc_in0, acc_in1, acc_in2, acc_in3, sec_ps, sec_out, squared, summed, rooted, inv, done, high, low = sems(
            nc, g, "hn_acc_in0 hn_acc_in1 hn_acc_in2 hn_acc_in3 hn_sec_ps hn_sec_out hn_squared hn_summed hn_rooted hn_inv hn_done hn_high hn_low")
        acc_in = (acc_in0, acc_in1, acc_in2, acc_in3)
        acc = ctx.enter_context(nc.sbuf_tensor("hn_acc", [P, 4, D], F32))
        sq = ctx.enter_context(nc.sbuf_tensor("hn_sq", [P, 2, T], F32))
        root = ctx.enter_context(nc.sbuf_tensor("hn_root", [P, 2, T], F32))
        gs = ctx.enter_context(nc.sbuf_tensor("hn_gs", [P, 1], F32))
        ps = ctx.enter_context(nc.psum_tensor("hn_ps", [P, 2, T], F32))
        pm = ctx.enter_context(nc.psum_tensor("hn_pm", [P, 2, D], F32))
        with nc.Block() as block:

            @block.sync
            def _(sp):
                for i in range(len(sections)):
                    if i >= 4:
                        sp.wait_ge(sec_ps, i - 3)
                    sp.dma_start(acc[:, i % 4, :], g.acc_dram[i]).then_inc(acc_in[i % 4], 16)

            @block.scalar
            def _(act):
                def out(i):
                    act.wait_ge(sec_ps, i + 1)
                    to, row = sections[i]
                    act.activation(to, pm[:, i % 2, 0:(D if row else KD)], ACT.Copy).then_inc(sec_out, 1)

                def square(h):
                    act.activation(sq[:, h % 2, :], g.dmix[:, h, :], ACT.Square).then_inc(squared, 1)

                square(0)
                square(1)
                for h in range(HEADS):
                    act.wait_ge(summed, h + 1)
                    if h >= 2:
                        act.wait_ge(done, h - 1)
                    act.activation(root[:, h % 2, :], ps[:, h % 2, :], ACT.Sqrt, bias=g.eps[:], scale=1.0 / P).then_inc(rooted, 1)
                    if h + 2 < HEADS:
                        square(h + 2)
                    out(2 * h)
                    out(2 * h + 1)
                    if h >= 1:
                        act.wait_ge(done, h)
                        act.activation(mix_b[0][:, h - 1, :], g.dmix[:, h - 1, :], ACT.Copy).then_inc(high, 1)
                out(2 * HEADS)
                out(2 * HEADS + 1)
                act.wait_ge(done, HEADS)
                act.activation(mix_b[0][:, HEADS - 1, :], g.dmix[:, HEADS - 1, :], ACT.Copy).then_inc(high, 1)

            @block.tensor
            def _(pe):
                def section(i):
                    pe.wait_ge(acc_in[i % 4], 16 * (i // 4 + 1))
                    if i >= 2:
                        pe.wait_ge(sec_out, i - 1)
                    add = sum_rows if sections[i][1] else sum_columns
                    add(pe, pm[:, i % 2, :], acc[:, i % 4, :], g.ones).then_inc(sec_ps, 1)

                for h in range(HEADS):
                    pe.wait_ge(squared, h + 1)
                    if h >= 2:
                        pe.wait_ge(rooted, h - 1)
                    for hf in range(2):
                        o = pe.matmul(ps[:, h % 2, hf * HALF:(hf + 1) * HALF], g.ones[:], sq[:, h % 2, hf * HALF:(hf + 1) * HALF], start=True, stop=True)
                    o.then_inc(summed, 1)
                    if h >= 1:
                        section(2 * h - 2)
                        section(2 * h - 1)
                for i in range(2 * HEADS - 2, 2 * HEADS + 2):
                    section(i)

            @block.vector
            def _(dve):
                dve.tensor_scalar(gs[:], g.col["sub_g"], 1.0 - LAMBDA_INIT, None, ALU.mult).then_inc(inv, 1)
                for h in range(HEADS):
                    dve.wait_ge(rooted, h + 1)
                    dve.reciprocal(root[:, h % 2, :], root[:, h % 2, :]).then_inc(inv, 1)
                    dve.wait_ge(inv, h + 2)
                    dve.scalar_tensor_tensor(out=g.dmix[:, h, :], in0=g.dmix[:, h, :], scalar=gs[:], in1=root[:, h % 2, :],
                                             op0=ALU.mult, op1=ALU.mult).then_inc(done, 1)
                for h in range(HEADS):
                    dve.wait_ge(high, h + 1)
                    dve.tensor_tensor(mix_b[1][:, h, :], g.dmix[:, h, :], mix_b[0][:, h, :].bitcast(F32), ALU.subtract).then_inc(low, 1)


def project_rows(nc, g, tag, src, w_dram, gate, x_from, x_keep, x_to=None, gain=None):
    with ExitStack() as ctx:
        raw_in0, raw_in1, x_in, x_out, gain_in, gg, high, low, done, squared, rooted, inv, scaled, added, x_sq = sems(
            nc, g, " ".join(tag + s for s in ("raw_in0 raw_in1 x_in x_out gain_in gg high low done squared rooted inv "
                                              "scaled added x_sq").split()))
        raw_in = (raw_in0, raw_in1)
        raw = ctx.enter_context(nc.sbuf_tensor(tag + "raw", [P, 2, D], F32))
        w = [ctx.enter_context(nc.sbuf_tensor(tag + f"w{j}", [P, KD, D], F32R)) for j in range(2)]
        gr = ctx.enter_context(nc.sbuf_tensor(tag + "gr", [P, D], F32)) if gain is not None else None
        junk = ctx.enter_context(nc.sbuf_tensor(tag + "junk", [P, D], F32)) if gain is not None else None
        x2 = ctx.enter_context(nc.sbuf_tensor(tag + "x2", [P, D], F32))
        ss = ctx.enter_context(nc.sbuf_tensor(tag + "ss", [P, 3, NT], F32))
        t = ctx.enter_context(nc.sbuf_tensor(tag + "t", [P, 2, D], F32))
        ps = ctx.enter_context(nc.psum_tensor(tag + "ps", [P, 4, D], F32))

        with nc.Block() as block:

            @block.sync
            def _(sp):
                for k in range(KD):
                    if k >= 2:
                        sp.wait_ge(low, k - 1)
                    sp.dma_start(raw[:, k % 2, :], w_dram[k * P:(k + 1) * P, :]).then_inc(raw_in[k % 2], 16)
                if gain is not None:
                    sp.dma_start(gr[:], gain.partition_broadcast(P)).then_inc(gain_in, 16)
                sp.dma_start(x_keep[:], x_from.rearrange("(n p) d -> p n d", p=P)).then_inc(x_in, 16)
                if x_to is not None:
                    for n in range(NT):
                        sp.wait_ge(added, n + 1)
                        sp.dma_start(x_to[n * P:(n + 1) * P, :], x_keep[:, n, :]).then_inc(x_out, 16)
                    sp.wait_ge(x_out, 16 * NT)

            @block.tensor
            def _(pe):
                for r in range(2):
                    for k in range(KD):
                        if r == 0:
                            pe.wait_ge(low, k + 1)
                        for m in range(4):
                            n = 4 * r + m
                            if r == 1 and k == 0:
                                pe.wait_ge(scaled, m + 1)
                            for h in range(2):
                                cols = slice(h * HALF, (h + 1) * HALF)
                                o = three_passes(pe, ps[:, m, cols], [x[:, n * P:(n + 1) * P] for x in src(k)],
                                                 [x[:, k, cols] for x in w], k == 0, k == KD - 1)
                            if k == KD - 1:
                                o.then_inc(done, 1)

            @block.scalar
            def _(act):
                for k in range(KD):
                    act.wait_ge(raw_in[k % 2], 16 * (k // 2 + 1))
                    act.activation(w[0][:, k, :], raw[:, k % 2, :], ACT.Copy).then_inc(high, 1)

                def square_x(n):
                    act.wait_ge(added, n + 1)
                    if n:
                        act.wait_ge(x_sq, n)
                    act.activation(x2[:], x_keep[:, n, :], ACT.Square, accum_out=g.ss[:, n:n + 1]).then_inc(x_sq, 1)

                for n in range(NT):
                    if gain is not None:
                        act.wait_ge(done, n + 1)
                        if n:
                            act.wait_ge(squared, n)
                        act.activation(junk[:], ps[:, n % 4, :], ACT.Square, accum_out=ss[:, 0, n:n + 1]).then_inc(squared, 1)
                        act.wait_ge(squared, n + 1)
                        act.activation(ss[:, 1, n:n + 1], ss[:, 0, n:n + 1], ACT.Sqrt, bias=g.eps[:], scale=1.0 / D).then_inc(rooted, 1)
                    if n:
                        square_x(n - 1)
                square_x(NT - 1)

            @block.vector
            def _(dve):
                for k in range(KD):
                    dve.wait_ge(high, k + 1)
                    dve.tensor_tensor(w[1][:, k, :], raw[:, k % 2, :], w[0][:, k, :].bitcast(F32), ALU.subtract).then_inc(low, 1)
                row = gate
                if gain is not None:
                    dve.wait_ge(gain_in, 16)
                    dve.tensor_tensor(gr[:], gr[:], gate, ALU.mult).then_inc(gg, 1)
                    dve.wait_ge(gg, 1)
                    row = gr[:]
                for n in range(NT):
                    if gain is None:
                        dve.wait_ge(done, n + 1)
                        dve.tensor_tensor(t[:, n % 2, :], ps[:, n % 4, :], row, ALU.mult).then_inc(scaled, 1)
                    else:
                        dve.wait_ge(rooted, n + 1)
                        dve.reciprocal(ss[:, 2, n:n + 1], ss[:, 1, n:n + 1]).then_inc(inv, 1)
                        dve.wait_ge(inv, n + 1)
                        dve.scalar_tensor_tensor(out=t[:, n % 2, :], in0=ps[:, n % 4, :], scalar=ss[:, 2, n:n + 1], in1=row,
                                                 op0=ALU.mult, op1=ALU.mult).then_inc(scaled, 1)
                    dve.wait_ge(scaled, n + 1)
                    dve.wait_ge(x_in, 16)
                    dve.tensor_tensor(x_keep[:, n, :], x_keep[:, n, :], t[:, n % 2, :], ALU.add).then_inc(added, 1)


def router_constants(nc, where, a, w_in, b_in, c_in):
    def sb(name, shape):
        return where.enter_context(nc.sbuf_tensor("r_" + name, shape, F32))

    wr, br, iota = sb("wr", [P, KD, GROUPS + EXPERTS]), sb("br", [P, GROUPS + EXPERTS]), sb("iota", [P, MAX_BLOCKS])
    tri, tok = sb("tri", [P, P]), sb("tok", [P, NT])

    def load(sp):
        sp.dma_start(wr[:, :, 0:GROUPS], a["w_router_group"][0].rearrange("(k p) n -> p k n", p=P)).then_inc(w_in, 16)
        sp.dma_start(wr[:, :, GROUPS:], a["w_router_expert"][0].rearrange("(k p) n -> p k n", p=P)).then_inc(w_in, 16)
        sp.dma_start(br[:, 0:GROUPS], a["b_router_group"][0].partition_broadcast(P)).then_inc(b_in, 16)
        sp.dma_start(br[:, GROUPS:], a["b_router_expert"][0].partition_broadcast(P)).then_inc(b_in, 16)
        sp.dma_start(iota[:], a["const_iota"][0].partition_broadcast(P)).then_inc(c_in, 16)
        sp.dma_start(tri[:], a["const_before"]).then_inc(c_in, 16)
        sp.dma_start(tok[:], a["const_token"]).then_inc(c_in, 16)

    return (wr, br, iota, tri, tok), load


def route(nc, g, consts, w_in, b_in, c_in):
    with ExitStack() as ctx:
        logit_t, logit_row, logit, pads, step, ex, prefix, scattered, zeroed, table_in, table_t, done = sems(nc, g, "r_logit_t r_logit_row r_logit r_pads r_step r_ex r_prefix r_scattered r_zeroed r_table_in r_table_t r_done")

        def sb(name, shape, dt=F32):
            return ctx.enter_context(nc.sbuf_tensor("r_" + name, shape, dt))

        NL = GROUPS + EXPERTS
        wr, br, iota, tri, tok = consts
        lg = sb("lg", [P, NT, NL])
        gl = sb("gl", [P, NT, 8])
        gm = sb("gm", [P, NT, 8])
        gi = sb("gi", [P, NT, 8], U32)
        gif = sb("gif", [P, NT])
        gd = sb("gd", [P, NT, GROUPS])
        gp = sb("gp", [P, NT])
        oh = sb("oh", [P, NT, GROUPS])
        em = sb("em", [P, NT, EXPERTS])
        tm = sb("tm", [P, NT, 8])
        ti = sb("ti", [P, NT, 8], U32)
        tif = sb("tif", [P, NT, 2])
        dl = sb("dl", [P, NT])
        hot = sb("hot", [P, 2, NT, EXPERTS])
        both = sb("both", [P, NT, EXPERTS])
        pos = sb("pos", [P, NT, EXPERTS])
        off = sb("off", [P, NT + 1, EXPERTS])
        nb = sb("nb", [P, EXPERTS])
        inc = sb("inc", [P, EXPERTS])
        one = sb("one", [P, EXPERTS])
        sel = sb("sel", [P, NT, EXPERTS])
        dst = sb("dst", [P, 2, NT])
        cmp = sb("cmp", [1, MAX_BLOCKS, EXPERTS])
        blk = sb("blk", [1, MAX_BLOCKS + 1])
        zero = sb("zero", [P, MAX_BLOCKS])
        rt = sb("rt", [MAX_BLOCKS, P])
        lt = sb("lt", [NL, T])
        plt = ctx.enter_context(nc.psum_tensor("r_plt", [NL, 2, HALF], F32))
        pl = ctx.enter_context(nc.psum_tensor("r_pl", [P, NT, 64], F32))
        pp = ctx.enter_context(nc.psum_tensor("r_pp", [P, HALF], F32))
        pn = ctx.enter_context(nc.psum_tensor("r_pn", [P, HALF], F32))
        prt = ctx.enter_context(nc.psum_tensor("r_prt", [P, MAX_BLOCKS], F32))
        NE = NT * EXPERTS
        with nc.Block() as block:

            @block.sync
            def _(sp):
                sp.wait_ge(pads, 1)
                sp.dma_start(g.row_token.rearrange("(p n) a -> p (n a)", p=P), zero[:]).then_inc(zeroed, 16)
                sp.wait_ge(scattered, 16 * 2 * NT)
                sp.dma_start(rt[:], g.row_token.rearrange("(n p) a -> n (p a)", p=P)).then_inc(table_in, 16)
                sp.wait_ge(table_in, 16)

            @block.tensor
            def _(pe):
                pe.wait_ge(w_in, 32)
                for hf in range(2):
                    for k in range(KD):
                        o = pe.matmul(plt[:, hf, :], wr[:, k, :], g.ht[:, k, hf * HALF:(hf + 1) * HALF], start=(k == 0), stop=(k == KD - 1))
                    o.then_inc(logit_t, 1)
                pe.wait_ge(logit_row, 2)
                for n in range(NT):
                    o = pe.transpose(pl[:, n, 0:NL], lt[:, n * P:(n + 1) * P], g.ident[0:NL, 0:NL])
                o.then_inc(logit, 1)
                pe.wait_ge(ex, 2)
                pe.wait_ge(c_in, 48)
                bv = both[:].rearrange("p n e -> p (n e)")
                pe.matmul(pp[:, 0:NE], tri[:], bv, start=True, stop=True).then_inc(prefix, 1)
                pe.matmul(pn[:, 0:NE], g.ones[:], bv, start=True, stop=True).then_inc(prefix, 1)
                pe.wait_ge(table_in, 16)
                pe.transpose(prt[:], rt[:], g.ident[0:MAX_BLOCKS, 0:MAX_BLOCKS]).then_inc(table_t, 1)

            @block.scalar
            def _(act):
                for hf in range(2):
                    act.wait_ge(logit_t, hf + 1)
                    act.activation(lt[:, hf * HALF:(hf + 1) * HALF], plt[:, hf, :], ACT.Copy).then_inc(logit_row, 1)
                act.wait_ge(ex, 1)
                act.activation(gd[:], gd[:], ACT.Exp).then_inc(done, 1)
                act.activation(dl[:], dl[:], ACT.Exp).then_inc(done, 1)

            @block.vector
            def _(dve):
                count = [0]

                def seq(o):
                    count[0] += 1
                    o.then_inc(step, 1)
                    dve.wait_ge(step, count[0])

                def bc(x, n):
                    return x.unsqueeze(2).broadcast_to([P, NT, n])

                dve.memset(zero[:], 0.0).then_inc(pads, 1)
                dve.memset(one[:], 1.0)
                dve.memset(off[:, 0, :], 0.0)
                seq(dve.memset(gl[:], -BIG))
                dve.wait_ge(logit, 1)
                dve.wait_ge(b_in, 32)
                dve.wait_ge(c_in, 48)
                seq(dve.tensor_tensor(lg[:], pl[:, :, 0:NL], br[:].unsqueeze(1).broadcast_to([P, NT, NL]), ALU.add))
                seq(dve.tensor_copy(gl[:, :, 0:GROUPS], lg[:, :, 0:GROUPS]))
                for n in range(NT):
                    o = dve.max(gm[:, n, :], gl[:, n, :])
                seq(o)
                for n in range(NT):
                    o = dve.max_index(gi[:, n, :], gm[:, n, :], gl[:, n, :])
                seq(o)
                seq(dve.tensor_copy(gif[:], gi[:, :, 0]))
                seq(dve.tensor_tensor(oh[:], iota[:, 0:GROUPS].unsqueeze(1).broadcast_to([P, NT, GROUPS]), bc(gif[:], GROUPS), ALU.is_equal))
                for n in range(NT):
                    o = dve.tensor_tensor(em[:, n, :].rearrange("p (a b) -> p a b", a=GROUPS),
                                          lg[:, n, GROUPS:].rearrange("p (a b) -> p a b", a=GROUPS),
                                          oh[:, n, :].unsqueeze(2).broadcast_to([P, GROUPS, PER_GROUP]), ALU.mult)
                seq(o)
                seq(dve.tensor_scalar(oh[:], oh[:], -1.0, BIG, ALU.add, ALU.mult))
                for n in range(NT):
                    o = dve.tensor_tensor(em[:, n, :].rearrange("p (a b) -> p a b", a=GROUPS),
                                          em[:, n, :].rearrange("p (a b) -> p a b", a=GROUPS),
                                          oh[:, n, :].unsqueeze(2).broadcast_to([P, GROUPS, PER_GROUP]), ALU.add)
                seq(o)
                for n in range(NT):
                    o = dve.max(tm[:, n, :], em[:, n, :])
                seq(o)
                for n in range(NT):
                    o = dve.max_index(ti[:, n, :], tm[:, n, :], em[:, n, :])
                seq(o)
                seq(dve.tensor_copy(tif[:], ti[:, :, 0:2]))
                seq(dve.tensor_tensor(gd[:], lg[:, :, 0:GROUPS], bc(gm[:, :, 0], GROUPS), ALU.subtract))
                dve.tensor_tensor(dl[:], tm[:, :, 1], tm[:, :, 0], ALU.subtract).then_inc(ex, 1)
                for s in range(2):
                    o = dve.tensor_tensor(hot[:, s, :, :], iota[:, 0:EXPERTS].unsqueeze(1).broadcast_to([P, NT, EXPERTS]),
                                          bc(tif[:, :, s], EXPERTS), ALU.is_equal)
                seq(o)
                dve.tensor_tensor(both[:], hot[:, 0], hot[:, 1], ALU.add).then_inc(ex, 1)
                dve.wait_ge(done, 2)
                seq(dve.tensor_reduce(gp[:], gd[:], AX_X, ALU.add))
                seq(dve.scalar_tensor_tensor(out=gp[:], in0=dl[:], scalar=1.0, in1=gp[:], op0=ALU.add, op1=ALU.mult))
                seq(dve.reciprocal(g.wt[:, 0, :], gp[:]))
                seq(dve.tensor_tensor(g.wt[:, 1, :], g.wt[:, 0, :], dl[:], ALU.mult))
                dve.wait_ge(prefix, 2)
                for n in range(NT):
                    seq(dve.tensor_tensor(off[:, n + 1, :], off[:, n, :], pn[:, n * EXPERTS:(n + 1) * EXPERTS], ALU.add))
                seq(dve.tensor_scalar(nb[:], off[:, NT, :], 0.0, None, ALU.is_gt))
                for j in range(1, NT):
                    seq(dve.scalar_tensor_tensor(out=nb[:], in0=off[:, NT, :], scalar=float(j * P), in1=nb[:], op0=ALU.is_gt, op1=ALU.add))
                seq(dve.tensor_tensor_scan(inc[:], one[:], nb[:], 0.0, ALU.mult, ALU.add))
                seq(dve.tensor_tensor(nb[:], inc[:], nb[:], ALU.subtract))
                seq(dve.tensor_scalar(nb[:], nb[:], float(P), None, ALU.mult))
                seq(dve.tensor_tensor(pos[:].rearrange("p n e -> p (n e)"), pp[:, 0:NE], off[:, 0:NT, :].rearrange("p n e -> p (n e)"), ALU.add))
                seq(dve.tensor_tensor(pos[:], pos[:], nb[:].unsqueeze(1).broadcast_to([P, NT, EXPERTS]), ALU.add))
                for s in range(2):
                    seq(dve.tensor_tensor(sel[:], hot[:, s], pos[:], ALU.mult))
                    seq(dve.tensor_reduce(dst[:, s, :], sel[:], AX_X, ALU.add))
                dve.tensor_copy(g.dest[:], dst[:]).then_inc(pads, 1)
                seq(dve.tensor_tensor(cmp[:], inc[0:1, :].unsqueeze(1).broadcast_to([1, MAX_BLOCKS, EXPERTS]),
                                      iota[0:1, :].unsqueeze(2).broadcast_to([1, MAX_BLOCKS, EXPERTS]), ALU.is_le))
                seq(dve.tensor_reduce(blk[:, 0:MAX_BLOCKS], cmp[:], AX_X, ALU.add))
                seq(dve.tensor_scalar(blk[:, 0:MAX_BLOCKS], blk[:, 0:MAX_BLOCKS], float(EXPERTS - 1), None, ALU.min))
                seq(dve.tensor_scalar(cmp[:, 0, 0:MAX_BLOCKS // 2], iota[0:1, 0:MAX_BLOCKS // 2], 2.0, None, ALU.mult))
                seq(dve.tensor_scalar(cmp[:, 1, 0:MAX_BLOCKS // 2], cmp[:, 0, 0:MAX_BLOCKS // 2], inc[0:1, EXPERTS - 1:EXPERTS], None, ALU.is_lt))
                seq(dve.tensor_reduce(blk[:, MAX_BLOCKS:], cmp[:, 1, 1:MAX_BLOCKS // 2], AX_X, ALU.add))
                seq(dve.tensor_copy(g.blocks[:], blk[:]))
                dve.wait_ge(table_t, 1)
                seq(dve.tensor_copy(g.rows[:], prt[:]))

            @block.gpsimd
            def _(pool):
                pool.wait_ge(c_in, 48)
                pool.wait_ge(pads, 2)
                pool.wait_ge(zeroed, 16)
                for s in range(2):
                    for n in range(NT):
                        pool.indirect_dma_start(g.row_token, bass.IndirectOffsetOnAxis(ap=g.dest[:, s, n:n + 1], axis=0),
                                                tok[:, n:n + 1], None).then_inc(scattered, 16)
                pool.wait_ge(scattered, 16 * 2 * NT)


def experts(nc, g, a, ahead):
    with ExitStack() as ctx:
        names = ("g_in0 g_in1 u_in0 u_in1 d_in0 d_in1 idx idx_seen got0 got1 x_turned x_mul x_mod gate_done gu_done silu act_ready "
                 "a_turned a_copied y_done y_copied y_out0 y_out1 done")
        (g_in0, g_in1, u_in0, u_in1, d_in0, d_in1, idx_ready, idx_seen, got0, got1, x_turned, x_mul, x_mod, gate_done, gu_done, silu_done,
         act_ready, a_turned, a_copied, y_done, y_copied, y_out0, y_out1, all_done) = sems(nc, g, " ".join("e_" + s for s in names.split()))
        g_in, u_in, d_in, y_out, got = (g_in0, g_in1), (u_in0, u_in1), (d_in0, d_in1), (y_out0, y_out1), (got0, got1)

        def sb(name, shape, dt=F32):
            return ctx.enter_context(nc.sbuf_tensor("e_" + name, shape, dt))

        wg = sb("wg", [P, 2, KD, FE])
        wu = sb("wu", [P, 2, KD, FE])
        wd = sb("wd", [P, 2, KE, D])
        idx = [sb(f"idx{b}", [P, 1], U32) for b in range(2)]
        xg = [sb(f"xg{b}", [P, D]) for b in range(2)]
        xt = sb("xt", [P, 2, KD, P])
        sg = sb("sg", [P, 2, FE])
        at = sb("at", [P, 2, FE])
        att = sb("att", [P, 2, KE, P])
        yo = sb("yo", [P, 2, D])
        px = ctx.enter_context(nc.psum_tensor("e_px", [P, KD, P], F32))
        pa = ctx.enter_context(nc.psum_tensor("e_pa", [P, KE, P], F32))
        pgu = ctx.enter_context(nc.psum_tensor("e_pgu", [P, 2, FE], F32))
        py = ctx.enter_context(nc.psum_tensor("e_py", [P, D], F32))
        wg_d = a["w_expert_gate"][0].rearrange("e (k p) n -> e p k n", p=P)
        wu_d = a["w_expert_up"][0].rearrange("e (k p) n -> e p k n", p=P)
        wd_d = a["w_expert_down"][0].rearrange("e (k p) n -> e p k n", p=P)
        y_rows = g.y_dram.rearrange("(n p) d -> n p d", p=P)

        def last_pair(eng):
            return eng.value_load(g.blocks[0:1, MAX_BLOCKS:MAX_BLOCKS + 1], min_val=0, max_val=MAX_BLOCKS // 2 - 1)

        with nc.Block() as block:

            @block.sync
            def _(sp):
                def expert(j):
                    return sp.value_load(g.blocks[0:1, ds(j, 1)], min_val=0, max_val=EXPERTS - 1)

                def load_gu(j, b):
                    ex = expert(j)
                    sp.wait_ge(gu_done, j + 1)
                    sp.dma_start(wg[:, b, :, :], wg_d[ds(ex, 1)].squeeze(0)).then_inc(g_in[b], 16)
                    sp.dma_start(wu[:, b, :, :], wu_d[ds(ex, 1)].squeeze(0)).then_inc(u_in[b], 16)

                def load_d(j, b):
                    ex = expert(j)
                    sp.wait_ge(y_done, j + 1)
                    sp.dma_start(wd[:, b, :, :], wd_d[ds(ex, 1)].squeeze(0)).then_inc(d_in[b], 16)

                m = last_pair(sp)
                load_gu(0, 0)
                load_gu(1, 1)
                load_d(0, 0)
                with sp.Fori(0, m) as i:
                    load_gu(2 * i + 2, 0)
                    load_d(2 * i + 1, 1)
                    load_gu(2 * i + 3, 1)
                    load_d(2 * i + 2, 0)
                load_d(2 * m + 1, 1)
                ahead(sp)

            @block.gpsimd
            def _(pool):
                m = last_pair(pool)
                with pool.Fori(0, m + 1) as i:
                    for b in range(2):
                        pool.wait_ge(x_turned, 2 * i + b + 1)
                        pool.sem_inc(idx_seen, 1)
                        pool.tensor_copy(idx[b][:], g.rows[:, ds(2 * i + b, 1)]).then_inc(idx_ready, 1)
                        pool.wait_ge(idx_ready, 2 * i + b + 1)
                        pool.sem_inc(idx_seen, 1)
                        pool.indirect_dma_start(xg[b][:], None, g.xn_dram, bass.IndirectOffsetOnAxis(ap=idx[b][:], axis=0)).then_inc(got[b], 16)

            @block.tensor
            def _(pe):
                def turn_x(j, b, r):
                    pe.wait_ge(got[b], 16 * r)
                    if not (isinstance(j, int) and j == 0):
                        pe.wait_ge(x_mul, j)
                    for k in range(KD):
                        o = pe.transpose(px[:, k, :], xg[b][:, k * P:(k + 1) * P], g.ident[:])
                    o.then_inc(x_turned, 1)

                def gate_up(j, b, r):
                    pe.wait_ge(x_mod, j + 1)
                    pe.wait_ge(g_in[b], 16 * r)
                    for k in range(KD):
                        o = pe.matmul(pgu[:, 0, :], xt[:, b, k, :], wg[:, b, k, :], start=(k == 0), stop=(k == KD - 1))
                    o.then_inc(gate_done, 1)
                    pe.wait_ge(u_in[b], 16 * r)
                    for k in range(KD):
                        o = pe.matmul(pgu[:, 1, :], xt[:, b, k, :], wu[:, b, k, :], start=(k == 0), stop=(k == KD - 1))
                    o.then_inc(gu_done, 1)

                def turn_a(j, b):
                    pe.wait_ge(act_ready, j + 1)
                    for k in range(KE):
                        o = pe.transpose(pa[:, k, :], at[:, b, k * P:(k + 1) * P], g.ident[:])
                    o.then_inc(a_turned, 1)

                def down(j, b, r):
                    pe.wait_ge(a_copied, j + 1)
                    pe.wait_ge(d_in[b], 16 * r)
                    pe.wait_ge(y_copied, j + 1)
                    for h in range(2):
                        for k in range(KE):
                            o = pe.matmul(py[:, h * HALF:(h + 1) * HALF], att[:, b, k, :], wd[:, b, k, h * HALF:(h + 1) * HALF],
                                          start=(k == 0), stop=(k == KE - 1))
                    o.then_inc(y_done, 1)

                m = last_pair(pe)
                pe.sem_inc(gu_done, 2)
                pe.sem_inc(y_done, 2)
                pe.sem_inc(x_turned, 2)
                turn_x(0, 0, 1)
                gate_up(0, 0, 1)
                turn_x(1, 1, 1)
                turn_a(0, 0)
                with pe.Fori(0, m) as i:
                    gate_up(2 * i + 1, 1, i + 1)
                    turn_x(2 * i + 2, 0, i + 2)
                    down(2 * i, 0, i + 1)
                    turn_a(2 * i + 1, 1)
                    gate_up(2 * i + 2, 0, i + 2)
                    turn_x(2 * i + 3, 1, i + 2)
                    down(2 * i + 1, 1, i + 1)
                    turn_a(2 * i + 2, 0)
                gate_up(2 * m + 1, 1, m + 1)
                down(2 * m, 0, m + 1)
                turn_a(2 * m + 1, 1)
                down(2 * m + 1, 1, m + 1)

            @block.vector
            def _(dve):
                def modulate(j, b):
                    dve.wait_ge(x_turned, j + 3)
                    dve.tensor_tensor(xt[:, b], px[:], g.a_col[:].unsqueeze(2).broadcast_to([P, KD, P]), ALU.mult).then_inc(x_mul, 1)
                    dve.wait_ge(x_mul, j + 1)
                    dve.tensor_tensor(xt[:, b], xt[:, b], g.b_col[:].unsqueeze(2).broadcast_to([P, KD, P]), ALU.add).then_inc(x_mod, 1)

                def gated(j, b):
                    dve.wait_ge(silu_done, j + 1)
                    dve.wait_ge(gu_done, j + 3)
                    dve.tensor_tensor(at[:, b, :], sg[:, b, :], pgu[:, 1, :], ALU.mult).then_inc(act_ready, 1)

                def copy_y(j, b, r):
                    dve.wait_ge(y_done, j + 3)
                    dve.wait_ge(y_out[b], 16 * r)
                    dve.tensor_tensor(yo[:, b, :], py[:], g.gate[:, 1, :], ALU.mult).then_inc(y_copied, 1)

                dve.sem_inc(y_copied, 1)
                m = last_pair(dve)
                modulate(0, 0)
                gated(0, 0)
                modulate(1, 1)
                with dve.Fori(0, m) as i:
                    gated(2 * i + 1, 1)
                    modulate(2 * i + 2, 0)
                    copy_y(2 * i, 0, i + 1)
                    gated(2 * i + 2, 0)
                    modulate(2 * i + 3, 1)
                    copy_y(2 * i + 1, 1, i + 1)
                gated(2 * m + 1, 1)
                copy_y(2 * m, 0, m + 1)
                copy_y(2 * m + 1, 1, m + 1)

            @block.scalar
            def _(act):
                def silu(j, b):
                    act.wait_ge(gate_done, j + 1)
                    act.activation(sg[:, b, :], pgu[:, 0, :], ACT.Silu).then_inc(silu_done, 1)

                def copy_a(j, b):
                    act.wait_ge(a_turned, j + 1)
                    act.activation(att[:, b], pa[:], ACT.Copy).then_inc(a_copied, 1)

                def store_y(j, b):
                    act.wait_ge(y_copied, j + 2)
                    act.dma_start(y_rows[ds(j, 1)].squeeze(0), yo[:, b, :]).then_inc(y_out[b], 16)

                m = last_pair(act)
                act.sem_inc(y_out0, 16)
                act.sem_inc(y_out1, 16)
                silu(0, 0)
                copy_a(0, 0)
                with act.Fori(0, m) as i:
                    silu(2 * i + 1, 1)
                    store_y(2 * i, 0)
                    copy_a(2 * i + 1, 1)
                    silu(2 * i + 2, 0)
                    store_y(2 * i + 1, 1)
                    copy_a(2 * i + 2, 0)
                silu(2 * m + 1, 1)
                store_y(2 * m, 0)
                copy_a(2 * m + 1, 1)
                store_y(2 * m + 1, 1)
                for b in range(2):
                    act.wait_ge(y_out[b], 16 * m + 32)
                    act.sem_inc(all_done, 1)


def combine(nc, g, a, x_in):
    with ExitStack() as ctx:
        x_out, fg_in, rows_in0, rows_in1, rows_in2, rows_in3, first, added, squared, rooted, inv, normed, x_sq = sems(
            nc, g, "c_x_out c_fg_in c_rows_in0 c_rows_in1 c_rows_in2 c_rows_in3 c_first c_added c_squared c_rooted c_inv c_normed c_x_sq")
        rows_in = (rows_in0, rows_in1, rows_in2, rows_in3)
        y = ctx.enter_context(nc.sbuf_tensor("c_y", [P, 4, 2, D], F32))
        fg = ctx.enter_context(nc.sbuf_tensor("c_fg", [P, D], F32))
        junk = ctx.enter_context(nc.sbuf_tensor("c_junk", [P, 2, D], F32))
        ss = ctx.enter_context(nc.sbuf_tensor("c_ss", [P, 3, NT], F32))
        with nc.Block() as block:

            @block.sync
            def _(sp):
                sp.dma_start(fg[:], a["final_norm_g"].partition_broadcast(P)).then_inc(fg_in, 16)
                for n in range(NT):
                    sp.wait_ge(normed, n + 1)
                    sp.dma_start(g.x_dram[n * P:(n + 1) * P, :], g.x[:, n, :]).then_inc(x_out, 16)
                sp.wait_ge(x_out, 16 * NT)

            @block.gpsimd
            def _(pool):
                for n in range(NT):
                    if n >= 4:
                        pool.wait_ge(added, n - 3)
                    for s in range(2):
                        pool.indirect_dma_start(y[:, n % 4, s, :], None, g.y_dram,
                                                bass.IndirectOffsetOnAxis(ap=g.dest[:, s, n:n + 1], axis=0)).then_inc(rows_in[n % 4], 16)

            @block.vector
            def _(dve):
                def norm(n):
                    dve.wait_ge(rooted, n + 1)
                    dve.reciprocal(ss[:, 2, n:n + 1], ss[:, 1, n:n + 1]).then_inc(inv, 1)
                    dve.wait_ge(inv, n + 1)
                    dve.scalar_tensor_tensor(out=g.x[:, n, :], in0=g.x[:, n, :], scalar=ss[:, 2, n:n + 1], in1=fg[:],
                                             op0=ALU.mult, op1=ALU.mult).then_inc(normed, 1)

                dve.wait_ge(x_in, 16)
                dve.wait_ge(fg_in, 16)
                for n in range(NT):
                    dve.wait_ge(rows_in[n % 4], 32 * (n // 4 + 1))
                    dve.scalar_tensor_tensor(out=g.x[:, n, :], in0=y[:, n % 4, 0, :], scalar=g.wt[:, 0, n:n + 1], in1=g.x[:, n, :],
                                             op0=ALU.mult, op1=ALU.add).then_inc(first, 1)
                    if n:
                        norm(n - 1)
                    dve.wait_ge(first, n + 1)
                    dve.scalar_tensor_tensor(out=g.x[:, n, :], in0=y[:, n % 4, 1, :], scalar=g.wt[:, 1, n:n + 1], in1=g.x[:, n, :],
                                             op0=ALU.mult, op1=ALU.add).then_inc(added, 1)
                norm(NT - 1)

            @block.scalar
            def _(act):
                def square_normed(n):
                    act.wait_ge(normed, n + 1)
                    if n:
                        act.wait_ge(x_sq, n)
                    act.activation(junk[:, 1, :], g.x[:, n, :], ACT.Square, accum_out=g.ss[:, n:n + 1]).then_inc(x_sq, 1)

                for n in range(NT):
                    act.wait_ge(added, n + 1)
                    if n:
                        act.wait_ge(squared, n)
                    act.activation(junk[:, 0, :], g.x[:, n, :], ACT.Square, accum_out=ss[:, 0, n:n + 1]).then_inc(squared, 1)
                    act.wait_ge(squared, n + 1)
                    act.activation(ss[:, 1, n:n + 1], ss[:, 0, n:n + 1], ACT.Sqrt, bias=g.eps[:], scale=1.0 / D).then_inc(rooted, 1)
                    if n:
                        square_normed(n - 1)
                square_normed(NT - 1)


def short_conv(nc, g, a, h_t, y_t):
    with ExitStack() as ctx:
        asked, raw_in0, raw_in1, raw_in2, high, low, used, c_out, u_done, t1, t2, t3, freed, y_high, y_low, halo = sems(
            nc, g, "s_asked s_raw_in0 s_raw_in1 s_raw_in2 s_high s_low s_used s_c_out s_u_done s_t1 s_t2 s_t3 s_freed s_y_high s_y_low s_halo")
        raw_in = (raw_in0, raw_in1, raw_in2)
        raw = ctx.enter_context(nc.sbuf_tensor("s_raw", [P, 3, KD, P], F32))
        w = [ctx.enter_context(nc.sbuf_tensor(f"s_w{j}", [P, 3, KD, P], F32R)) for j in range(2)]
        cc = ctx.enter_context(nc.sbuf_tensor("s_cc", [P, T], F32))
        u = ctx.enter_context(nc.sbuf_tensor("s_u", [P, T + 2], F32))
        t = ctx.enter_context(nc.sbuf_tensor("s_t", [P, 2, T], F32))
        ps = [ctx.enter_context(nc.psum_tensor(f"s_ps{i}", [P, 1, T], F32)) for i in range(3)]
        w_v = a["conv_w_in_2"][0].rearrange("(k p) (s n) -> p k s n", p=P, s=3)
        cw = g.col["conv_w"]
        order = (1, 2, 0)
        with nc.Block() as block:

            @block.sync
            def _(sp):
                with sp.Fori(0, KD) as f:
                    for j, s in enumerate(order):
                        sp.wait_ge(low, 3 * f + j + 1)
                        sp.sem_inc(asked, 1)
                        sp.dma_start(raw[:, j], w_v[:, :, s, ds(f * P, P)]).then_inc(raw_in[j], 16)

            @block.tensor
            def _(pe):
                pe.sem_inc(used, 3)
                with pe.Fori(0, KD) as f:
                    for j in range(3):
                        pe.wait_ge(low, 3 * f + j + 4)
                        if j == 0:
                            pe.wait_ge(c_out, f + 1)
                        elif j == 1:
                            pe.wait_ge(u_done, f + 1)
                        else:
                            pe.wait_ge(freed, f + 1)
                        for h in range(2):
                            cols = slice(h * HALF, (h + 1) * HALF)
                            for k in range(KD):
                                o = three_passes(pe, ps[j][:, 0, cols], [x[:, j, k, :] for x in w], [x[:, k, cols] for x in h_t],
                                                 k == 0, k == KD - 1)
                        o.then_inc(used, 1)

            @block.scalar
            def _(act):
                act.sem_inc(c_out, 1)

                def leading(f, j):
                    act.wait_ge(raw_in[j], 16 * f + 16)
                    act.wait_ge(used, 3 * f + j + 1)
                    act.activation(w[0][:, j], raw[:, j], ACT.Copy).then_inc(high, 1)

                def chunk(f, last):
                    act.wait_ge(used, 3 * f + 4)
                    act.wait_ge(u_done, f + 1)
                    act.activation(cc[:], ps[0][:, 0, :], ACT.Copy).then_inc(c_out, 1)
                    if not last:
                        for j in range(3):
                            leading(f + 1, j)

                for j in range(3):
                    leading(0, j)
                with act.Fori(0, KD - 1) as f:
                    chunk(f, False)
                chunk(KD - 1, True)

            @block.vector
            def _(dve):
                dve.sem_inc(low, 3)
                dve.sem_inc(u_done, 1)
                dve.sem_inc(freed, 1)
                dve.memset(u[:, 0:2], 0.0).then_inc(halo, 1)
                dve.wait_ge(halo, 1)

                def rest(f, j):
                    dve.wait_ge(high, 3 * f + j + 1)
                    dve.tensor_tensor(w[1][:, j], raw[:, j], w[0][:, j].bitcast(F32), ALU.subtract).then_inc(low, 1)

                def chunk(f, last):
                    dve.wait_ge(c_out, f + 2)
                    if not last:
                        rest(f + 1, 0)
                    dve.wait_ge(used, 3 * f + 5)
                    dve.tensor_tensor(u[:, 2:], cc[:], ps[1][:, 0, :], ALU.mult).then_inc(u_done, 1)
                    dve.wait_ge(u_done, f + 2)
                    dve.tensor_scalar(t[:, 0, :], u[:, 0:T], cw[:, ds(f, 1)], None, ALU.mult).then_inc(t1, 1)
                    dve.wait_ge(t1, f + 1)
                    dve.scalar_tensor_tensor(out=t[:, 1, :], in0=u[:, 1:T + 1], scalar=cw[:, ds(KD + f, 1)],
                                             in1=t[:, 0, :], op0=ALU.mult, op1=ALU.add).then_inc(t2, 1)
                    dve.wait_ge(t2, f + 1)
                    dve.scalar_tensor_tensor(out=t[:, 0, :], in0=u[:, 2:T + 2], scalar=cw[:, ds(2 * KD + f, 1)],
                                             in1=t[:, 1, :], op0=ALU.mult, op1=ALU.add).then_inc(t3, 1)
                    dve.wait_ge(t3, f + 1)
                    if not last:
                        rest(f + 1, 1)
                    dve.wait_ge(used, 3 * f + 6)
                    dve.tensor_tensor(t[:, 1, :], t[:, 0, :], ps[2][:, 0, :], ALU.mult).then_inc(freed, 1)
                    dve.wait_ge(freed, f + 2)
                    if not last:
                        rest(f + 1, 2)
                    dve.tensor_copy(y_t[0][:, ds(f, 1), :], t[:, 1:2, :]).then_inc(y_high, 1)
                    dve.wait_ge(y_high, f + 1)
                    dve.tensor_tensor(y_t[1][:, ds(f, 1), :], t[:, 1:2, :], y_t[0][:, ds(f, 1), :].bitcast(F32), ALU.subtract).then_inc(y_low, 1)
                    dve.wait_ge(y_low, f + 1)

                for j in range(3):
                    rest(0, j)
                with dve.Fori(0, KD - 1) as f:
                    chunk(f, False)
                chunk(KD - 1, True)


def feed_forward(nc, g, a, out):
    NH = NT // 2
    TH = T // 2
    PIECES = 3 * KF
    with ExitStack() as ctx:
        names = ("raw_in0 raw_in1 high low used x_out gain_in gg root inv staged turned full_done h_high h_low silu acted a_high "
                 "a_low down squared rooted inv2 scaled added ab")
        (raw_in0, raw_in1, high, low, used, x_out, gain_in, gg, root, inv, staged, turned, full_done, h_high, h_low, silu, acted,
         a_high, a_low, down, squared, rooted, inv2, scaled, added, ab) = sems(nc, g, " ".join("f_" + s for s in names.split()))
        raw_in = (raw_in0, raw_in1)

        def sb(name, shape, dt=F32):
            return ctx.enter_context(nc.sbuf_tensor("f_" + name, shape, dt))

        x = g.x
        h_t = [sb(f"h{j}", [P, KD, TH], F32R) for j in range(2)]
        a_t = [sb(f"a{j}", [P, KF, TH], F32R) for j in range(2)]
        raw = sb("raw", [P, 2, D])
        w = [sb(f"w{j}", [P, 2, D], F32R) for j in range(2)]
        sg = sb("sg", [P, 2, TH])
        y = sb("y", [P, 2, TH])
        r = sb("r", [P, 2, D])
        gr = sb("gr", [P, D])
        ss = sb("ss", [P, 6, NH])
        ps = ctx.enter_context(nc.psum_tensor("f_ps", [P, NH, 2, HALF], F32))
        pg, pu = ps[:, 0, 0, :], ps[:, 0, 1, :]
        w_up = a["ffn_w_gate_up_2"][0].rearrange("(k p) (s n) -> p k s n", p=P, s=2)
        w_down = a["ffn_w_down_2"][0].rearrange("(f p) n -> f p n", p=P)
        out_rows = out[0].rearrange("(n p) d -> p n d", p=P)
        with nc.Block() as block:

            @block.sync
            def _(sp):
                sp.dma_start(gr[:], a["norm_gains_2"][0, 3].partition_broadcast(P)).then_inc(gain_in, 16)
                with sp.Fori(0, 2) as h:
                    with sp.Fori(0, KF) as f:
                        for s in range(2):
                            sp.wait_ge(low, PIECES * h + 2 * f + s + 1)
                            sp.dma_start(raw[:, s, :].rearrange("p (k n) -> p k n", k=KD), w_up[:, :, s, ds(f * P, P)]).then_inc(raw_in[s], 16)
                    with sp.Fori(0, KF // 2) as f:
                        for s in range(2):
                            sp.wait_ge(low, PIECES * h + 2 * KF + 2 * f + s + 1)
                            sp.dma_start(raw[:, s, :], w_down[ds(2 * f + s, 1)].squeeze(0)).then_inc(raw_in[s], 16)
                    for n in range(NH):
                        sp.wait_ge(added, NH * h + n + 1)
                        sp.dma_start(out_rows[:, ds(NH * h + n, 1), :], x[:, ds(NH * h + n, 1), :]).then_inc(x_out, 16)
                sp.wait_ge(x_out, 16 * NT)

            @block.tensor
            def _(pe):
                pe.sem_inc(used, 2)
                pe.sem_inc(turned, 2)
                with pe.Fori(0, 2) as h:
                    pe.wait_ge(scaled, NH * h + 1)
                    for k in range(KD):
                        pe.wait_ge(staged, KD * h + k + 1)
                        pe.wait_ge(full_done, KD * h + k + 1)
                        for n in range(NH):
                            o = pe.transpose(ps[:, 0, k % 2, n * P:(n + 1) * P], sg[:, k % 2, n * P:(n + 1) * P], g.ident[:])
                        o.then_inc(turned, 1)
                    with pe.Fori(0, KF) as f:
                        pe.wait_ge(h_low, KD * h + KD)
                        for s, bank in enumerate((pg, pu)):
                            pe.wait_ge(low, PIECES * h + 2 * f + s + 3)
                            if s == 0:
                                pe.wait_ge(silu, KF * h + f + 1)
                            else:
                                pe.wait_ge(acted, KF * h + f + 1)
                            for k in range(KD):
                                o = three_passes(pe, bank, [v[:, s, k * P:(k + 1) * P] for v in w], [v[:, k, :] for v in h_t],
                                                 k == 0, k == KD - 1)
                            o.then_inc(used, 1)
                    pe.wait_ge(a_low, KF * h + KF)
                    for f in range(KF):
                        pe.wait_ge(low, PIECES * h + 2 * KF + f + 3)
                        for n in range(NH):
                            for c in range(2):
                                cols = slice(c * HALF, (c + 1) * HALF)
                                o = three_passes(pe, ps[:, n, c, :], [v[:, f, n * P:(n + 1) * P] for v in a_t],
                                                 [v[:, f % 2, cols] for v in w], f == 0, f == KF - 1)
                            if f == KF - 1 and n < NH - 1:
                                o.then_inc(down, 1)
                        o.then_inc(used, 1)

            @block.scalar
            def _(act):
                act.sem_inc(silu, 1)
                act.sem_inc(full_done, 2)

                def leading(j_in_half, h, pair, s):
                    act.wait_ge(raw_in[s], 16 * (PIECES // 2 * h + pair) + 16)
                    act.wait_ge(used, PIECES * h + j_in_half + 1)
                    act.activation(w[0][:, s, :], raw[:, s, :], ACT.Copy).then_inc(high, 1)

                with act.Fori(0, 2) as h:
                    for s in range(2):
                        leading(s, h, 0, s)
                    act.activation(ss[:, 1, :], g.ss[:, ds(NH * h, NH)], ACT.Sqrt, bias=g.eps[:], scale=1.0 / D).then_inc(root, 1)
                    act.wait_ge(ab, 1)
                    for k in range(KD):
                        act.wait_ge(turned, KD * h + k + 3)
                        if k >= 2:
                            act.wait_ge(h_low, KD * h + k - 1)
                        act.activation(y[:, k % 2, :], ps[:, 0, k % 2, :], ACT.Identity, bias=g.b_col[:, k:k + 1],
                                       scale=g.a_col[:, k:k + 1]).then_inc(full_done, 1)
                    with act.Fori(0, KF) as f:
                        act.wait_ge(used, PIECES * h + 2 * f + 3)
                        act.wait_ge(acted, KF * h + f + 1)
                        act.activation(sg[:, 0, :], pg, ACT.Silu).then_inc(silu, 1)
                        leading(2 * f + 2, h, f + 1, 0)
                        leading(2 * f + 3, h, f + 1, 1)
                    for f in range(KF - 2):
                        leading(2 * KF + f + 2, h, KF + f // 2 + 1, f % 2)
                    for n in range(NH):
                        if n < NH - 1:
                            act.wait_ge(down, (NH - 1) * h + n + 1)
                        else:
                            act.wait_ge(used, PIECES * (h + 1) + 2)
                        act.activation(r[:, 1, :], ps[:, n], ACT.Square, accum_out=ss[:, 3, n:n + 1]).then_inc(squared, 1)
                        act.wait_ge(squared, NH * h + n + 1)
                        act.activation(ss[:, 4, n:n + 1], ss[:, 3, n:n + 1], ACT.Sqrt, bias=g.eps[:], scale=1.0 / D).then_inc(rooted, 1)

            @block.vector
            def _(dve):
                dve.sem_inc(low, 2)
                dve.sem_inc(acted, 1)
                dve.sem_inc(scaled, 1)
                dve.scalar_tensor_tensor(out=g.a_col[:], in0=g.mod2[:, 1, 8:16], scalar=1.0, in1=g.col["g2"], op0=ALU.add, op1=ALU.mult)
                dve.tensor_copy(g.b_col[:], g.mod2[:, 1, 0:8]).then_inc(ab, 1)
                dve.wait_ge(gain_in, 16)
                dve.tensor_tensor(gr[:], gr[:], g.gate2[:, 1, :], ALU.mult).then_inc(gg, 1)
                dve.wait_ge(gg, 1)

                def rest(j_in_half, h, s):
                    dve.wait_ge(high, PIECES * h + j_in_half + 1)
                    dve.tensor_tensor(w[1][:, s, :], raw[:, s, :], w[0][:, s, :].bitcast(F32), ALU.subtract).then_inc(low, 1)

                with dve.Fori(0, 2) as h:
                    for s in range(2):
                        rest(s, h, s)
                    dve.wait_ge(root, h + 1)
                    dve.reciprocal(ss[:, 2, :], ss[:, 1, :]).then_inc(inv, 1)
                    dve.wait_ge(inv, h + 1)
                    for k in range(KD + 1):
                        if k < KD:
                            dve.wait_ge(turned, KD * h + k + 1)
                            dve.tensor_tensor(sg[:, k % 2, :].rearrange("p (n q) -> p n q", n=NH), x[:, ds(NH * h, NH), k * P:(k + 1) * P],
                                              ss[:, 2, :].unsqueeze(2).broadcast_to([P, NH, P]), ALU.mult).then_inc(staged, 1)
                        if k >= 1:
                            dve.wait_ge(full_done, KD * h + k + 2)
                            dve.tensor_copy(h_t[0][:, k - 1, :], y[:, (k - 1) % 2, :]).then_inc(h_high, 1)
                            dve.wait_ge(h_high, KD * h + k)
                            dve.tensor_tensor(h_t[1][:, k - 1, :], y[:, (k - 1) % 2, :], h_t[0][:, k - 1, :].bitcast(F32),
                                              ALU.subtract).then_inc(h_low, 1)
                    with dve.Fori(0, KF) as f:
                        rest(2 * f + 2, h, 0)
                        dve.wait_ge(h_low, KD * h + KD)
                        dve.wait_ge(silu, KF * h + f + 2)
                        dve.wait_ge(used, PIECES * h + 2 * f + 4)
                        dve.tensor_tensor(y[:, 0, :], sg[:, 0, :], pu, ALU.mult).then_inc(acted, 1)
                        dve.wait_ge(acted, KF * h + f + 2)
                        rest(2 * f + 3, h, 1)
                        dve.tensor_copy(a_t[0][:, ds(f, 1), :], y[:, 0:1, :]).then_inc(a_high, 1)
                        dve.wait_ge(a_high, KF * h + f + 1)
                        dve.tensor_tensor(a_t[1][:, ds(f, 1), :], y[:, 0:1, :], a_t[0][:, ds(f, 1), :].bitcast(F32),
                                          ALU.subtract).then_inc(a_low, 1)
                        dve.wait_ge(a_low, KF * h + f + 1)
                    for f in range(KF - 2):
                        rest(2 * KF + f + 2, h, f % 2)
                    for n in range(NH):
                        dve.wait_ge(rooted, NH * h + n + 1)
                        dve.reciprocal(ss[:, 5, n:n + 1], ss[:, 4, n:n + 1]).then_inc(inv2, 1)
                        dve.wait_ge(inv2, NH * h + n + 1)
                        dve.scalar_tensor_tensor(out=r[:, 0, :].rearrange("p (c n) -> p c n", c=2), in0=ps[:, n], scalar=ss[:, 5, n:n + 1],
                                                 in1=gr[:].rearrange("p (c n) -> p c n", c=2), op0=ALU.mult, op1=ALU.mult).then_inc(scaled, 1)
                        dve.wait_ge(scaled, NH * h + n + 2)
                        xn = x[:, ds(NH * h + n, 1), :]
                        dve.tensor_tensor(xn, xn, r[:, 0:1, :], ALU.add).then_inc(added, 1)
                        dve.wait_ge(added, NH * h + n + 1)


def build(nc, a, out, stop=None):
    g = Program()
    with ExitStack() as ctx:
        g.sems = []

        def sb(name, shape, dt=F32):
            return ctx.enter_context(nc.sbuf_tensor(name, shape, dt))

        g.ident = sb("ident", [P, P])
        g.ones = sb("ones", [P, P])
        g.eps = sb("eps", [P, 1])
        g.vcol = sb("vcol", [P, 2, P])
        g.neg_lam = sb("neg_lam", [P, 1])
        g.cond = sb("cond", [P, 2, KD])
        g.mod = sb("mod", [P, 2, 16])
        g.mod2 = sb("mod2", [P, 2, 16])
        g.ss = sb("ss", [P, NT])
        g.a_col = sb("a_col", [P, KD])
        g.b_col = sb("b_col", [P, KD])
        g.wt = sb("wt", [P, 2, NT])
        g.dest = sb("dest", [P, 2, NT], U32)
        g.blocks = sb("blocks", [1, MAX_BLOCKS + 1], U32)
        g.rows = sb("rows", [P, MAX_BLOCKS], U32)
        g.gate2 = sb("gate2", [P, 2, D])
        g.row_token = nc.dram_tensor("row_token", [MAX_BLOCKS * P, 1], F32, kind="Internal").ap()
        g.xn_dram = nc.dram_tensor("xn_rows", [T, D], F32, kind="Internal").ap()
        g.x_dram = nc.dram_tensor("x_rows", [T, D], F32, kind="Internal").ap()
        g.acc_dram = nc.dram_tensor("acc_sections", [10, P, D], F32, kind="Internal").ap()
        g.y_dram = nc.dram_tensor("y_rows", [Y_BLOCKS * P, D], F32, kind="Internal").ap()

        def pair(where, name, chunks):
            return [where.enter_context(nc.sbuf_tensor(f"{name}{j}", [P, chunks, T], F32R)) for j in range(2)]

        with ExitStack() as first:
            g.gate = first.enter_context(nc.sbuf_tensor("gate", [P, 2, D], F32))
            with ExitStack() as mixed:
                with ExitStack() as early:
                    g.cs = early.enter_context(nc.sbuf_tensor("cos_sin", [P, 2, T], F32, side="right"))
                    load_constants(nc, g, a)
                    lat_in, mla_in, diff_in = sems(nc, g, "lat_in mla_in diff_in")
                    g.dmix = early.enter_context(nc.sbuf_tensor("dmix", [P, HEADS, T], F32, side="right"))
                    g.ht = early.enter_context(nc.sbuf_tensor("ht", [P, KD, T], F32, side="right"))
                    lat_w = ExitStack()
                    w_lat = lat_w.enter_context(nc.sbuf_tensor("w_lat", [P, KD, DQ0], F32, side="right"))
                    with nc.sbuf_tensor("x_in_rows", [P, NT, D], F32) as g.x:
                        first_modulation(nc, g, a)
                        norm_transposed(nc, g, "n1_", g.col["norm1_g"], g.mod[:, 0, :], out_t=g.ht,
                                        ahead=lambda sp: sp.dma_start(
                                            w_lat[:], a["w_in"][0].rearrange("(k p) n -> p k n", p=P)[:, :, 0:DQ0]).then_inc(lat_in, 16))
                    g.mix_a = pair(mixed, "mix_a", HEADS)
                    staged = g.dmix[:, 0:3, :].rearrange("p h t -> p (h t)").rearrange("p (k n) -> p k n", k=KD)
                    with ExitStack() as mla:
                        g.lat = mla.enter_context(nc.sbuf_tensor("lat", [P, 4, T], F32))
                        g.kpe = [mla.enter_context(nc.sbuf_tensor(f"kpe{j}", [P, T], F32R)) for j in range(2)]
                        w_mla = mla.enter_context(nc.sbuf_tensor("w_mla", [P, QR // P, QH + KVH], F32))
                        with lat_w:
                            latents(nc, g, a, w_lat, lat_in, lambda sp: load_head(sp, a, w_mla, mla_in, False, 0))
                        attention(nc, g, a, "am_", False, w_mla, mla_in, (a["w_ada"], a["b_ada"], g.cond[:, 0, :], 2, 4, 0, (g.dmix[:, 3, :],)),
                                  ahead=lambda sp: load_head(sp, a, staged, diff_in, True, 0))
                    with nc.sbuf_tensor("w_diff", [P, KD, 3 * P], F32) as w_diff:
                        attention(nc, g, a, "ad_", True, w_diff, diff_in, (a["ada_w_2"], a["ada_b_2"], g.cond[:, 1, :], 0, 6, 4),
                                  staged=staged)
                    mix_b = pair(mixed, "mix_b", HEADS)
                    head_norm(nc, g, mix_b)
                    clear_sems(nc, g)
                x1 = ExitStack()
                g.x = x1.enter_context(nc.sbuf_tensor("x1_rows", [P, NT, D], F32, side="right"))
                project_rows(nc, g, "po_", lambda k: [x[:, k % HEADS, :] for x in (g.mix_a if k < HEADS else mix_b)],
                             a["w_out"][0], g.gate[:, 0, :], a["x"][0], g.x, x_to=g.x_dram)
            with x1:
                g.ht = x1.enter_context(nc.sbuf_tensor("ht_moe", [P, KD, T], F32, side="right"))
                router_in = sems(nc, g, "r_w_in r_b_in r_c_in")
                consts, load_router = router_constants(nc, x1, a, *router_in)
                norm_transposed(nc, g, "n2_", g.col["norm2_g"], g.mod[:, 1, :], out_t=g.ht, keep=g.xn_dram, ahead=load_router)
                route(nc, g, consts, *router_in)
            clear_sems(nc, g)
            x2 = ExitStack()
            g.x = x2.enter_context(nc.sbuf_tensor("x2_rows", [P, NT, D], F32))
            x2_in, = sems(nc, g, "x2_in")
            experts(nc, g, a, lambda sp: sp.dma_start(g.x[:], g.x_dram.rearrange("(n p) d -> p n d", p=P)).then_inc(x2_in, 16))
            hidden = ExitStack()
            h_t = [hidden.enter_context(nc.sbuf_tensor(f"h2_{j}", [P, KD, T], F32R, side="right")) for j in range(2)]
            with x2:
                combine(nc, g, a, x2_in)
                norm_transposed(nc, g, "n3_", g.col["g0"], g.mod2[:, 0, :], split=h_t)
        with ExitStack() as conv:
            y_t = pair(conv, "y2_", KD)
            with hidden:
                short_conv(nc, g, a, h_t, y_t)
            x4 = ExitStack()
            g.x = x4.enter_context(nc.sbuf_tensor("x4_rows", [P, NT, D], F32, side="right"))
            project_rows(nc, g, "pc_", lambda k: [x[:, k, :] for x in y_t], a["conv_w_out_2"][0], g.gate2[:, 0, :],
                         g.x_dram, g.x, gain=a["norm_gains_2"][0, 1])
        clear_sems(nc, g)
        with x4:
            feed_forward(nc, g, a, out)


def constants():
    half = ROPE // 2
    inv = np.float32(10000.0) ** (-np.arange(0, ROPE, 2, dtype=np.float32) / np.float32(ROPE))
    ang = inv.astype(np.float32)[:, None] * np.arange(T, dtype=np.float32)[None, :]
    cos, sin = np.cos(ang).astype(np.float32), np.sin(ang).astype(np.float32)
    rope = np.zeros((2, P, T), np.float32)
    for q in range(P // half):
        rope[0, q * half:(q + 1) * half] = cos
        rope[1, q * half:(q + 1) * half] = sin if q % 2 else -sin
    return {
        "const_rope": rope,
        "const_ident": np.eye(P, dtype=np.float32),
        "const_before": np.triu(np.ones((P, P), np.float32), 1),
        "const_iota": np.arange(MAX_BLOCKS, dtype=np.float32)[None, :],
        "const_token": np.arange(T, dtype=np.float32).reshape(NT, P).T.copy(),
    }


_INS = ["x", "c", "w_ada", "b_ada", "norm1_g", "w_in", "q_a_norm_g", "w_q_up", "kv_a_norm_g", "w_kv_up", "lambda_q1",
        "lambda_k1", "lambda_q2", "lambda_k2", "subln_g", "w_out", "norm2_g", "w_router_group", "b_router_group",
        "w_router_expert", "b_router_expert", "w_expert_gate", "w_expert_up", "w_expert_down", "final_norm_g",
        "c_2", "ada_w_2", "ada_b_2", "norm_gains_2", "conv_w_in_2", "conv_w_2", "conv_w_out_2",
        "ffn_w_gate_up_2", "ffn_w_down_2"]


def kernel(**inputs):
    import numpy as _np
    import concourse.bacc as _bacc
    from concourse import mybir as _mybir
    from concourse.bass_utils import run_bass_kernel_spmd as _run

    nc = _bacc.Bacc("TRN2", target_bir_lowering=False, num_devices=1)
    arrays, aps = {}, {}
    given = {name: _np.ascontiguousarray(inputs[name]) for name in _INS}
    given.update(constants())
    for name, value in given.items():
        arrays[f"in_{name}_dram"] = value
        aps[name] = nc.dram_tensor(f"in_{name}_dram", value.shape, _mybir.dt.from_np(value.dtype), kind="ExternalInput").ap()
    out = nc.dram_tensor("out_0_dram", (1, T, D), _mybir.dt.float32, kind="ExternalOutput").ap()
    build(nc, aps, out)
    r = _run(nc, [arrays], core_ids=[0])
    return r.results[0]["out_0_dram"]
```
